# Optimizing a Trainium2 kernel written in Bass

```python
import math
import jax, jax.numpy as jnp
from jax import lax
import numpy as np

D_MODEL = 1024
BATCH = 1
SEQ = 256
DEPTH = 1

HEAD_DIM = 64
N_MOBA_HEADS = 6
N_DIFF_HEADS = 6
N_SB_HEADS = 6
DIFF_QK_DIM = HEAD_DIM // 2
MOBA_BLOCK = 256
MOBA_TOPK = 3
MOBA_Q_CHUNK = 64
Q_BLOCK = 128
D_FF = 2816
N_BRANCH = 3
LN_EPS = 1e-5
SUBLN_EPS = 1e-5
MOBA_W = N_MOBA_HEADS * HEAD_DIM
DIFF_QK_W = N_DIFF_HEADS * 2 * DIFF_QK_DIM
DIFF_V_W = N_DIFF_HEADS * HEAD_DIM
SB_W = N_SB_HEADS * HEAD_DIM
IN_SIZES = (MOBA_W, MOBA_W, MOBA_W, DIFF_QK_W, DIFF_QK_W, DIFF_V_W, SB_W, SB_W, SB_W, N_BRANCH * D_MODEL)
N_IN = 3 * MOBA_W + 2 * DIFF_QK_W + DIFF_V_W + 3 * SB_W + N_BRANCH * D_MODEL


F32 = jnp.float32

def _alibi_slopes(n):
    return (2.0 ** (-8.0 * np.arange(1, n + 1, dtype=np.float32) / n)).astype(np.float32)

def layer_norm(x, g, b):
    xf = x.astype(F32)
    mu = jnp.mean(xf, axis=-1, keepdims=True)
    var = jnp.mean(jnp.square(xf - mu), axis=-1, keepdims=True)
    return ((xf - mu) * lax.rsqrt(var + LN_EPS) * g + b).astype(x.dtype)

def swiglu(x, w_gate, w_up, w_down):
    return (jax.nn.silu(x @ w_gate) * (x @ w_up)) @ w_down

def split_heads(t, n_heads):
    B, S, _ = t.shape
    return t.reshape(B, S, n_heads, -1).transpose(0, 2, 1, 3)

def merge_heads(t):
    B, H, S, d = t.shape
    return t.transpose(0, 2, 1, 3).reshape(B, S, H * d)

def moba_attention(q, k, v, slopes):
    B, H, S, Dh = q.shape
    nb = -(-S // MOBA_BLOCK)
    pad = nb * MOBA_BLOCK - S
    kp = jnp.pad(k, ((0, 0), (0, 0), (0, pad), (0, 0)))
    vp = jnp.pad(v, ((0, 0), (0, 0), (0, pad), (0, 0)))
    kb = kp.reshape(B, H, nb, MOBA_BLOCK, Dh)
    vb = vp.reshape(B, H, nb, MOBA_BLOCK, Dh)
    kmean = jnp.mean(kb.astype(F32), axis=3)
    topk = min(MOBA_TOPK, nb)
    scale = Dh ** -0.5
    bi = jnp.arange(B)[:, None, None, None]
    hi = jnp.arange(H)[None, :, None, None]
    slope = slopes.reshape(1, H, 1, 1)
    blk_off = jnp.arange(MOBA_BLOCK)
    blk_ids = jnp.arange(nb)
    n_chunks = S // MOBA_Q_CHUNK

    def chunk(i):
        t0 = i * MOBA_Q_CHUNK
        qc = lax.dynamic_slice_in_dim(q, t0, MOBA_Q_CHUNK, axis=2)
        tpos = t0 + jnp.arange(MOBA_Q_CHUNK)
        own = t0 // MOBA_BLOCK
        gate = jnp.einsum('bhcd,bhnd->bhcn', qc.astype(F32), kmean)
        gate = jnp.where(blk_ids < own, gate, -jnp.inf)
        _, sel = lax.top_k(gate, topk)
        valid = sel < own
        ksel = kb[bi, hi, sel]
        vsel = vb[bi, hi, sel]
        s_sel = jnp.einsum('bhcd,bhcnkd->bhcnk', qc, ksel).astype(F32) * scale
        dist_sel = tpos[None, None, :, None, None] - (sel[..., None] * MOBA_BLOCK + blk_off)
        s_sel = jnp.where(valid[..., None], s_sel - slope[..., None] * dist_sel, -jnp.inf)
        kown = lax.dynamic_index_in_dim(kb, own, axis=2, keepdims=False)
        vown = lax.dynamic_index_in_dim(vb, own, axis=2, keepdims=False)
        s_own = jnp.einsum('bhcd,bhkd->bhck', qc, kown).astype(F32) * scale
        dist_own = tpos[:, None] - (own * MOBA_BLOCK + blk_off)[None, :]
        s_own = jnp.where(dist_own >= 0, s_own - slope * dist_own, -jnp.inf)
        scores = jnp.concatenate([s_sel.reshape(B, H, MOBA_Q_CHUNK, topk * MOBA_BLOCK), s_own], axis=-1)
        p = jax.nn.softmax(scores, axis=-1).astype(v.dtype)
        p_sel = p[..., :topk * MOBA_BLOCK].reshape(B, H, MOBA_Q_CHUNK, topk, MOBA_BLOCK)
        p_own = p[..., topk * MOBA_BLOCK:]
        return (jnp.einsum('bhcnk,bhcnkd->bhcd', p_sel, vsel)
                + jnp.einsum('bhck,bhkd->bhcd', p_own, vown))

    out = lax.map(chunk, jnp.arange(n_chunks))
    return out.transpose(1, 2, 0, 3, 4).reshape(B, H, S, Dh)

def diff_attention(q, k, v, slopes, lam, subln_g, lambda_init):
    B, H, _, S, dq = q.shape
    dv = v.shape[-1]
    scale = dq ** -0.5
    kpos = jnp.arange(S)
    slope = slopes.reshape(1, H, 1, 1, 1)

    def block(i):
        t0 = i * Q_BLOCK
        qc = lax.dynamic_slice_in_dim(q, t0, Q_BLOCK, axis=3)
        dist = (t0 + jnp.arange(Q_BLOCK))[:, None] - kpos[None, :]
        s = jnp.einsum('bhmcd,bhmsd->bhmcs', qc, k).astype(F32) * scale
        s = jnp.where(dist >= 0, s - slope * dist, -jnp.inf)
        p = jax.nn.softmax(s, axis=-1)
        w = p[:, :, 0] - lam * p[:, :, 1]
        return jnp.einsum('bhcs,bhsd->bhcd', w.astype(v.dtype), v)

    o = lax.map(block, jnp.arange(S // Q_BLOCK))
    o = o.transpose(1, 2, 0, 3, 4).reshape(B, H, S, dv).astype(F32)
    o = o * lax.rsqrt(jnp.mean(jnp.square(o), axis=-1, keepdims=True) + SUBLN_EPS) * subln_g
    return (o * (1.0 - lambda_init)).astype(v.dtype)

def stick_breaking_attention(q, k, v):
    B, H, S, Dh = q.shape
    scale = Dh ** -0.5
    kpos = jnp.arange(S)

    def block(i):
        t0 = i * Q_BLOCK
        qc = lax.dynamic_slice_in_dim(q, t0, Q_BLOCK, axis=2)
        before = kpos[None, :] < (t0 + jnp.arange(Q_BLOCK))[:, None]
        z = jnp.einsum('bhcd,bhsd->bhcs', qc, k).astype(F32) * scale
        log_1m = jnp.where(before, jax.nn.log_sigmoid(-z), 0.0)
        tail = lax.cumsum(log_1m, axis=3, reverse=True) - log_1m
        w = jnp.where(before, jnp.exp(jax.nn.log_sigmoid(z) + tail), 0.0)
        return jnp.einsum('bhcs,bhsd->bhcd', w.astype(v.dtype), v)

    o = lax.map(block, jnp.arange(S // Q_BLOCK))
    return o.transpose(1, 2, 0, 3, 4).reshape(B, H, S, Dh)

def hybrid_mixer(x, w_in, b_gate, diff_lambda, diff_subln_g, w_br_moba, w_br_diff, w_br_sb, w_out, layer_idx):
    B, S, D = x.shape
    h = x @ w_in
    offs = []
    acc = 0
    for n in IN_SIZES[:-1]:
        acc += n
        offs.append(acc)
    q_m, k_m, v_m, q_d, k_d, v_d, q_s, k_s, v_s, g = jnp.split(h, offs, axis=-1)

    slopes = jnp.asarray(_alibi_slopes(N_MOBA_HEADS + N_DIFF_HEADS))
    o_m = moba_attention(split_heads(q_m, N_MOBA_HEADS), split_heads(k_m, N_MOBA_HEADS),
                         split_heads(v_m, N_MOBA_HEADS), slopes[0::2])

    lambda_init = 0.8 - 0.6 * math.exp(-0.3 * layer_idx)
    lf = diff_lambda.astype(F32)
    lam = jnp.exp(jnp.sum(lf[0] * lf[1])) - jnp.exp(jnp.sum(lf[2] * lf[3])) + lambda_init
    qd = q_d.reshape(B, S, N_DIFF_HEADS, 2, DIFF_QK_DIM).transpose(0, 2, 3, 1, 4)
    kd = k_d.reshape(B, S, N_DIFF_HEADS, 2, DIFF_QK_DIM).transpose(0, 2, 3, 1, 4)
    o_d = diff_attention(qd, kd, split_heads(v_d, N_DIFF_HEADS), slopes[1::2], lam, diff_subln_g, lambda_init)

    o_s = stick_breaking_attention(split_heads(q_s, N_SB_HEADS), split_heads(k_s, N_SB_HEADS),
                                   split_heads(v_s, N_SB_HEADS))

    gates = jax.nn.sigmoid((g.reshape(B, S, N_BRANCH, D) + b_gate).astype(F32)).astype(x.dtype)
    merged = (gates[:, :, 0] * (merge_heads(o_m) @ w_br_moba)
              + gates[:, :, 1] * (merge_heads(o_d) @ w_br_diff)
              + gates[:, :, 2] * (merge_heads(o_s) @ w_br_sb))
    return merged @ w_out

def first_inputs(seed: int = 0) -> dict:
    key = jax.random.key(seed)
    ks = jax.random.split(key, 14)
    D = D_MODEL
    beta = (8.0 * DEPTH) ** -0.25
    nrm = jax.random.normal
    segs = [(MOBA_W, 1.0), (MOBA_W, 1.0), (MOBA_W, beta), (DIFF_QK_W, 1.0), (DIFF_QK_W, 1.0),
            (DIFF_V_W, beta), (SB_W, 1.0), (SB_W, 1.0), (SB_W, beta), (N_BRANCH * D, 1.0)]
    col_scale = jnp.asarray(np.concatenate([np.full(n, s, np.float32) for n, s in segs]))
    return {
        "x": nrm(ks[0], (BATCH, SEQ, D), F32),
        "ln_g": 1.0 + 0.02 * nrm(ks[1], (DEPTH, 3, D), F32),
        "ln_b": 0.02 * nrm(ks[2], (DEPTH, 3, D), F32),
        "ffn_w_gate": nrm(ks[3], (DEPTH, 2, D, D_FF), F32) * D ** -0.5,
        "ffn_w_up": nrm(ks[4], (DEPTH, 2, D, D_FF), F32) * (D ** -0.5 * beta),
        "ffn_w_down": nrm(ks[5], (DEPTH, 2, D_FF, D), F32) * (D_FF ** -0.5 * beta),
        "w_in": nrm(ks[6], (DEPTH, D, N_IN), F32) * D ** -0.5 * col_scale,
        "b_gate": 0.01 * nrm(ks[7], (DEPTH, N_BRANCH, D), F32),
        "diff_lambda": 0.1 * nrm(ks[8], (DEPTH, 4, DIFF_QK_DIM), F32),
        "diff_subln_g": 1.0 + 0.02 * nrm(ks[9], (DEPTH, HEAD_DIM), F32),
        "w_br_moba": nrm(ks[10], (DEPTH, MOBA_W, D), F32) * MOBA_W ** -0.5,
        "w_br_diff": nrm(ks[11], (DEPTH, DIFF_V_W, D), F32) * DIFF_V_W ** -0.5,
        "w_br_sb": nrm(ks[12], (DEPTH, SB_W, D), F32) * SB_W ** -0.5,
        "w_out": nrm(ks[13], (DEPTH, D, D), F32) * (D ** -0.5 * beta),
    }

def first_block(x, ln_g, ln_b, ffn_w_gate, ffn_w_up, ffn_w_down, w_in, b_gate, diff_lambda,
              diff_subln_g, w_br_moba, w_br_diff, w_br_sb, w_out):
    alpha = (2.0 * DEPTH) ** 0.25
    for l in range(DEPTH):
        x = layer_norm(alpha * x + 0.5 * swiglu(x, ffn_w_gate[l, 0], ffn_w_up[l, 0], ffn_w_down[l, 0]),
                       ln_g[l, 0], ln_b[l, 0])
        x = layer_norm(alpha * x + hybrid_mixer(x, w_in[l], b_gate[l], diff_lambda[l], diff_subln_g[l],
                                                w_br_moba[l], w_br_diff[l], w_br_sb[l], w_out[l], l),
                       ln_g[l, 1], ln_b[l, 1])
        x = layer_norm(alpha * x + 0.5 * swiglu(x, ffn_w_gate[l, 1], ffn_w_up[l, 1], ffn_w_down[l, 1]),
                       ln_g[l, 2], ln_b[l, 2])
    return x


DEPTH_2 = 2

N_A_LAYERS = DEPTH_2 // 2
N_B_LAYERS = DEPTH_2 - N_A_LAYERS
CONV_WIDTH = 3
N_HEADS = 16
HEAD_DIM_2 = D_MODEL // N_HEADS
N_KV_GROUPS = 4
HEADS_PER_GROUP = N_HEADS // N_KV_GROUPS
CMP_BLOCK = 32
CMP_STRIDE = 16
CMP_HIDDEN = 4 * HEAD_DIM_2
SEL_BLOCK = 64
N_SELECT = 16
WINDOW = 512
N_KV_SLOTS = 6
QUERY_CHUNK = 32
EPS = 1e-6
FORCE_SCORE = 1e9
MASK_SCORE = -1e30


def _rmsnorm(x, g):
    xf = x.astype(jnp.float32)
    y = xf * lax.rsqrt(jnp.mean(xf * xf, axis=-1, keepdims=True) + EPS)
    return (y * g.astype(jnp.float32)).astype(x.dtype)

def _swiglu(x, w_gate_up, w_down):
    a, b = jnp.split(x @ w_gate_up, 2, axis=-1)
    return (jax.nn.silu(a) * b) @ w_down

def _short_conv(x, w_in, conv_w, w_out):
    b_gate, c_gate, u = jnp.split(x @ w_in, 3, axis=-1)
    v = c_gate * u
    conv = lax.conv_general_dilated(
        v, conv_w[:, None, :], window_strides=(1,), padding=[(CONV_WIDTH - 1, 0)],
        dimension_numbers=("NWC", "WIO", "NWC"), feature_group_count=D_MODEL)
    return (b_gate * conv) @ w_out

def _compress(x_raw, pos, w1, b1, w2):
    s = x_raw.shape[2]
    n_cmp = (s - CMP_BLOCK) // CMP_STRIDE + 1
    idx = np.arange(n_cmp)[:, None] * CMP_STRIDE + np.arange(CMP_BLOCK)[None, :]
    blocks = x_raw[:, :, idx] + pos
    flat = blocks.reshape(blocks.shape[:3] + (CMP_BLOCK * HEAD_DIM_2,))
    return jax.nn.gelu(flat @ w1 + b1) @ w2

def _shared_kv(h, kv_norm, kv_w, cmp_pos, cmp_w1, cmp_b1, cmp_w2, k_norm):
    b, s, _ = h.shape
    kv = (_rmsnorm(h, kv_norm) @ kv_w).reshape(b, s, N_KV_SLOTS, N_KV_GROUPS, HEAD_DIM_2)
    kv = jnp.transpose(kv, (2, 0, 3, 1, 4))
    k_cmp = _rmsnorm(_compress(kv[0], cmp_pos[0], cmp_w1[0], cmp_b1[0], cmp_w2[0]), k_norm[0])
    v_cmp = _compress(kv[1], cmp_pos[1], cmp_w1[1], cmp_b1[1], cmp_w2[1])
    n_blk = s // SEL_BLOCK
    k_sel = _rmsnorm(kv[2], k_norm[1]).reshape(b, N_KV_GROUPS, n_blk, SEL_BLOCK, HEAD_DIM_2)
    v_sel = kv[3].reshape(b, N_KV_GROUPS, n_blk, SEL_BLOCK, HEAD_DIM_2)
    pad = ((0, 0), (0, 0), (WINDOW, 0), (0, 0))
    k_win = jnp.pad(_rmsnorm(kv[4], k_norm[2]), pad)
    v_win = jnp.pad(kv[5], pad)
    return (k_cmp, v_cmp, k_sel, v_sel, k_win, v_win)

def _softmax_f32(logits, mask):
    return jax.nn.softmax(jnp.where(mask, logits, MASK_SCORE), axis=-1)

def _nsa(x, w_qg, q_norm, w_o, k_cmp, v_cmp, k_sel, v_sel, k_win, v_win):
    b, s, _ = x.shape
    n_chunk = s // QUERY_CHUNK
    n_cmp = k_cmp.shape[2]
    n_blk = k_sel.shape[2]
    n_sel = min(N_SELECT, n_blk)
    scale = HEAD_DIM_2 ** -0.5

    proj = x @ w_qg
    q = _rmsnorm(proj[..., :N_HEADS * HEAD_DIM_2].reshape(b, s, N_HEADS, HEAD_DIM_2), q_norm)
    gate = jax.nn.sigmoid(proj[..., N_HEADS * HEAD_DIM_2:].astype(jnp.float32))
    q = q.reshape(b, n_chunk, QUERY_CHUNK, N_KV_GROUPS, HEADS_PER_GROUP, HEAD_DIM_2)
    q = q.transpose(1, 0, 3, 4, 2, 5)
    gate = gate.reshape(b, n_chunk, QUERY_CHUNK, N_KV_GROUPS, HEADS_PER_GROUP, N_BRANCH)
    gate = gate.transpose(1, 0, 3, 4, 2, 5)

    cmp_start = np.arange(n_cmp) * CMP_STRIDE
    cmp_end = cmp_start + CMP_BLOCK - 1
    blk_start = np.arange(n_blk) * SEL_BLOCK
    overlap = ((cmp_start[:, None] < blk_start[None, :] + SEL_BLOCK)
               & (cmp_start[:, None] + CMP_BLOCK > blk_start[None, :])).astype(np.float32)
    gather_blocks = jax.vmap(jax.vmap(lambda kb, ib: kb[ib]))
    blk_ids = jnp.arange(n_blk)

    def chunk_fn(args):
        c, qc, gc = args
        t = c * QUERY_CHUNK + jnp.arange(QUERY_CHUNK)
        logits = jnp.einsum("bghtd,bgnd->bghtn", qc, k_cmp).astype(jnp.float32) * scale
        valid = cmp_end[None, :] <= t[:, None]
        p_cmp = _softmax_f32(logits, valid) * valid
        o_cmp = jnp.einsum("bghtn,bgnd->bghtd", p_cmp.astype(v_cmp.dtype), v_cmp)
        imp = jnp.einsum("bghtn,nj->bgtj", p_cmp, overlap)
        cur = (t // SEL_BLOCK)[:, None]
        forced = (blk_ids[None] == 0) | (blk_ids[None] == cur) | (blk_ids[None] == cur - 1)
        imp = jnp.where(forced, FORCE_SCORE, imp)
        imp = jnp.where(blk_ids[None] > cur, MASK_SCORE, imp)
        _, idx = lax.top_k(imp, n_sel)
        ks = gather_blocks(k_sel, idx).reshape(b, N_KV_GROUPS, QUERY_CHUNK, n_sel * SEL_BLOCK, HEAD_DIM_2)
        vs = gather_blocks(v_sel, idx).reshape(b, N_KV_GROUPS, QUERY_CHUNK, n_sel * SEL_BLOCK, HEAD_DIM_2)
        kpos = (idx[..., None] * SEL_BLOCK + jnp.arange(SEL_BLOCK)).reshape(
            b, N_KV_GROUPS, QUERY_CHUNK, n_sel * SEL_BLOCK)
        smask = (kpos <= t[:, None])[:, :, None]
        logits = jnp.einsum("bghtd,bgtkd->bghtk", qc, ks).astype(jnp.float32) * scale
        p_sel = _softmax_f32(logits, smask)
        o_sel = jnp.einsum("bghtk,bgtkd->bghtd", p_sel.astype(vs.dtype), vs)
        start = c * QUERY_CHUNK
        kw = lax.dynamic_slice_in_dim(k_win, start, WINDOW + QUERY_CHUNK, axis=2)
        vw = lax.dynamic_slice_in_dim(v_win, start, WINDOW + QUERY_CHUNK, axis=2)
        wpos = start - WINDOW + jnp.arange(WINDOW + QUERY_CHUNK)
        wmask = ((wpos[None] <= t[:, None]) & (wpos[None] > t[:, None] - WINDOW)
                 & (wpos[None] >= 0))
        logits = jnp.einsum("bghtd,bgkd->bghtk", qc, kw).astype(jnp.float32) * scale
        p_win = _softmax_f32(logits, wmask)
        o_win = jnp.einsum("bghtk,bgkd->bghtd", p_win.astype(vw.dtype), vw)
        out = gc[..., 0:1] * o_cmp + gc[..., 1:2] * o_sel + gc[..., 2:3] * o_win
        return out.astype(qc.dtype)

    outs = lax.map(chunk_fn, (jnp.arange(n_chunk), q, gate))
    o = outs.transpose(1, 0, 4, 2, 3, 5).reshape(b, s, N_HEADS * HEAD_DIM_2)
    return o @ w_o

def second_inputs(seed: int = 0) -> dict:
    key = jax.random.key(seed)
    ks = jax.random.split(key, 20)
    nrm = lambda k, shape, scale: jax.random.normal(k, shape, jnp.float32) * scale
    gain = lambda k, shape: 1.0 + 0.02 * jax.random.normal(k, shape, jnp.float32)
    qg_width = N_HEADS * HEAD_DIM_2 + N_BRANCH * N_HEADS
    return {
        "x": nrm(ks[0], (BATCH, SEQ, D_MODEL), 1.0),
        "ffn_norm": gain(ks[1], (DEPTH_2, 2, D_MODEL)),
        "ffn_w_gate_up": nrm(ks[2], (DEPTH_2, 2, D_MODEL, 2 * D_FF), D_MODEL ** -0.5),
        "ffn_w_down": nrm(ks[3], (DEPTH_2, 2, D_FF, D_MODEL), D_FF ** -0.5),
        "mix_norm": gain(ks[4], (DEPTH_2, D_MODEL)),
        "conv_w_in": nrm(ks[5], (N_A_LAYERS, D_MODEL, 3 * D_MODEL), D_MODEL ** -0.5),
        "conv_w": nrm(ks[6], (N_A_LAYERS, CONV_WIDTH, D_MODEL), CONV_WIDTH ** -0.5),
        "conv_w_out": nrm(ks[7], (N_A_LAYERS, D_MODEL, D_MODEL), D_MODEL ** -0.5),
        "kv_norm": gain(ks[8], (D_MODEL,)),
        "kv_w": nrm(ks[9], (D_MODEL, N_KV_SLOTS * N_KV_GROUPS * HEAD_DIM_2), D_MODEL ** -0.5),
        "cmp_pos": nrm(ks[10], (2, CMP_BLOCK, HEAD_DIM_2), 0.1),
        "cmp_w1": nrm(ks[11], (2, CMP_BLOCK * HEAD_DIM_2, CMP_HIDDEN), (CMP_BLOCK * HEAD_DIM_2) ** -0.5),
        "cmp_b1": nrm(ks[12], (2, CMP_HIDDEN), 0.01),
        "cmp_w2": nrm(ks[13], (2, CMP_HIDDEN, HEAD_DIM_2), CMP_HIDDEN ** -0.5),
        "k_norm": gain(ks[14], (N_BRANCH, HEAD_DIM_2)),
        "nsa_w_qg": nrm(ks[15], (N_B_LAYERS, D_MODEL, qg_width), D_MODEL ** -0.5),
        "q_norm": gain(ks[16], (N_B_LAYERS, HEAD_DIM_2)),
        "nsa_w_o": nrm(ks[17], (N_B_LAYERS, N_HEADS * HEAD_DIM_2, D_MODEL), (N_HEADS * HEAD_DIM_2) ** -0.5),
    }

def second_block(x, ffn_norm, ffn_w_gate_up, ffn_w_down, mix_norm, conv_w_in, conv_w, conv_w_out,
              kv_norm, kv_w, cmp_pos, cmp_w1, cmp_b1, cmp_w2, k_norm, nsa_w_qg, q_norm, nsa_w_o):
    h = x
    shared = None
    for layer in range(DEPTH_2):
        h = h + 0.5 * _swiglu(_rmsnorm(h, ffn_norm[layer, 0]), ffn_w_gate_up[layer, 0], ffn_w_down[layer, 0])
        hn = _rmsnorm(h, mix_norm[layer])
        if layer < N_A_LAYERS:
            h = h + _short_conv(hn, conv_w_in[layer], conv_w[layer], conv_w_out[layer])
        else:
            i = layer - N_A_LAYERS
            h = h + _nsa(hn, nsa_w_qg[i], q_norm[i], nsa_w_o[i], *shared)
        h = h + 0.5 * _swiglu(_rmsnorm(h, ffn_norm[layer, 1]), ffn_w_gate_up[layer, 1], ffn_w_down[layer, 1])
        if layer == N_A_LAYERS - 1:
            shared = _shared_kv(h, kv_norm, kv_w, cmp_pos, cmp_w1, cmp_b1, cmp_w2, k_norm)
    return h


def setup_inputs(seed=0):
    out = dict(first_inputs(seed))
    for name, value in second_inputs(seed + 1).items():
        if name != "x":
            out[name + "_2"] = value
    return out


def reference(
    x, ln_g, ln_b, ffn_w_gate, ffn_w_up, ffn_w_down, w_in, b_gate, diff_lambda, diff_subln_g,
    w_br_moba, w_br_diff, w_br_sb, w_out, ffn_norm_2, ffn_w_gate_up_2, ffn_w_down_2, mix_norm_2,
    conv_w_in_2, conv_w_2, conv_w_out_2, kv_norm_2, kv_w_2, cmp_pos_2, cmp_w1_2, cmp_b1_2,
    cmp_w2_2, k_norm_2, nsa_w_qg_2, q_norm_2, nsa_w_o_2,
):
    x = first_block(
        x, ln_g, ln_b, ffn_w_gate, ffn_w_up, ffn_w_down, w_in, b_gate, diff_lambda,
        diff_subln_g, w_br_moba, w_br_diff, w_br_sb, w_out,
    )
    return second_block(
        x, ffn_norm_2, ffn_w_gate_up_2, ffn_w_down_2, mix_norm_2, conv_w_in_2, conv_w_2,
        conv_w_out_2, kv_norm_2, kv_w_2, cmp_pos_2, cmp_w1_2, cmp_b1_2, cmp_w2_2, k_norm_2,
        nsa_w_qg_2, q_norm_2, nsa_w_o_2,
    )


_drawn_inputs = setup_inputs


def setup_inputs(seed=0):
    import zlib

    import numpy as np

    out = dict(_drawn_inputs(seed))
    spreads = {}
    factors = {'b_gate': 8.0,
     'diff_lambda': 3.325,
     'diff_subln_g': 8.0,
     'ffn_norm_2': 3.505,
     'kv_norm_2': 8.0,
     'cmp_pos_2': 2.876,
     'cmp_b1_2': 41.066,
     'k_norm_2': 8.0,
     'q_norm_2': 8.0}
    for name, (base, spread) in spreads.items():
        noise = np.random.default_rng([zlib.crc32(name.encode()), seed]).standard_normal(out[name].shape)
        drawn = base * np.exp(spread * noise) if base else spread * noise
        out[name] = __import__('jax').numpy.asarray(drawn.astype(out[name].dtype))
    for name, factor in factors.items():
        out[name] = (out[name] * factor).astype(out[name].dtype)
    return out
```

```python
from contextlib import ExitStack

import concourse.bass as bass
from concourse import mybir

F32 = mybir.dt.float32
F32R = mybir.dt.float32r
BF16 = mybir.dt.bfloat16
ALU = mybir.AluOpType
ACT = mybir.ActivationFunctionType
AX = mybir.AxisListType

P = 128
D = 1024
KC = D // P
S = 256
NT = S // P
FF = 2816
FT = FF // 256
FC = FF // P
SLOTS = 4
SLAB = 2048
HD = 64
BW = 384
BC = BW // P
BRANCH_HEADS = BW // HD
ALPHA = 2.0 ** 0.25
LN_EPS = 1e-5
SUBLN_EPS = 1e-5
RMS_EPS = 1e-6
LAMBDA_INIT = 0.8 - 0.6
DIFF_SCALE = 32.0 ** -0.5
MASKED = -1e30
N_CMP = 15
GROUPS = 4
PER_GROUP = 4
TOKPAD = 272

CONV_W, POS, CMP_B, Q_NORM, K_NORM, SUBLN, ROWS = 0, 24, 56, 60, 61, 64, 65

FFN, MIXER, CONV, KV, NSA = "ffn", "mixer", "conv", "kv", "nsa"
PHASES = [FFN, MIXER, FFN, FFN, CONV, FFN, KV, FFN, NSA, FFN]
LENGTH = {FFN: 33, MIXER: 36, CONV: 16, KV: 10, NSA: 8}
STOP = len(PHASES)


def alibi_slope(i):
    return 2.0 ** (-8.0 * (i + 1) / 12.0)


def two_block_kernel(nc, t, out):
    phases = PHASES[:STOP]
    first_slab = [sum(LENGTH[k] for k in phases[:n]) for n in range(len(phases) + 1)]
    TOTAL = first_slab[-1]
    ffn_number = [sum(k == FFN for k in phases[:n]) for n in range(len(phases))]

    with ExitStack() as ctx:
        def sb(name, shape, dt=F32):
            return ctx.enter_context(nc.sbuf_tensor(name, shape, dt))

        def sem(name):
            return ctx.enter_context(nc.semaphore(name))

        raw = sb("raw", [P, SLOTS, SLAB])
        w_hi = sb("w_hi", [P, SLOTS, SLAB], F32R)
        w_lo = sb("w_lo", [P, SLOTS, SLAB], F32R)
        x_sb = sb("x_sb", [P, NT, D])
        z_sb = sb("z_sb", [P, NT, D])
        xT_hi = sb("xT_hi", [P, KC, S], F32R)
        xT_lo = sb("xT_lo", [P, KC, S], F32R)
        gain = sb("gain", [P, 3, D])
        stats = sb("stats", [P, 64])
        bn = sb("bn", [P, NT, 2, 6])
        head_max = sb("head_max", [P, 2, 4])
        head_sum = sb("head_sum", [P, 2, 4])
        lam_col = sb("lam_col", [P, 8])
        near = sb("near", [P, P], BF16)
        causal = sb("causal", [P, P], BF16)
        same_head = sb("same_head", [P, P])
        minus_half = sb("minus_half", [P, 32])
        ident = sb("ident", [P, P])
        ident_b = sb("ident_b", [P, P], BF16)
        cols = sb("cols", [P, 80])

        bank = [ctx.enter_context(nc.psum_tensor(f"bank{i}", [P, 512], F32)) for i in range(8)]
        Y = [[bank[2], bank[3]], [bank[6], bank[7]]]
        TB = [[bank[0], bank[1]], [bank[4], bank[5]]]

        def layer_memory(tensors):
            with ExitStack() as own:
                return [own.enter_context(nc.sbuf_tensor(n, s, d)) for n, s, d in tensors]

        qk, v_mix, oT_hi, oT_lo, gates, b_gate, prob, probT, far, tmp, o_norm = layer_memory([
            ("qk", [P, 6 * BC, S], F32),
            ("v_mix", [P, NT, 3 * BW], F32),
            ("oT_hi", [P, BC, S], F32R), ("oT_lo", [P, BC, S], F32R),
            ("gates", [P, NT, D], F32), ("b_gate", [P, 3, D], F32),
            ("prob", [P, 2, BW], F32),
            ("probT", [P, 2, BW], F32),
            ("far", [P, BW], F32),
            ("tmp", [P, 512], F32), ("o_norm", [P, 2, S], F32)])
        ms_d, o_f = o_norm[:, 0, :], o_norm[:, 1, :]
        stick = o_norm[:].rearrange("p a s -> p (a s)")[:, 0:BW]
        k_sel = sb("k_sel", [P, 2, S])
        k_win = sb("k_win", [P, 2, S])
        v_sel = sb("v_sel", [P, NT, S])
        v_win = sb("v_win", [P, NT, S])
        k_cmp = sb("k_cmp", [P, GROUPS * 16])
        v_cmp = sb("v_cmp", [P, GROUPS, PER_GROUP * HD])
        xc_hi, xc_lo, pos, cmp_w2, hid, hid_v, key_sq, key_n, key_ms, cmp_bias, kc_sq, kc_n, kc_ms = layer_memory([
            ("xc_hi", [P, 2, GROUPS, TOKPAD], F32R), ("xc_lo", [P, 2, GROUPS, TOKPAD], F32R),
            ("pos", [P, 32, 2], F32R),
            ("cmp_w2", [P, 2, 2, HD], F32), ("hid", [P, 2, 2, GROUPS * 16], F32),
            ("hid_v", [P, 2, GROUPS, PER_GROUP, 32], F32),
            ("key_sq", [P, 2, NT, S], F32), ("key_n", [P, 2, NT, S], F32), ("key_ms", [P, 2, 2, NT * GROUPS], F32),
            ("cmp_bias", [P, 2, 4], F32), ("kc_sq", [GROUPS * 16, HD], F32), ("kc_n", [GROUPS * 16, 2 * HD], F32),
            ("kc_ms", [GROUPS * 16, 4], F32)])
        NQ = D // HD
        wg, wg_hi, wg_lo, branch_gate, q_ms, qT, sel_p, sel_pT, cmp_p, cmp_pT, cmp_mask, cmp_valid, cmp_row, sel_max, sel_sum, \
            sel_coef, sel_add = layer_memory([
                ("wg", [P, KC, 3 * NQ], F32), ("wg_hi", [P, KC, 3 * NQ], F32R), ("wg_lo", [P, KC, 3 * NQ], F32R),
                ("branch_gate", [P, NT, 3 * NQ], F32), ("q_ms", [P, 2, 2, NQ], F32),
                ("qT", [P, 2, PER_GROUP, S], F32),
                ("sel_p", [P, 2, 3, 512], F32), ("sel_pT", [P, 2, 3, 512], F32),
                ("cmp_p", [P, NT, NQ, 32], F32), ("cmp_pT", [P, NT, GROUPS, P], F32),
                ("cmp_mask", [P, NT, 16], F32), ("cmp_valid", [P, NT, 16], F32), ("cmp_row", [P, 2, NT, NQ], F32),
                ("sel_max", [P, 2, 8], F32), ("sel_sum", [P, 2, NT, PER_GROUP], F32), ("sel_coef", [P, NT, PER_GROUP], F32),
                ("sel_add", [P, 512], F32)])
        q_n = sel_pT[:].rearrange("p a b c -> p (a b c)")[:, 0:NT * D].rearrange("p (t n c) -> p t n c", t=NT, n=2)
        cmp_l = sel_add[:].rearrange("p (t h n) -> p t h n", t=NT, h=NQ)
        hT_hi, hT_lo, silu, h = layer_memory([
            ("hT_hi", [P, FC, S], F32R), ("hT_lo", [P, FC, S], F32R),
            ("silu", [P, NT, 256], F32), ("h", [P, NT, 256], F32)])
        conv_v, conv_a, conv_c, conv_y, yT_hi, yT_lo = layer_memory([
            ("conv_v", [P, KC, S + 2], F32), ("conv_a", [P, KC, S], F32), ("conv_c", [P, 2, 512], F32),
            ("conv_y", [P, 2, 512], F32), ("yT_hi", [P, KC, S], F32R), ("yT_lo", [P, KC, S], F32R)])

        arrived = [sem(f"arrived{i}") for i in range(SLOTS)]
        high_ready = sem("high_ready")
        low_ready = sem("low_ready")
        slab_used = sem("slab_used")
        loaded_x = sem("loaded_x")
        loaded_p = sem("loaded_p")
        loaded_mix = sem("loaded_mix")
        loaded_lam = sem("loaded_lam")
        lam_dots = sem("lam_dots")
        lam_exp = sem("lam_exp")
        pair_read = [sem("pair0_read"), sem("pair1_read")]
        far_ready = sem("far_ready")
        scored = sem("scored")
        score_read = sem("score_read")
        neg_ready = sem("neg_ready")
        exped = sem("exped")
        logs = sem("logs")
        prob_ready = sem("prob_ready")
        probT_psum = sem("probT_psum")
        probT_ready = sem("probT_ready")
        o_psum = sem("o_psum")
        o_square = sem("o_square")
        o_sums = sem("o_sums")
        o_spread = sem("o_spread")
        o_log = sem("o_log")
        o_rstd = sem("o_rstd")
        o_normed = sem("o_normed")
        oT_high = sem("oT_high")
        oT_ready = sem("oT_ready")
        gate_sum = sem("gate_sum")
        gated = sem("gated")
        merged = sem("merged")
        conv_c_ready = sem("conv_c_ready")
        conv_v_ready = sem("conv_v_ready")
        conv_y_ready = sem("conv_y_ready")
        yT_high = sem("yT_high")
        yT_ready = sem("yT_ready")
        loaded_kv = sem("loaded_kv")
        xc_high = sem("xc_high")
        xc_ready = sem("xc_ready")
        bias_ready = sem("bias_ready")
        hid_ready = sem("hid_ready")
        hid_v_ready = sem("hid_v_ready")
        cmp_psum = sem("cmp_psum")
        kc_squared = sem("kc_squared")
        kc_spread = sem("kc_spread")
        kc_rstd = sem("kc_rstd")
        kc_normed = sem("kc_normed")
        kcT_psum = sem("kcT_psum")
        cmp_ready = sem("cmp_ready")
        key_squared = sem("key_squared")
        key_spread = sem("key_spread")
        key_rstd = sem("key_rstd")
        key_normed = sem("key_normed")
        keyT_psum = sem("keyT_psum")
        keys_ready = sem("keys_ready")
        values_ready = sem("values_ready")
        loaded_wg = sem("loaded_wg")
        wg_high = sem("wg_high")
        wg_ready = sem("wg_ready")
        gates_psum = sem("gates_psum")
        branch_gates = sem("branch_gates")
        q_squared = sem("q_squared")
        q_spread = sem("q_spread")
        q_rstd = sem("q_rstd")
        q_normed = sem("q_normed")
        qT_psum = sem("qT_psum")
        qT_ready = sem("qT_ready")
        cmp_masks = sem("cmp_masks")
        cmp_scored = sem("cmp_scored")
        cmp_shifted = sem("cmp_shifted")
        cmp_exped = sem("cmp_exped")
        cmp_weighted = sem("cmp_weighted")
        cmpT_psum = sem("cmpT_psum")
        cmpT_ready = sem("cmpT_ready")
        cmp_out = sem("cmp_out")
        z_started = sem("z_started")
        sel_scored = sem("sel_scored")
        sel_neg = sem("sel_neg")
        sel_exped = sem("sel_exped")
        selT_psum = sem("selT_psum")
        selT_act = sem("selT_act")
        selT_dve = sem("selT_dve")
        sel_out = sem("sel_out")
        attended = sem("attended")
        consts = sem("consts")
        cols_psum = sem("cols_psum")
        cols_ready = sem("cols_ready")
        gain_loaded = [sem(f"gain_loaded{i}") for i in range(3)]
        scaled = sem("scaled")
        summed = sem("summed")
        squared = sem("squared")
        spread = sem("spread")
        rstd_ready = sem("rstd_ready")
        normed = sem("normed")
        xT_psum = sem("xT_psum")
        xT_high = sem("xT_high")
        xT_ready = sem("xT_ready")
        silu_ready = sem("silu_ready")
        h_ready = sem("h_ready")
        hT_psum = sem("hT_psum")
        hT_high = sem("hT_high")
        hT_ready = sem("hT_ready")
        act_step = sem("act_step")
        loaded_rows = sem("loaded_rows")
        dve_step = sem("dve_step")
        pool_step = sem("pool_step")
        stored = sem("stored")

        LN, RMS = "ln", "rms"
        ln_row = {0: 0, 1: 1, 2: 2}
        rms_of = {2: t["ffn_norm_2"][0, 0], 3: t["mix_norm_2"][0], 4: t["ffn_norm_2"][0, 1], 5: t["kv_norm_2"],
                  6: t["ffn_norm_2"][1, 0], 7: t["mix_norm_2"][1], 8: t["ffn_norm_2"][1, 1]}
        last = len(phases) - 1

        def has_ln(n):
            return n in ln_row

        def has_rms(n):
            return n in rms_of and n < last

        def operand(n):
            return x_sb if n in (0, 1, 2) else z_sb

        ln_uses = [sum(has_ln(m) for m in range(n)) for n in range(len(phases) + 1)]
        rms_uses = [sum(has_rms(m) for m in range(n)) for n in range(len(phases) + 1)]
        y_layers = [sum(k != KV for k in phases[:n]) for n in range(len(phases) + 1)]

        def normed_before(n):
            return NT * (ln_uses[n] + rms_uses[n])

        def summed_before(n):
            return NT * y_layers[n]

        QKV = [([(0, 256), (256, 256)], 4), ([(512, 256), (1152, 256)], 4), ([(1408, 256), (1664, 256)], 4),
               ([(2304, 256), (2560, 256)], 4), ([(2816, 256), (3072, 256)], 2), ([(768, 384), (3328, 128)], 0),
               ([(1920, 192), (2112, 192)], 0)]
        GATE0 = 3 * 3 * BW
        HEADS = BRANCH_HEADS
        MOBA, DIFF, STICK = range(3)

        def pair_of(tile):
            return [bank[2 * (tile % 2)], bank[2 * (tile % 2) + 1]]

        def gate_tile(b, half):
            return len(QKV) + 4 * b + half

        def branch_tile(b, half):
            return len(QKV) + 4 * b + 2 + half

        def pair_reads(tile):
            return 2 * (tile // 2)

        def before(u):
            return u if u // HEADS == DIFF or u == 2 * HEADS else u - 1

        ROWS_A, ROWS_B = slice(0, P), slice(P, 3 * P)

        UNITS = 2 * GROUPS
        Q_T = [[5, 6], [7, 0]]
        SCORES = [[3, 4, 5], [0, 1, 2]]
        CMP_OUT = [[6, 7], [1, 0]]

        def score_place(tt, r):
            return (0, slice(r * P, (r + 1) * P)) if tt == 0 else (1 + r // 2, slice((r % 2) * S, (r % 2 + 1) * S))

        def ffn_weights(f):
            if f < 2:
                return t["ffn_w_gate"][0, f], t["ffn_w_up"][0, f], t["ffn_w_down"][0, f]
            both = t["ffn_w_gate_up_2"][(f - 2) // 2, (f - 2) % 2]
            return both[:, 0:FF], both[:, FF:2 * FF], t["ffn_w_down_2"][(f - 2) // 2, (f - 2) % 2]

        def half_rows(w, kh):
            return w[kh * 512:(kh + 1) * 512, :].rearrange("(k p) n -> p k n", p=P)

        def inputs_before(n):
            return n + sum(k in (MIXER, NSA) for k in phases[:n])

        def width_of(k):
            n = max(m for m in range(len(phases)) if first_slab[m] <= k)
            d = k - first_slab[n]
            narrow = phases[n] == MIXER and (d in (12, 13) or 14 <= d < 32 and (d - 14) % 6 >= 4)
            return 4 * BW if narrow else SLAB

        block = ctx.enter_context(nc.Block())

        @block.sync
        def _(sp):
            def load(k, pieces, i=0):
                slot = k % SLOTS
                if k >= SLOTS:
                    sp.wait_ge(low_ready, k - SLOTS + 1 + 4 * i)
                for dst, src in pieces(slot):
                    sp.dma_start(dst, src).then_inc(arrived[slot], 32 // len(pieces(slot)))

            def columns(w, kh, spans, width=512):
                def pieces(slot):
                    dst = raw[:, slot, 0:4 * width].rearrange("p (k n) -> p k n", k=4)
                    at, found = 0, []
                    for c0, n in spans:
                        found.append((dst[:, :, at:at + n], half_rows(w, kh)[:, :, c0:c0 + n]))
                        at += n
                    return found
                return pieces

            def rows(w, c0, chunks=2):
                def pieces(slot):
                    return [(raw[:, slot, j * D:(j + 1) * D], w[(c0 + j) * P:(c0 + j + 1) * P, :]) for j in range(chunks)]
                return pieces

            def gain_row(row, src, n_before):
                sp.dma_start(gain[:, row, :], src.partition_broadcast(P)).then_inc(gain_loaded[row], 16)

            def gains(n):
                if n > 0:
                    sp.wait_ge(normed, normed_before(n))
                if has_ln(n):
                    gain_row(0, t["ln_g"][0, ln_row[n]], n)
                    gain_row(1, t["ln_b"][0, ln_row[n]], n)
                if has_rms(n):
                    gain_row(2, rms_of[n], n)

            xr = t["x"][0].rearrange("(t p) d -> p t d", p=P)
            sp.dma_start(x_sb[:], xr).then_inc(loaded_x, 16)
            for n, kind in enumerate(phases):
                s0 = first_slab[n]
                if kind == FFN:
                    gate, up, down = ffn_weights(ffn_number[n])

                    def gate_up(j, kh, i=0):
                        def pieces(slot):
                            dst = raw[:, slot, :].rearrange("p (k n) -> p k n", k=4)
                            at = bass.ds(256 * j + 512 * i, 256)
                            return [(dst[:, :, 0:256], half_rows(gate, kh)[:, :, at]),
                                    (dst[:, :, 256:512], half_rows(up, kh)[:, :, at])]
                        load(s0 + 2 * j + kh, pieces, i)

                    for j in range(3):
                        for kh in range(2):
                            gate_up(j, kh)
                    with sp.Fori(0, (FT - 3) // 2) as i:
                        for j in range(3, 5):
                            for kh in range(2):
                                gate_up(j, kh, i)
                    gains(n)
                    for d in range(FC // 2):
                        load(s0 + 2 * FT + d, rows(down, 2 * d))
                elif kind == MIXER:
                    w = t["w_in"][0]
                    for j, (spans, _) in enumerate(QKV):
                        for kh in range(2):
                            load(s0 + 2 * j + kh, columns(w, kh, spans, sum(c for _, c in spans)))
                    gains(n)
                    sp.wait_ge(normed, normed_before(n))
                    sp.dma_start(b_gate[:], t["b_gate"][0].partition_broadcast(P)).then_inc(loaded_mix, 16)
                    for b, name in enumerate(("w_br_moba", "w_br_diff", "w_br_sb")):
                        g0 = s0 + 14 + 6 * b
                        for half in range(2):
                            c0 = GATE0 + b * D + half * 512
                            for kh in range(2):
                                load(g0 + 2 * half + kh, columns(w, kh, [(c0, 256), (c0 + 256, 256)]))
                        for half in range(2):
                            src = t[name][0][:, half * 512:(half + 1) * 512].rearrange("(k p) n -> p k n", p=P)

                            def pieces(slot):
                                dst = raw[:, slot, 0:BC * 512].rearrange("p (k n) -> p k n", k=BC)
                                return [(dst[:, :, 0:256], src[:, :, 0:256]), (dst[:, :, 256:512], src[:, :, 256:512])]
                            load(g0 + 4 + half, pieces)
                    for d in range(KC // 2):
                        load(s0 + 32 + d, rows(t["w_out"][0], 2 * d))
                elif kind == CONV:
                    w = t["conv_w_in_2"][0]
                    for j in range(4):
                        for kh in range(2):
                            load(s0 + 2 * j + kh, columns(w, kh, [(D + 256 * j, 256), (2 * D + 256 * j, 256)]))
                    for j in range(2):
                        for kh in range(2):
                            load(s0 + 8 + 2 * j + kh, columns(w, kh, [(512 * j, 256), (512 * j + 256, 256)]))
                    gains(n)
                    for d in range(KC // 2):
                        load(s0 + 12 + d, rows(t["conv_w_out_2"][0], 2 * d))
                elif kind == KV:
                    w = t["kv_w_2"]
                    for kh in range(2):
                        load(s0 + kh, columns(w, kh, [(0, 256), (256, 256)]))
                    for kv in range(2):
                        for part in range(2):
                            src = t["cmp_w1_2"][kv, part * 1024:(part + 1) * 1024, :].rearrange("(k p) n -> p k n", p=P)

                            def pieces(slot):
                                dst = raw[:, slot, :].rearrange("p (k n) -> p k n", k=8)
                                return [(dst[:, 0:4, :], src[:, 0:4, :]), (dst[:, 4:8, :], src[:, 4:8, :])]
                            load(s0 + 2 + 2 * kv + part, pieces)
                    gains(n)
                    for kv in range(2):
                        sp.dma_start(cmp_w2[:, kv, :, :], t["cmp_w2_2"][kv].rearrange("(b p) d -> p b d", p=P)).then_inc(loaded_kv, 16)
                    for slot in range(2):
                        for kh in range(2):
                            load(s0 + 6 + 2 * slot + kh, columns(w, kh, [(512 * (slot + 1), 256), (512 * (slot + 1) + 256, 256)]))
                elif kind == NSA:
                    w = t["nsa_w_qg_2"][0]
                    for j in range(2):
                        for kh in range(2):
                            load(s0 + 2 * j + kh, columns(w, kh, [(512 * j, 256), (512 * j + 256, 256)]))
                    gains(n)
                    sp.dma_start(wg[:], w[:, D:D + 3 * NQ].rearrange("(k p) n -> p k n", p=P)).then_inc(loaded_wg, 16)
                    for d in range(KC // 2):
                        load(s0 + 4 + d, rows(t["nsa_w_o_2"][0], 2 * d))
            if has_ln(last):
                sp.wait_ge(normed, normed_before(len(phases)))
            else:
                sp.wait_ge(summed, summed_before(len(phases)))
            for tt in range(NT):
                sp.dma_start(out[tt * P:(tt + 1) * P, :], x_sb[:, tt, :]).then_inc(stored, 16)
            sp.wait_ge(stored, 16 * NT)

        @block.gpsimd
        def _(pool):
            pool.memset(ident[:], 0.0).then_inc(pool_step, 1)
            pool.wait_ge(pool_step, 1)
            pool.affine_select(out=ident[:], in_=ident[:], compare_op=ALU.not_equal, fill=1.0, base=0,
                               pattern=[[-1, P]], channel_multiplier=1).then_inc(pool_step, 1)
            pool.wait_ge(pool_step, 2)
            pool.tensor_copy(ident_b[:], ident[:]).then_inc(consts, 1)
            pool.memset(minus_half[:], -0.5).then_inc(pool_step, 1)
            pool.wait_ge(pool_step, 3)
            made = [3]

            def step(ins):
                made[0] += 1
                ins.then_inc(pool_step, 1)
                pool.wait_ge(pool_step, made[0])

            for m, first in ((near, 1), (causal, 0)):
                step(pool.memset(m[:], 0.0))
                step(pool.affine_select(out=m[:], in_=m[:], compare_op=ALU.is_ge, fill=MASKED, base=-first,
                                        pattern=[[-1, P]], channel_multiplier=1))
            step(pool.memset(same_head[:], 0.0))
            step(pool.memset(same_head[0:HD, 0:HD], 1.0))
            step(pool.memset(same_head[HD:P, HD:P], 1.0))
            pool.engine_nop().then_inc(consts, 1)

            def root(first, tt, col):
                pool.wait_ge(spread, first + tt + 1)
                pool.tensor_tensor(stats[:, col + 1:col + 2], stats[:, col:col + 1], minus_half[:, 0:1], ALU.pow).then_inc(rstd_ready, 1)

            for n, kind in enumerate(phases):
                if kind == MIXER:
                    pool.wait_ge(normed, normed_before(n))
                    for at, off in ((ROWS_A, 0), (ROWS_B, P)):
                        size = at.stop - at.start
                        step(pool.iota(far[:, at], pattern=[[1, size]], base=-off, channel_multiplier=-1,
                                       allow_small_or_imprecise_dtypes=True))
                        ins = pool.affine_select(out=far[:, at], in_=far[:, at], compare_op=ALU.is_ge, fill=MASKED, base=off,
                                                 pattern=[[-1, size]], channel_multiplier=1)
                    step(ins)
                    pool.engine_nop().then_inc(far_ready, 1)
                if kind == NSA:
                    pool.wait_ge(normed, normed_before(n))
                    step(pool.memset(cmp_mask[:], 0.0))
                    step(pool.memset(cmp_valid[:], 1.0))
                    step(pool.memset(cmp_p[:], 0.0))
                    for m, out_of in ((cmp_mask, MASKED), (cmp_valid, 0.0)):
                        for tt in range(NT):
                            step(pool.affine_select(out=m[:, tt, :], in_=m[:, tt, :], compare_op=ALU.is_ge, fill=out_of,
                                                    base=tt * P - 31, pattern=[[-16, 16]], channel_multiplier=1))
                    pool.engine_nop().then_inc(cmp_masks, 1)
                    for j in range(2):
                        pool.wait_ge(q_spread, j + 1)
                        pool.tensor_tensor(q_ms[:, j, 1, :], q_ms[:, j, 0, :], minus_half[:, 0:NQ], ALU.pow).then_inc(q_rstd, 1)
                if has_ln(n):
                    pool.wait_ge(xT_psum, 4 * (inputs_before(n) + 1))
                    pool.tensor_scalar(x_sb[:].rearrange("p t d -> p (t d)"), x_sb[:].rearrange("p t d -> p (t d)"),
                                       ALPHA, None, ALU.mult).then_inc(scaled, 1)
                    for tt in range(NT):
                        root(normed_before(n), tt, 4 * tt + 2)
                if has_rms(n):
                    for tt in range(NT):
                        root(normed_before(n) + NT * has_ln(n), tt, 10 + 2 * tt)
                if kind == KV:
                    for slot in range(2):
                        if slot == 1:
                            pool.wait_ge(kc_spread, 1)
                            pool.tensor_tensor(kc_ms[:, 2:3], kc_ms[:, 1:2], minus_half[0:GROUPS * 16, 0:1], ALU.pow).then_inc(kc_rstd, 1)
                        pool.wait_ge(key_spread, slot + 1)
                        pool.tensor_tensor(key_ms[:, slot, 1, :], key_ms[:, slot, 0, :], minus_half[:, 0:NT * GROUPS],
                                           ALU.pow).then_inc(key_rstd, 1)

        @block.scalar
        def _(act):
            def split(k, i=0):
                if k >= TOTAL:
                    return
                slot, width = k % SLOTS, width_of(k)
                act.wait_ge(arrived[slot], 32 * (k // SLOTS + 1) + 32 * i)
                if k >= SLOTS:
                    act.wait_ge(slab_used, k - SLOTS + 1 + 4 * i)
                nc.scalar.activation(w_hi[:, slot, 0:width], raw[:, slot, 0:width], ACT.Copy).then_inc(high_ready, 1)

            def evacuate_input(index):
                for b in range(4):
                    tt, q = b // 2, b % 2
                    act.wait_ge(xT_psum, 4 * index + b + 1)
                    nc.scalar.activation(xT_hi[:, 4 * q:4 * q + 4, tt * P:(tt + 1) * P],
                                         TB[tt][q][:].rearrange("p (k m) -> p k m", k=4), ACT.Copy).then_inc(xT_high, 1)

            def norm(n):
                if has_rms(n):
                    for tt in range(NT):
                        if has_ln(n):
                            act.wait_ge(normed, normed_before(n) + tt + 1)
                        else:
                            act.wait_ge(summed, summed_before(n) + (tt + 1 if kind != KV else 0))
                        nc.scalar.activation(z_sb[:, tt, :], x_sb[:, tt, :], ACT.Square,
                                             accum_out=stats[:, 8 + tt:9 + tt]).then_inc(squared, 1)

            def boundary(n):
                norm(n)
                if n < last:
                    evacuate_input(inputs_before(n + 1))

            rows_sb = z_sb[0:ROWS, 0, 0:P]
            for at, src in ((CONV_W, t["conv_w_2"][0].rearrange("w (k p) -> (w k) p", p=P)),
                            (POS, t["cmp_pos_2"].rearrange("a (c q) d -> (a c) (q d)", q=2)),
                            (CMP_B, t["cmp_b1_2"].rearrange("a (b p) -> (a b) p", p=P))):
                act.dma_start(z_sb[at:at + src.shape[0], 0, 0:P], src).then_inc(loaded_rows, 16)
            for at, src in ((Q_NORM, t["q_norm_2"]), (K_NORM, t["k_norm_2"]), (SUBLN, t["diff_subln_g"])):
                for twice in range(2):
                    act.dma_start(z_sb[at:at + src.shape[0], 0, twice * HD:(twice + 1) * HD], src).then_inc(loaded_rows, 16)

            act.dma_start(z_sb[:, 1, 0:P], t["diff_lambda"][0].rearrange("a d -> (a d)").partition_broadcast(P)).then_inc(loaded_lam, 16)
            for k in range(SLOTS):
                split(k)
            evacuate_input(0)
            act.wait_ge(lam_dots, 1)
            nc.scalar.activation(lam_col[:, 2:4], lam_col[:, 0:2], ACT.Exp).then_inc(lam_exp, 1)
            for n, kind in enumerate(phases):
                s0 = first_slab[n]
                if kind == MIXER:
                    for tile, (_, blocks) in enumerate(QKV):
                        split(s0 + 2 * tile + 4)
                        act.wait_ge(slab_used, s0 + 2 * tile + 2)
                        for i in range(blocks // 2):
                            nc.scalar.activation(qk[:, 4 * tile + 2 * i:4 * tile + 2 * i + 2, :],
                                                 pair_of(tile)[i][:].rearrange("p (k m) -> p k m", k=2),
                                                 ACT.Copy).then_inc(pair_read[tile % 2], 1)
                        split(s0 + 2 * tile + 5)

                    def weights_of(u):
                        b, hd = u // HEADS, u % HEADS
                        if b == STICK:
                            p = prob[:, u % 2, :]
                            z = bank[4 + u % 2][:, 0:BW]
                            act.wait_ge(scored, u + 1)
                            if before(u) > 0:
                                act.wait_ge(probT_psum, before(u))
                            k = 3 * (u - 2 * HEADS)
                            nc.scalar.activation(p, z, ACT.Abs).then_inc(logs, 1)
                            act.wait_ge(logs, k + 1)
                            nc.scalar.activation(p, p, ACT.Exp, scale=-(HD ** -0.5)).then_inc(logs, 1)
                            act.wait_ge(logs, k + 2)
                            nc.scalar.activation(p, p, ACT.Ln, bias=1.0).then_inc(logs, 1)
                            act.wait_ge(score_read, u + 1)
                            nc.scalar.activation(p, p, ACT.Exp).then_inc(prob_ready, 1)
                            return
                        scale = HD ** -0.5 if b == MOBA else DIFF_SCALE
                        act.wait_ge(neg_ready, u + 1)
                        for m in range(1 if b == MOBA else 2):
                            side = u % 2 if b == MOBA else m
                            for i, at in enumerate((ROWS_A, ROWS_B)):
                                c = 2 * m + i
                                ins = nc.scalar.activation(prob[:, side, at], prob[:, side, at], ACT.Exp, scale=scale,
                                                           bias=head_max[:, u % 2, c:c + 1],
                                                           accum_out=head_sum[:, u % 2, c:c + 1])
                        ins.then_inc(exped, 1)

                    def transposed(u):
                        act.wait_ge(probT_psum, u + 1)
                        if u >= 2:
                            act.wait_ge(o_psum, u - 1)
                        nc.scalar.activation(probT[:, u % 2, :], bank[6][:, 0:BW], ACT.Copy).then_inc(probT_ready, 1)

                    def pair_out(b, pair):
                        act.wait_ge(o_psum, b * HEADS + 2 * pair + 2)
                        src = bank[7][:, 0:S]
                        if b == DIFF:
                            if pair > 0:
                                act.wait_ge(oT_ready, b * BC + pair)
                            nc.scalar.activation(ms_d, src, ACT.Square).then_inc(o_square, 1)
                            act.wait_ge(o_spread, pair + 1)
                            nc.scalar.activation(ms_d, ms_d, ACT.Ln).then_inc(o_log, 1)
                            act.wait_ge(o_log, pair + 1)
                            nc.scalar.activation(ms_d, ms_d, ACT.Exp, scale=-0.5).then_inc(o_rstd, 1)
                            act.wait_ge(o_normed, pair + 1)
                            src = o_f
                        nc.scalar.activation(oT_hi[:, pair, :], src, ACT.Copy).then_inc(oT_high, 1)

                    for b in range(3):
                        g0 = s0 + 14 + 6 * b
                        nc.scalar.preload_act_table_set("natural_log_exp_and_others")
                        for hd in range(HEADS):
                            u = b * HEADS + hd
                            weights_of(u)
                            if hd < 4:
                                split(g0 + hd + 4)
                            if hd == 3:
                                for half in range(2):
                                    for tt in range(NT):
                                        g = gates[:, tt, half * 512:(half + 1) * 512]
                                        act.wait_ge(gate_sum, 4 * b + 2 * half + tt + 1)
                                        nc.scalar.activation(g, g, ACT.Sigmoid).then_inc(gated, 1)
                                nc.scalar.preload_act_table_set("natural_log_exp_and_others")
                            transposed(u)
                            if hd in (2, 4):
                                pair_out(b, hd // 2 - 1)
                        pair_out(b, 2)
                        for half in range(2):
                            split(g0 + 4 + half + 4)
                    evacuate_input(inputs_before(n) + 1)
                    for d in range(KC // 2 - 1):
                        split(s0 + 32 + d + 4)
                    boundary(n)
                    split(s0 + 32 + KC // 2 - 1 + 4)
                if kind == CONV:
                    for j in range(6):
                        split(s0 + 2 * j + 4)
                        act.wait_ge(slab_used, s0 + 2 * j + 2)
                        if j < 4:
                            if j >= 2:
                                act.wait_ge(conv_v_ready, j - 1)
                            nc.scalar.activation(conv_c[:, j % 2, :], bank[4 * (j % 2)][:], ACT.Copy).then_inc(conv_c_ready, 1)
                        else:
                            for b in range(2):
                                act.wait_ge(conv_y_ready, 2 * (j - 4) + b + 1)
                                k = 4 * (j - 4) + 2 * b
                                nc.scalar.activation(yT_hi[:, k:k + 2, :], conv_y[:, b, :].rearrange("p (k m) -> p k m", k=2),
                                                     ACT.Copy).then_inc(yT_high, 1)
                        split(s0 + 2 * j + 5)
                    for d in range(KC // 2 - 1):
                        split(s0 + 12 + d + 4)
                    boundary(n)
                    split(s0 + 12 + KC // 2 - 1 + 4)
                if kind == KV:
                    split(s0 + 4)
                    nc.scalar.activation(pos[:, :, 0], cols[:, POS:POS + 32], ACT.Copy).then_inc(xc_high, 1)
                    act.wait_ge(slab_used, s0 + 2)
                    for kv in range(2):
                        for gp in range(2):
                            src = bank[kv][HD * gp:HD * (gp + 1), :].rearrange("p (b m) -> p b m", b=2)
                            for on in range(2):
                                nc.scalar.activation(xc_hi[HD * on:HD * (on + 1), kv, gp::2, 0:S - on], src[:, :, on:S],
                                                     ACT.Copy).then_inc(xc_high, 1)
                    split(s0 + 5)
                    norm(n)
                    for kv in range(2):
                        split(s0 + 6 + 2 * kv)
                        act.wait_ge(slab_used, s0 + 4 + 2 * kv)
                        act.wait_ge(bias_ready, kv + 1)
                        for hb in range(2):
                            nc.scalar.activation(hid[:, kv, hb, :], bank[6 + kv][:, hb * 64:(hb + 1) * 64], ACT.Gelu_apprx_tanh,
                                                 bias=cmp_bias[:, kv, hb:hb + 1]).then_inc(hid_ready, 1)
                        split(s0 + 7 + 2 * kv)
                    for slot, (pair, v) in enumerate((([4, 5], v_sel), ([2, 3], v_win))):
                        split(s0 + 10 + 2 * slot)
                        act.wait_ge(slab_used, s0 + 8 + 2 * slot)
                        for tt in range(NT):
                            nc.scalar.activation(key_sq[:, slot, tt, :], bank[pair[tt]][:, 0:S], ACT.Square).then_inc(key_squared, 1)
                        for tt in range(NT):
                            nc.scalar.activation(v[:, tt, :], bank[pair[tt]][:, S:2 * S], ACT.Copy).then_inc(values_ready, 1)
                        if slot == 0:
                            split(s0 + 11)
                            act.wait_ge(cmp_psum, 1)
                            nc.scalar.activation(kc_sq[:], bank[6][0:GROUPS * 16, 256:256 + HD], ACT.Square,
                                                 accum_out=kc_ms[:, 0:1]).then_inc(kc_squared, 1)
                    evacuate_input(inputs_before(n + 1))
                    split(s0 + 13)
                if kind == NSA:
                    act.wait_ge(loaded_wg, 16)
                    nc.scalar.activation(wg_hi[:], wg[:], ACT.Copy).then_inc(wg_high, 1)
                    for j in range(2):
                        split(s0 + 2 * j + 4)
                        act.wait_ge(slab_used, s0 + 2 * j + 2)
                        for tt in range(NT):
                            nc.scalar.activation(z_sb[:, tt, 512 * j:512 * (j + 1)], bank[2 * j + tt][:], ACT.Square).then_inc(q_squared, 1)
                        split(s0 + 2 * j + 5)
                    act.wait_ge(gates_psum, 1)
                    nc.scalar.activation(branch_gate[:].rearrange("p t n -> p (t n)"), bank[4][:, 0:NT * 3 * NQ],
                                         ACT.Sigmoid).then_inc(branch_gates, 1)
                    act.wait_ge(cmp_shifted, 1)
                    nc.scalar.activation(cmp_l, cmp_l, ACT.Exp).then_inc(cmp_exped, 1)

                    def exponentials(w):
                        act.wait_ge(sel_neg, w + 1)
                        if w >= 2:
                            act.wait_ge(selT_psum, w - 1)
                            act.wait_ge(attended, w - 1)
                        for tt in range(NT):
                            for r in range(PER_GROUP):
                                b, at = score_place(tt, r)
                                ins = nc.scalar.activation(sel_p[:, w % 2, b, at], bank[SCORES[w % 2][b]][:, at], ACT.Exp,
                                                           bias=sel_max[:, w % 2, tt * PER_GROUP + r:tt * PER_GROUP + r + 1],
                                                           accum_out=sel_sum[:, w % 2, tt, r:r + 1])
                        ins.then_inc(sel_exped, 1)

                    def transposed_weights(w):
                        act.wait_ge(selT_psum, w + 1)
                        if w >= 2:
                            act.wait_ge(sel_out, w - 1)
                        for b in range(2):
                            ins = nc.scalar.activation(sel_pT[:, w % 2, b, :], bank[SCORES[w % 2][b]][:], ACT.Copy)
                        ins.then_inc(selT_act, 1)

                    exponentials(0)
                    for tt in range(NT):
                        act.wait_ge(cmpT_psum, tt + 1)
                        nc.scalar.activation(cmp_pT[:, tt, :, :].rearrange("p g m -> p (g m)"), bank[2 * tt][:], ACT.Copy)\
                            .then_inc(cmpT_ready, 1)
                    for tt in range(NT):
                        act.wait_ge(cmp_out, tt + 1)
                        for half in range(2):
                            nc.scalar.activation(z_sb[:, tt, 512 * half:512 * (half + 1)], bank[CMP_OUT[tt][half]][:], ACT.Copy)\
                                .then_inc(z_started, 1)
                    for w in range(UNITS):
                        if w > 0:
                            exponentials(w)
                        transposed_weights(w)
                    evacuate_input(inputs_before(n) + 1)
                    for d in range(KC // 2 - 1):
                        split(s0 + 4 + d + 4)
                    boundary(n)
                    split(s0 + 4 + KC // 2 - 1 + 4)
                if kind == FFN:
                    f = ffn_number[n]

                    def hidden(j, i=0):
                        act.wait_ge(hT_psum, FT * f + j + 1 + 2 * i)
                        nc.scalar.activation(hT_hi[:, bass.ds(2 * j + 4 * i, 2), :],
                                             bank[4 + j % 2][:].rearrange("p (c m) -> p c m", c=2),
                                             ACT.Copy).then_inc(hT_high, 1)

                    def tile(j, i=0):
                        if not (isinstance(i, int) and j == 0):
                            hidden(j - 1, i)
                        split(s0 + 2 * j + 4, i)
                        act.wait_ge(slab_used, s0 + 2 * j + 2 + 4 * i)
                        for tt in range(NT):
                            if not (isinstance(i, int) and j == 0):
                                act.wait_ge(h_ready, 2 * FT * f + 2 * j - 1 + tt + 4 * i)
                            nc.scalar.activation(silu[:, tt, :], bank[2 * (j % 2) + tt][:, 0:256],
                                                 ACT.Silu).then_inc(silu_ready, 1)
                        split(s0 + 2 * j + 5, i)

                    for j in range(3):
                        tile(j)
                    with act.Fori(0, (FT - 3) // 2) as i:
                        for j in range(3, 5):
                            tile(j, i)
                    for d in range(FC // 2):
                        if d == 1:
                            hidden(FT - 1)
                        if d < FC // 2 - 1:
                            split(s0 + 2 * FT + d + 4)
                    boundary(n)
                    split(s0 + 2 * FT + FC // 2 - 1 + 4)

        @block.vector
        def _(dve):
            steps = [0]

            def step(ins):
                steps[0] += 1
                ins.then_inc(dve_step, 1)
                dve.wait_ge(dve_step, steps[0])

            def split(k, i=0):
                if k >= TOTAL:
                    return
                slot, width = k % SLOTS, width_of(k)
                dve.wait_ge(high_ready, k + 1 + 4 * i)
                nc.vector.tensor_tensor(w_lo[:, slot, 0:width], raw[:, slot, 0:width],
                                        w_hi[:, slot, 0:width].bitcast(F32), ALU.subtract).then_inc(low_ready, 1)

            def evacuate_input(index):
                for b in range(4):
                    tt, q = b // 2, b % 2
                    dve.wait_ge(xT_high, 4 * index + b + 1)
                    nc.vector.tensor_tensor(xT_lo[:, 4 * q:4 * q + 4, tt * P:(tt + 1) * P],
                                            TB[tt][q][:].rearrange("p (k m) -> p k m", k=4),
                                            xT_hi[:, 4 * q:4 * q + 4, tt * P:(tt + 1) * P].bitcast(F32),
                                            ALU.subtract).then_inc(xT_ready, 1)

            def add_output(n, tt, factor, y_at):
                if tt == 0:
                    dve.wait_ge(slab_used, y_at)
                    if has_ln(n):
                        dve.wait_ge(scaled, ln_uses[n] + 1)
                for half in range(2):
                    part = x_sb[:, tt, half * 512:(half + 1) * 512]
                    ins = nc.vector.scalar_tensor_tensor(out=part, in0=Y[tt][half][:], scalar=factor, in1=part,
                                                         op0=ALU.mult, op1=ALU.add)
                ins.then_inc(summed, 1)

            def layer_norm(n, tt):
                dve.wait_ge(summed, summed_before(n) + tt + 1)
                for half in range(2):
                    ins = nc.vector.bn_stats(bn[:, tt, half, :], x_sb[:, tt, half * 512:(half + 1) * 512])
                step(ins)
                step(nc.vector.bn_aggr(stats[:, 4 * tt:4 * tt + 2], bn[:, tt, :, :]))
                nc.vector.tensor_scalar(stats[:, 4 * tt + 2:4 * tt + 3], stats[:, 4 * tt + 1:4 * tt + 2], LN_EPS, None,
                                        ALU.add).then_inc(spread, 1)

            def layer_norm_apply(n, tt):
                xt, mean, rstd = x_sb[:, tt, :], stats[:, 4 * tt:4 * tt + 1], stats[:, 4 * tt + 3:4 * tt + 4]
                dve.wait_ge(rstd_ready, normed_before(n) + tt + 1)
                dve.wait_ge(gain_loaded[0], 16 * (ln_uses[n] + 1))
                dve.wait_ge(gain_loaded[1], 16 * (ln_uses[n] + 1))
                step(nc.vector.scalar_tensor_tensor(out=xt, in0=xt, scalar=mean, in1=gain[:, 0, :],
                                                    op0=ALU.subtract, op1=ALU.mult))
                nc.vector.scalar_tensor_tensor(out=xt, in0=xt, scalar=rstd, in1=gain[:, 1, :],
                                               op0=ALU.mult, op1=ALU.add).then_inc(normed, 1)

            def rms_norm(n, tt):
                dve.wait_ge(squared, NT * rms_uses[n] + tt + 1)
                nc.vector.tensor_scalar(stats[:, 10 + 2 * tt:11 + 2 * tt], stats[:, 8 + tt:9 + tt], 1.0 / D, RMS_EPS,
                                        ALU.mult, ALU.add).then_inc(spread, 1)

            def rms_norm_apply(n, tt):
                dve.wait_ge(rstd_ready, normed_before(n) + NT * has_ln(n) + tt + 1)
                dve.wait_ge(gain_loaded[2], 16 * (rms_uses[n] + 1))
                nc.vector.scalar_tensor_tensor(out=z_sb[:, tt, :], in0=x_sb[:, tt, :], scalar=stats[:, 11 + 2 * tt:12 + 2 * tt],
                                               in1=gain[:, 2, :], op0=ALU.mult, op1=ALU.mult).then_inc(normed, 1)

            def boundary(n, factor, y_at):
                for tt in range(NT):
                    add_output(n, tt, factor, y_at)
                norm(n)
                if n < last:
                    evacuate_input(inputs_before(n + 1))

            def norm(n):
                if has_ln(n):
                    for tt in range(NT):
                        layer_norm(n, tt)
                    for tt in range(NT):
                        layer_norm_apply(n, tt)
                if has_rms(n):
                    for tt in range(NT):
                        rms_norm(n, tt)
                    for tt in range(NT):
                        rms_norm_apply(n, tt)

            for k in range(SLOTS):
                split(k)
            evacuate_input(0)
            dve.wait_ge(cols_psum, 1)
            nc.vector.tensor_copy(cols[:, 0:ROWS], bank[2][:, 0:ROWS]).then_inc(cols_ready, 1)
            dve.wait_ge(cols_ready, 1)
            dve.wait_ge(loaded_lam, 16)
            lf = z_sb[:, 1, 0:P].rearrange("p (a b d) -> p a b d", a=2, b=2)
            dots = z_sb[:, 1, P:P + HD].rearrange("p (a d) -> p a d", a=2)
            step(nc.vector.tensor_tensor(dots, lf[:, :, 0, :], lf[:, :, 1, :], ALU.mult))
            nc.vector.tensor_reduce(lam_col[:, 0:2], dots, AX.X, ALU.add).then_inc(lam_dots, 1)
            dve.wait_ge(lam_exp, 1)
            step(nc.vector.tensor_tensor(lam_col[:, 4:5], lam_col[:, 3:4], lam_col[:, 2:3], ALU.subtract))
            step(nc.vector.tensor_scalar(lam_col[:, 5:6], lam_col[:, 4:5], -LAMBDA_INIT, None, ALU.add))
            minus_lam = lam_col[:, 5:6]
            step(nc.vector.tensor_scalar(lam_col[:, 6:7], cols[:, SUBLN:SUBLN + 1], 1.0 - LAMBDA_INIT, None, ALU.mult))
            out_gain = lam_col[:, 6:7]
            for n, kind in enumerate(phases):
                s0 = first_slab[n]
                if kind == MIXER:
                    for tile, (spans, blocks) in enumerate(QKV):
                        split(s0 + 2 * tile + 4)
                        src = pair_of(tile)
                        dve.wait_ge(slab_used, s0 + 2 * tile + 2)
                        if blocks == 2:
                            nc.vector.tensor_copy(v_mix[:, :, 2 * BW:2 * BW + 256], src[1][:].rearrange("p (t n) -> p t n", t=NT))\
                                .then_inc(pair_read[tile % 2], 1)
                        if blocks == 0:
                            for tt in range(NT):
                                if tile == 5:
                                    nc.vector.tensor_copy(v_mix[:, tt, 2 * BW + 256:3 * BW], src[tt][:, BW:512])
                                c0 = 0 if tile == 5 else BW
                                nc.vector.tensor_copy(v_mix[:, tt, c0:c0 + BW], src[tt][:, 0:BW]).then_inc(pair_read[tile % 2], 1)
                        split(s0 + 2 * tile + 5)

                    def weights_of(u):
                        b, hd = u // HEADS, u % HEADS
                        dve.wait_ge(scored, u + 1)
                        if b == STICK:
                            p, z = prob[:, u % 2, :], bank[4 + u % 2][:, 0:BW]
                            dve.wait_ge(logs, 3 * (u - 2 * HEADS) + 3)
                            soft, sums = tmp[:, 0:BW], stick
                            step(nc.vector.tensor_scalar(soft, z, 0.0, HD ** -0.5, ALU.max, ALU.mult))
                            step(nc.vector.tensor_tensor(soft, soft, p, ALU.add))
                            for at in (ROWS_A, ROWS_B):
                                part, to = soft[:, at], sums[:, at]
                                ins = nc.vector.tensor_tensor_scan(to[:, ::-1], part[:, ::-1], part[:, ::-1], 0.0, ALU.add, ALU.max)
                            step(ins)
                            nc.vector.scalar_tensor_tensor(out=p, in0=z, scalar=HD ** -0.5, in1=sums, op0=ALU.mult,
                                                           op1=ALU.subtract).then_inc(score_read, 1)
                            dve.wait_ge(score_read, u + 1)
                            return
                        if u == 0:
                            dve.wait_ge(far_ready, 1)
                        if before(u) > 0:
                            dve.wait_ge(probT_psum, before(u))
                        scale = HD ** -0.5 if b == MOBA else DIFF_SCALE
                        slope = alibi_slope(2 * hd if b == MOBA else 2 * hd + 1)
                        maps = 1 if b == MOBA else 2
                        for m in range(maps):
                            side = u % 2 if b == MOBA else m
                            ins = nc.vector.scalar_tensor_tensor(out=prob[:, side, :], in0=far[:], scalar=slope / scale,
                                                                 in1=bank[4 + side][:, 0:BW], op0=ALU.mult, op1=ALU.add)
                        ins.then_inc(score_read, 1)
                        dve.wait_ge(score_read, u + 1)
                        mx, sm = head_max[:, u % 2, 0:2 * maps], head_sum[:, u % 2, 0:2 * maps]
                        for m in range(maps):
                            side = u % 2 if b == MOBA else m
                            for i, at in enumerate((ROWS_A, ROWS_B)):
                                ins = nc.vector.tensor_reduce(head_max[:, u % 2, 2 * m + i:2 * m + i + 1], prob[:, side, at], AX.X, ALU.max)
                        step(ins)
                        nc.vector.tensor_scalar(mx, mx, -scale, None, ALU.mult).then_inc(neg_ready, 1)
                        dve.wait_ge(exped, u + 1)
                        step(nc.vector.reciprocal(sm, sm))
                        if b == DIFF:
                            step(nc.vector.tensor_scalar(sm[:, 2:4], sm[:, 2:4], minus_lam, None, ALU.mult))
                        side = u % 2 if b == MOBA else 0
                        for i, at in enumerate((ROWS_A, ROWS_B)):
                            ins = nc.vector.tensor_scalar(prob[:, side, at], prob[:, side, at], sm[:, i:i + 1], None, ALU.mult)
                        if b == DIFF:
                            step(ins)
                            for i, at in enumerate((ROWS_A, ROWS_B)):
                                ins = nc.vector.scalar_tensor_tensor(out=prob[:, 0, at], in0=prob[:, 1, at], scalar=sm[:, 2 + i:3 + i],
                                                                     in1=prob[:, 0, at], op0=ALU.mult, op1=ALU.add)
                        ins.then_inc(prob_ready, 1)
                        dve.wait_ge(prob_ready, u + 1)

                    def pair_out(b, pair):
                        src = bank[7][:, 0:S]
                        if b == DIFF:
                            dve.wait_ge(o_sums, pair + 1)
                            nc.vector.tensor_scalar(ms_d, bank[7][:, S:2 * S], 1.0 / HD, SUBLN_EPS, ALU.mult, ALU.add)\
                                .then_inc(o_spread, 1)
                            dve.wait_ge(o_rstd, pair + 1)
                            nc.vector.scalar_tensor_tensor(out=o_f, in0=src, scalar=out_gain, in1=ms_d,
                                                           op0=ALU.mult, op1=ALU.mult).then_inc(o_normed, 1)
                            src = o_f
                        dve.wait_ge(oT_high, b * BC + pair + 1)
                        nc.vector.tensor_tensor(oT_lo[:, pair, :], src, oT_hi[:, pair, :].bitcast(F32), ALU.subtract)\
                            .then_inc(oT_ready, 1)

                    for b in range(3):
                        g0 = s0 + 14 + 6 * b
                        for hd in range(HEADS):
                            weights_of(b * HEADS + hd)
                            if hd < 4:
                                split(g0 + hd + 4)
                            if hd == 3:
                                dve.wait_ge(loaded_mix, 16)
                                for half in range(2):
                                    dve.wait_ge(slab_used, g0 + 2 * half + 2)
                                    tile = gate_tile(b, half)
                                    at = slice(half * 512, (half + 1) * 512)
                                    if b > 0:
                                        dve.wait_ge(merged, 4 * b)
                                    for tt in range(NT):
                                        nc.vector.tensor_tensor(gates[:, tt, at], pair_of(tile)[tt][:], b_gate[:, b, at],
                                                                ALU.add).then_inc(gate_sum, 1)
                                    dve.wait_ge(gate_sum, 4 * b + 2 * half + 2)
                                    nc.vector.engine_nop().then_inc(pair_read[tile % 2], 2)
                            if hd in (2, 4):
                                pair_out(b, hd // 2 - 1)
                        pair_out(b, 2)
                        for half in range(2):
                            split(g0 + 4 + half + 4)
                        for half in range(2):
                            tile = branch_tile(b, half)
                            at = slice(half * 512, (half + 1) * 512)
                            dve.wait_ge(slab_used, g0 + 4 + half + 1)
                            for tt in range(NT):
                                dve.wait_ge(gated, 4 * b + 2 * half + tt + 1)
                                y = z_sb[:, tt, at]
                                if b == 0:
                                    nc.vector.tensor_tensor(y, gates[:, tt, at], pair_of(tile)[tt][:], ALU.mult).then_inc(merged, 1)
                                else:
                                    step(nc.vector.tensor_tensor(tmp[:], gates[:, tt, at], pair_of(tile)[tt][:], ALU.mult))
                                    nc.vector.tensor_tensor(y, y, tmp[:], ALU.add).then_inc(merged, 1)
                                dve.wait_ge(merged, 4 * b + 2 * half + tt + 1)
                            nc.vector.engine_nop().then_inc(pair_read[tile % 2], 2)
                    evacuate_input(inputs_before(n) + 1)
                    for d in range(KC // 2 - 1):
                        split(s0 + 32 + d + 4)
                    boundary(n, 1.0, s0 + 36)
                    split(s0 + 32 + KC // 2 - 1 + 4)
                if kind == CONV:
                    nc.vector.memset(conv_v[:, :, 0:2], 0.0)
                    for j in range(6):
                        split(s0 + 2 * j + 4)
                        if j < 4:
                            dve.wait_ge(conv_c_ready, j + 1)
                            nc.vector.tensor_tensor(conv_v[:, 2 * j:2 * j + 2, 2:S + 2],
                                                    conv_c[:, j % 2, :].rearrange("p (k m) -> p k m", k=2),
                                                    bank[4 * (j % 2) + 1][:].rearrange("p (k m) -> p k m", k=2),
                                                    ALU.mult).then_inc(conv_v_ready, 1)
                            dve.wait_ge(conv_v_ready, j + 1)
                            for k in (2 * j, 2 * j + 1):
                                a = conv_a[:, k, :]
                                w = [cols[:, CONV_W + tap * KC + k:CONV_W + tap * KC + k + 1] for tap in range(3)]
                                step(nc.vector.tensor_scalar(a, conv_v[:, k, 2:S + 2], w[2], None, ALU.mult))
                                for tap in (1, 0):
                                    step(nc.vector.scalar_tensor_tensor(out=a, in0=conv_v[:, k, tap:tap + S], scalar=w[tap],
                                                                        in1=a, op0=ALU.mult, op1=ALU.add))
                        else:
                            dve.wait_ge(slab_used, s0 + 2 * j + 2)
                            for b in range(2):
                                k, done = 4 * (j - 4) + 2 * b, 2 * (j - 4) + b + 1
                                if j == 5:
                                    dve.wait_ge(yT_ready, done - 2)
                                nc.vector.tensor_tensor(conv_y[:, b, :], bank[4 * (j % 2) + b][:],
                                                        conv_a[:, k:k + 2, :].rearrange("p k m -> p (k m)"),
                                                        ALU.mult).then_inc(conv_y_ready, 1)
                            for b in range(2):
                                k, done = 4 * (j - 4) + 2 * b, 2 * (j - 4) + b + 1
                                dve.wait_ge(yT_high, done)
                                nc.vector.tensor_tensor(yT_lo[:, k:k + 2, :], conv_y[:, b, :].rearrange("p (k m) -> p k m", k=2),
                                                        yT_hi[:, k:k + 2, :].bitcast(F32), ALU.subtract).then_inc(yT_ready, 1)
                        split(s0 + 2 * j + 5)
                    for d in range(KC // 2 - 1):
                        split(s0 + 12 + d + 4)
                    boundary(n, 1.0, s0 + 16)
                    split(s0 + 12 + KC // 2 - 1 + 4)
                if kind == KV:
                    zero = ident[:].rearrange("p (a g t) -> p a g t", a=2, g=GROUPS)
                    for part, t0, size in ((slice(0, P), S, 16), (slice(HD, P), S - 1, 1)):
                        for x in (xc_hi, xc_lo):
                            nc.vector.tensor_tensor(x[part, :, :, t0:t0 + size], zero[part, :, :, 0:size], zero[part, :, :, 0:size], ALU.subtract)
                    step(nc.vector.memset(v_cmp[:], 0.0))
                    step(nc.vector.memset(hid_v[:], 0.0))
                    split(s0 + 4)
                    dve.wait_ge(xc_high, 1)
                    nc.vector.tensor_tensor(pos[:, :, 1], cols[:, POS:POS + 32], pos[:, :, 0].bitcast(F32), ALU.subtract).then_inc(xc_ready, 1)
                    for kv in range(2):
                        dve.wait_ge(xc_high, 1 + 4 * (kv + 1))
                        for gp in range(2):
                            src = bank[kv][HD * gp:HD * (gp + 1), :].rearrange("p (b m) -> p b m", b=2)
                            for on in range(2):
                                part = slice(HD * on, HD * (on + 1))
                                nc.vector.tensor_tensor(xc_lo[part, kv, gp::2, 0:S - on], src[:, :, on:S],
                                                        xc_hi[part, kv, gp::2, 0:S - on].bitcast(F32), ALU.subtract).then_inc(xc_ready, 1)
                    split(s0 + 5)
                    norm(n)
                    for kv in range(2):
                        split(s0 + 6 + 2 * kv)
                        dve.wait_ge(slab_used, s0 + 4 + 2 * kv)
                        terms = bank[6 + kv][:, 128:132].rearrange("p (b t) -> p b t", b=2)
                        step(nc.vector.tensor_reduce(cmp_bias[:, kv, 2:4], terms, AX.X, ALU.add))
                        c0 = CMP_B + 2 * kv
                        nc.vector.tensor_tensor(cmp_bias[:, kv, 0:2], cmp_bias[:, kv, 2:4], cols[:, c0:c0 + 2], ALU.add).then_inc(bias_ready, 1)
                        split(s0 + 7 + 2 * kv)
                    dve.wait_ge(hid_ready, 4)
                    for hb in range(2):
                        for r in range(PER_GROUP):
                            ins = nc.vector.tensor_copy(hid_v[:, hb, :, r, 0:16], hid[:, 1, hb, :].rearrange("p (g n) -> p g n", g=GROUPS))
                    ins.then_inc(hid_v_ready, 1)
                    for slot, pair in enumerate(([4, 5], [2, 3])):
                        split(s0 + 10 + 2 * slot)
                        dve.wait_ge(key_squared, NT * (slot + 1))
                        ms, rstd = key_ms[:, slot, 0, :], key_ms[:, slot, 1, :]
                        step(nc.vector.tensor_reduce(ms, key_sq[:, slot, :, :].rearrange("p t (g d) -> p (t g) d", g=GROUPS), AX.X, ALU.add))
                        nc.vector.tensor_scalar(ms, ms, 1.0 / HD, RMS_EPS, ALU.mult, ALU.add).then_inc(key_spread, 1)
                        dve.wait_ge(key_rstd, slot + 1)
                        dve.wait_ge(values_ready, NT * (slot + 1))
                        for tt in range(NT):
                            each = rstd[:, tt * GROUPS:(tt + 1) * GROUPS].unsqueeze(2).to_broadcast([P, GROUPS, HD])
                            ins = nc.vector.tensor_tensor(key_n[:, slot, tt, :].rearrange("p (g d) -> p g d", g=GROUPS),
                                                          bank[pair[tt]][:, 0:S].rearrange("p (g d) -> p g d", g=GROUPS), each, ALU.mult)
                        ins.then_inc(key_normed, 1)
                        if slot == 0:
                            split(s0 + 11)
                            dve.wait_ge(cmp_psum, 2)
                            for r in range(PER_GROUP):
                                part = slice(32 * r, 32 * (r + 1))
                                ins = nc.vector.tensor_copy(v_cmp[part, :, HD * r:HD * (r + 1)],
                                                            bank[7][part, S:2 * S].rearrange("p (g d) -> p g d", g=GROUPS))
                            ins.then_inc(cmp_ready, 1)
                            dve.wait_ge(kc_squared, 1)
                            nc.vector.tensor_scalar(kc_ms[:, 1:2], kc_ms[:, 0:1], 1.0 / HD, RMS_EPS, ALU.mult, ALU.add).then_inc(kc_spread, 1)
                            dve.wait_ge(kc_rstd, 1)
                            for twice in range(2):
                                ins = nc.vector.tensor_scalar(kc_n[:, twice * HD:(twice + 1) * HD], bank[6][0:GROUPS * 16, 256:256 + HD],
                                                              kc_ms[:, 2:3], None, ALU.mult)
                            ins.then_inc(kc_normed, 1)
                            dve.wait_ge(kcT_psum, 1)
                            nc.vector.tensor_scalar(k_cmp[:], bank[6][:, 384:384 + GROUPS * 16], cols[:, K_NORM:K_NORM + 1], None,
                                                    ALU.mult).then_inc(cmp_ready, 1)
                    evacuate_input(inputs_before(n + 1))
                    split(s0 + 13)
                    for slot, (b, keys) in enumerate(((7, k_sel), (6, k_win))):
                        dve.wait_ge(keyT_psum, slot + 1)
                        nc.vector.tensor_scalar(keys[:].rearrange("p b m -> p (b m)"), bank[b][:], cols[:, K_NORM + 1 + slot:K_NORM + 2 + slot],
                                                None, ALU.mult).then_inc(keys_ready, 1)
                if kind == NSA:
                    dve.wait_ge(wg_high, 1)
                    nc.vector.tensor_tensor(wg_lo[:], wg[:], wg_hi[:].bitcast(F32), ALU.subtract).then_inc(wg_ready, 1)
                    for j in range(2):
                        split(s0 + 2 * j + 4)
                        dve.wait_ge(q_squared, NT * (j + 1))
                        ms, rstd = q_ms[:, j, 0, :], q_ms[:, j, 1, :]
                        squares = z_sb[:, :, 512 * j:512 * (j + 1)].rearrange("p t (h d) -> p t h d", h=8)
                        step(nc.vector.tensor_reduce(ms.rearrange("p (t h) -> p t h", t=NT), squares, AX.X, ALU.add))
                        nc.vector.tensor_scalar(ms, ms, 1.0 / HD, RMS_EPS, ALU.mult, ALU.add).then_inc(q_spread, 1)
                        split(s0 + 2 * j + 5)
                        dve.wait_ge(q_rstd, j + 1)
                        for tt in range(NT):
                            for gp in range(2):
                                at = 256 * gp
                                each = rstd[:, 8 * tt + 4 * gp:8 * tt + 4 * gp + 4].unsqueeze(2).to_broadcast([P, PER_GROUP, HD])
                                ins = nc.vector.tensor_tensor(q_n[:, tt, j, :].rearrange("p (r g d) -> p r g d", r=PER_GROUP, g=2)[:, :, gp, :],
                                                              bank[2 * j + tt][:, at:at + 256].rearrange("p (r d) -> p r d", r=PER_GROUP),
                                                              each, ALU.mult)
                        ins.then_inc(q_normed, 1)
                    for j in range(2):
                        for rp in range(2):
                            dve.wait_ge(qT_psum, 2 * j + rp + 1)
                            nc.vector.tensor_scalar(qT[:, j, 2 * rp:2 * rp + 2, :].rearrange("p r m -> p (r m)"), bank[Q_T[j][rp]][:],
                                                    cols[:, Q_NORM:Q_NORM + 1], HD ** -0.5, ALU.mult, ALU.mult).then_inc(qT_ready, 1)

                    def per_query(x):
                        return x[:].unsqueeze(2).to_broadcast([P, NT, NQ, 16])

                    def per_head(x):
                        return x.unsqueeze(3).to_broadcast([P, NT, NQ, 16])

                    def row_maxima(w):
                        dve.wait_ge(sel_scored, w + 1)
                        if w >= 2:
                            dve.wait_ge(sel_exped, w - 1)
                        for b in range(3):
                            heads = 4 if b == 0 else 2
                            to = sel_max[:, w % 2, 0:4] if b == 0 else sel_max[:, w % 2, 2 + 2 * b:4 + 2 * b]
                            ins = nc.vector.tensor_reduce(to, bank[SCORES[w % 2][b]][:].rearrange("p (r m) -> p r m", r=heads), AX.X, ALU.max)
                        step(ins)
                        nc.vector.tensor_scalar(sel_max[:, w % 2, :], sel_max[:, w % 2, :], -1.0, None, ALU.mult).then_inc(sel_neg, 1)

                    def transposed_weights(w):
                        dve.wait_ge(selT_psum, w + 1)
                        if w >= 2:
                            dve.wait_ge(sel_out, w - 1)
                        nc.vector.tensor_copy(sel_pT[:, w % 2, 2, :], bank[SCORES[w % 2][2]][:]).then_inc(selT_dve, 1)

                    def add_unit(w):
                        g, branch = w // 2, 1 + w % 2
                        dve.wait_ge(sel_exped, w + 1)
                        step(nc.vector.reciprocal(sel_sum[:, w % 2, :, :], sel_sum[:, w % 2, :, :]))
                        gate = branch_gate[:].rearrange("p t (h c) -> p t h c", c=3)[:, :, PER_GROUP * g:PER_GROUP * (g + 1), branch]
                        step(nc.vector.tensor_tensor(sel_coef[:], sel_sum[:, w % 2, :, :], gate, ALU.mult))
                        dve.wait_ge(sel_out, w + 1)
                        each = sel_coef[:].rearrange("p t r -> p (t r)").unsqueeze(2).to_broadcast([P, NT * PER_GROUP, HD])
                        step(nc.vector.tensor_tensor(sel_add[:].rearrange("p (r d) -> p r d", d=HD),
                                                     bank[6 + w % 2][:].rearrange("p (r d) -> p r d", d=HD), each, ALU.mult))
                        zg = z_sb[:, :, 256 * g:256 * (g + 1)]
                        nc.vector.tensor_tensor(zg, zg, sel_add[:].rearrange("p (t n) -> p t n", t=NT), ALU.add).then_inc(attended, 1)
                        dve.wait_ge(attended, w + 1)

                    dve.wait_ge(cmp_masks, 1)
                    dve.wait_ge(cmp_scored, 1)
                    top, total = cmp_row[:, 0, :, :], cmp_row[:, 1, :, :]
                    for gp in range(2):
                        for tt in range(NT):
                            o = cmp_l[:, tt, :, :].rearrange("p (j g r) n -> p j g r n", j=2, g=2)[:, :, gp, :, :]
                            mask = cmp_mask[:, tt, :].unsqueeze(1).unsqueeze(1).to_broadcast([P, 2, PER_GROUP, 16])
                            ins = nc.vector.tensor_tensor(o, bank[1 + gp][:, tt * P:(tt + 1) * P].rearrange("p (j r n) -> p j r n", j=2, r=PER_GROUP),
                                                          mask, ALU.add)
                    step(ins)
                    step(nc.vector.tensor_reduce(top, cmp_l, AX.X, ALU.max))
                    nc.vector.tensor_tensor(cmp_l, cmp_l, per_head(top), ALU.subtract).then_inc(cmp_shifted, 1)
                    row_maxima(0)
                    dve.wait_ge(cmp_exped, 1)
                    step(nc.vector.tensor_reduce(total, cmp_l, AX.X, ALU.add))
                    step(nc.vector.reciprocal(total, total))
                    dve.wait_ge(branch_gates, 1)
                    gate = branch_gate[:].rearrange("p t (h c) -> p t h c", c=3)[:, :, :, 0]
                    step(nc.vector.tensor_tensor(total, total, gate, ALU.mult))
                    step(nc.vector.tensor_tensor(cmp_l, cmp_l, per_query(cmp_valid), ALU.mult))
                    nc.vector.tensor_tensor(cmp_p[:, :, :, 0:16], cmp_l, per_head(total), ALU.mult).then_inc(cmp_weighted, 1)
                    row_maxima(1)
                    dve.wait_ge(z_started, 2 * NT)
                    for w in range(UNITS):
                        transposed_weights(w)
                        if w > 0:
                            add_unit(w - 1)
                        if w + 2 < UNITS:
                            row_maxima(w + 2)
                    add_unit(UNITS - 1)
                    evacuate_input(inputs_before(n) + 1)
                    for d in range(KC // 2 - 1):
                        split(s0 + 4 + d + 4)
                    boundary(n, 1.0, s0 + 8)
                    split(s0 + 4 + KC // 2 - 1 + 4)
                if kind == FFN:
                    f = ffn_number[n]

                    def hidden(j, i=0):
                        dve.wait_ge(hT_high, FT * f + j + 1 + 2 * i)
                        nc.vector.tensor_tensor(hT_lo[:, bass.ds(2 * j + 4 * i, 2), :],
                                                bank[4 + j % 2][:].rearrange("p (c m) -> p c m", c=2),
                                                hT_hi[:, bass.ds(2 * j + 4 * i, 2), :].bitcast(F32),
                                                ALU.subtract).then_inc(hT_ready, 1)

                    def tile(j, i=0):
                        if not (isinstance(i, int) and j == 0):
                            hidden(j - 1, i)
                        split(s0 + 2 * j + 4, i)
                        for tt in range(NT):
                            dve.wait_ge(silu_ready, 2 * FT * f + 2 * j + tt + 1 + 4 * i)
                            nc.vector.tensor_tensor(h[:, tt, :], silu[:, tt, :], bank[2 * (j % 2) + tt][:, 256:512],
                                                    ALU.mult).then_inc(h_ready, 1)
                        split(s0 + 2 * j + 5, i)

                    for j in range(3):
                        tile(j)
                    with dve.Fori(0, (FT - 3) // 2) as i:
                        for j in range(3, 5):
                            tile(j, i)
                    for d in range(FC // 2):
                        if d == 1:
                            hidden(FT - 1)
                        if d < FC // 2 - 1:
                            split(s0 + 2 * FT + d + 4)
                    boundary(n, 0.5, s0 + 33)
                    split(s0 + 2 * FT + FC // 2 - 1 + 4)

        @block.tensor
        def _(pe):
            def product(o, x_hi, x_lo, wh, wl, first, last_one, shared=False):
                nc.tensor.matmul(o, x_lo, wh, start=first, stop=False, skip_group_check=shared)
                nc.tensor.matmul(o, x_hi, wl, start=False, stop=False, skip_group_check=shared)
                return nc.tensor.matmul(o, x_hi, wh, start=False, stop=last_one, skip_group_check=shared)

            def transpose_input(src, ready, count):
                for tt in range(NT):
                    pe.wait_ge(ready, count(tt))
                    for q in range(2):
                        for c in range(4):
                            k = 4 * q + c
                            ins = nc.tensor.transpose(TB[tt][q][:, c * P:(c + 1) * P], src[:, tt, k * P:(k + 1) * P], ident[:])
                        ins.then_inc(xT_psum, 1)

            def slab_view(slot, chunks, width):
                hi = w_hi[:, slot, 0:chunks * width].rearrange("p (k n) -> p k n", k=chunks)
                lo = w_lo[:, slot, 0:chunks * width].rearrange("p (k n) -> p k n", k=chunks)
                return hi, lo

            def project_slab(k, d, slabs, lhs_hi, lhs_lo):
                pe.wait_ge(low_ready, k + 1)
                hi, lo = slab_view(k % SLOTS, 2, D)
                for c in range(2):
                    for tt in range(NT):
                        for half in range(2):
                            at = slice(half * 512, (half + 1) * 512)
                            toks = slice(tt * P, (tt + 1) * P)
                            ins = product(Y[tt][half][:], lhs_hi[:, 2 * d + c, toks], lhs_lo[:, 2 * d + c, toks],
                                          hi[:, c, at], lo[:, c, at], d == 0 and c == 0, d == slabs - 1 and c == 1)
                ins.then_inc(slab_used, 1)

            def feature_slab(k, kh, banks, blocks):
                pe.wait_ge(low_ready, k + 1)
                hi, lo = slab_view(k % SLOTS, 4, 512)
                for c in range(4):
                    for fb in range(blocks):
                        at = slice(fb * P, (fb + 1) * P)
                        ins = product(banks[fb // 2][:, (fb % 2) * S:(fb % 2 + 1) * S], hi[:, c, at], lo[:, c, at],
                                      xT_hi[:, 4 * kh + c, :], xT_lo[:, 4 * kh + c, :],
                                      kh == 0 and c == 0 and fb % 2 == 0, kh == 1 and c == 3, shared=True)
                return ins

            def token_slab(k, kh, width, at, dst, shared=False):
                pe.wait_ge(low_ready, k + 1)
                hi, lo = slab_view(k % SLOTS, 4, width)
                for c in range(4):
                    for tt in range(NT):
                        toks = slice(tt * P, (tt + 1) * P)
                        ins = product(dst(tt), xT_hi[:, 4 * kh + c, toks], xT_lo[:, 4 * kh + c, toks], hi[:, c, at], lo[:, c, at],
                                      kh == 0 and c == 0 and not (shared and tt), kh == 1 and c == 3, shared=shared)
                return ins

            pe.wait_ge(consts, 1)
            transpose_input(x_sb, loaded_x, lambda tt: 16)
            pe.wait_ge(loaded_rows, 16 * 9)
            nc.tensor.transpose(bank[2][:, 0:ROWS], z_sb[0:ROWS, 0, 0:P], ident[0:ROWS, 0:ROWS]).then_inc(cols_psum, 1)
            pe.wait_ge(cols_ready, 1)
            for n, kind in enumerate(phases):
                s0 = first_slab[n]
                pe.wait_ge(xT_ready, 4 * (inputs_before(n) + 1))
                if kind == FFN:
                    f = ffn_number[n]

                    def gate_up(j, kh, i=0):
                        k = s0 + 2 * j + kh
                        pe.wait_ge(low_ready, k + 1 + 4 * i)
                        hi, lo = slab_view(k % SLOTS, 4, 512)
                        for c in range(4):
                            for tt in range(NT):
                                toks = slice(tt * P, (tt + 1) * P)
                                ins = product(bank[2 * (j % 2) + tt][:], xT_hi[:, 4 * kh + c, toks], xT_lo[:, 4 * kh + c, toks],
                                              hi[:, c, :], lo[:, c, :], kh == 0 and c == 0, kh == 1 and c == 3)
                        ins.then_inc(slab_used, 1)

                    def hidden(j, i=0, free=True):
                        pe.wait_ge(h_ready, 2 * FT * f + 2 * j + 2 + 4 * i)
                        if j >= 2:
                            pe.wait_ge(hT_ready, FT * f + j - 1 + 2 * i)
                        dst = bank[4 + j % 2][:].rearrange("p (c m) -> p c m", c=2)
                        for c in range(2):
                            for tt in range(NT):
                                ins = nc.tensor.transpose(dst[:, c, tt * P:(tt + 1) * P], h[:, tt, c * P:(c + 1) * P], ident[:])
                        ins.then_inc(hT_psum, 1)

                    def tile(j, i=0):
                        gate_up(j, 0, i)
                        if not (isinstance(i, int) and j == 0):
                            hidden(j - 1, i)
                        gate_up(j, 1, i)

                    for j in range(3):
                        tile(j)
                    with pe.Fori(0, (FT - 3) // 2) as i:
                        for j in range(3, 5):
                            tile(j, i)
                    if n > 0 and phases[n - 1] == KV:
                        pe.wait_ge(keys_ready, 2)
                    for d in range(FC // 2):
                        pe.wait_ge(hT_ready, FT * f + d + 1)
                        project_slab(s0 + 2 * FT + d, d, FC // 2, hT_hi, hT_lo)
                        if d == 0:
                            hidden(FT - 1)
                if kind == MIXER:
                    def free_pair(tile):
                        if tile >= 2:
                            pe.wait_ge(pair_read[tile % 2], pair_reads(tile))

                    for tile, (spans, blocks) in enumerate(QKV):
                        free_pair(tile)
                        banks, width = pair_of(tile), sum(c for _, c in spans)
                        for kh in range(2):
                            k = s0 + 2 * tile + kh
                            if blocks:
                                ins = feature_slab(k, kh, banks, blocks)
                            if blocks == 2:
                                ins = token_slab(k, kh, width, slice(256, 512), lambda tt: banks[1][:, tt * 256:(tt + 1) * 256], True)
                            if blocks == 0:
                                ins = token_slab(k, kh, width, slice(0, width), lambda tt: banks[tt][:, 0:width])
                            ins.then_inc(slab_used, 1)

                    def scores(u):
                        b, hd = u // HEADS, u % HEADS
                        if before(u) > 0:
                            pe.wait_ge(score_read, before(u))
                        for m in range(2 if b == DIFF else 1):
                            dst = bank[4 + (m if b == DIFF else u % 2)]
                            size = 32 if b == DIFF else HD
                            rows_at = slice(HD * (hd % 2) + 32 * m, HD * (hd % 2) + 32 * m + size)
                            q, key = qk[rows_at, 2 * BC * b + hd // 2, :], qk[rows_at, 2 * BC * b + BC + hd // 2, :]
                            if b == STICK:
                                for tt in range(NT):
                                    toks = slice(tt * P, (tt + 1) * P)
                                    o = dst[:, 2 * tt * P:(2 * tt + 1) * P]
                                    nc.tensor.matmul(o, q[:, toks], key[:, toks], start=True, stop=False)
                                    nc.tensor.matmul(o, ident_b[:], near[:], start=False, stop=True)
                                ins = nc.tensor.matmul(dst[:, P:2 * P], q[:, P:S], key[:, 0:P], start=True, stop=True)
                            else:
                                nc.tensor.matmul(dst[:, ROWS_A], q[:, 0:P], key[:, 0:P], start=True, stop=True)
                                ins = nc.tensor.matmul(dst[:, ROWS_B], q[:, P:S], key, start=True, stop=True)
                        ins.then_inc(scored, 1)

                    def transpose_weights(u):
                        side = 0 if u // HEADS == DIFF else u % 2
                        pe.wait_ge(prob_ready, u + 1)
                        if u > 0:
                            pe.wait_ge(probT_ready, u)
                        for i in range(3):
                            ins = nc.tensor.transpose(bank[6][:, i * P:(i + 1) * P], prob[:, side, i * P:(i + 1) * P], ident[:])
                        ins.then_inc(probT_psum, 1)

                    def outputs(u):
                        b, hd = u // HEADS, u % HEADS
                        pe.wait_ge(probT_ready, u + 1)
                        if hd % 2 == 0 and u > 0:
                            pe.wait_ge(oT_ready, u // 2)
                        dst = bank[7][HD * (hd % 2):HD * (hd % 2 + 1), :]
                        v = [v_mix[:, tt, b * BW + hd * HD:b * BW + (hd + 1) * HD] for tt in range(NT)]
                        p = probT[:, u % 2, :]
                        nc.tensor.matmul(dst[:, 0:P], v[0], p[:, 0:P], start=True, stop=True)
                        nc.tensor.matmul(dst[:, P:S], v[0], p[:, P:2 * P], start=True, stop=False)
                        nc.tensor.matmul(dst[:, P:S], v[1], p[:, 2 * P:3 * P], start=False, stop=True).then_inc(o_psum, 1)

                    def square_sums(pair):
                        pe.wait_ge(o_square, pair + 1)
                        nc.tensor.matmul(bank[7][:, S:2 * S], same_head[:], ms_d, start=True, stop=True).then_inc(o_sums, 1)

                    pe.wait_ge(pair_read[0], pair_reads(len(QKV) + 1))
                    pe.wait_ge(pair_read[1], pair_reads(len(QKV)))
                    pe.wait_ge(consts, 2)
                    scores(0)
                    scores(1)
                    for b in range(3):
                        g0 = s0 + 14 + 6 * b
                        for hd in range(HEADS):
                            u = b * HEADS + hd
                            if b == DIFF and hd in (3, 5):
                                square_sums(hd // 2 - 1)
                            if hd < 4:
                                tile = gate_tile(b, hd // 2)
                                if hd % 2 == 0:
                                    free_pair(tile)
                                token_slab(g0 + hd, hd % 2, 512, slice(0, 512), lambda tt: pair_of(tile)[tt][:]).then_inc(slab_used, 1)
                            transpose_weights(u)
                            for ahead in {MOBA: [u + 2] if hd < 4 else [u + 1] if hd == 5 else [],
                                          DIFF: [u + 1] if hd < 5 else [u + 1, u + 2],
                                          STICK: [u + 2] if hd < 4 else []}[b]:
                                scores(ahead)
                            if hd > 0:
                                outputs(u - 1)
                        outputs(b * HEADS + HEADS - 1)
                        if b == DIFF:
                            square_sums(2)
                        pe.wait_ge(oT_ready, BC * (b + 1))
                        for half in range(2):
                            k, tile = g0 + 4 + half, branch_tile(b, half)
                            free_pair(tile)
                            pe.wait_ge(low_ready, k + 1)
                            hi, lo = slab_view(k % SLOTS, BC, 512)
                            for c in range(BC):
                                for tt in range(NT):
                                    toks = slice(tt * P, (tt + 1) * P)
                                    ins = product(pair_of(tile)[tt][:], oT_hi[:, c, toks], oT_lo[:, c, toks], hi[:, c, :], lo[:, c, :],
                                                  c == 0, c == BC - 1)
                            ins.then_inc(slab_used, 1)
                    transpose_input(z_sb, merged, lambda tt: 12)
                    pe.wait_ge(xT_ready, 4 * (inputs_before(n) + 2))
                    for d in range(KC // 2):
                        project_slab(s0 + 32 + d, d, KC // 2, xT_hi, xT_lo)
                if kind == CONV:
                    for j in range(6):
                        if j >= 2:
                            pe.wait_ge(conv_v_ready, j - 1)
                        for kh in range(2):
                            feature_slab(s0 + 2 * j + kh, kh, [bank[4 * (j % 2)], bank[4 * (j % 2) + 1]], 4)\
                                .then_inc(slab_used, 1)
                    for d in range(KC // 2):
                        pe.wait_ge(yT_ready, d + 1)
                        project_slab(s0 + 12 + d, d, KC // 2, yT_hi, yT_lo)
                if kind == KV:
                    for kh in range(2):
                        feature_slab(s0 + kh, kh, [bank[0], bank[1]], 4).then_inc(slab_used, 1)
                    for kv in range(2):
                        pe.wait_ge(xc_ready, 1 + 4 * (kv + 1))
                        for part in range(2):
                            k = s0 + 2 + 2 * kv + part
                            pe.wait_ge(low_ready, k + 1)
                            hi, lo = slab_view(k % SLOTS, 8, 256)
                            for c in range(8):
                                chunk = 8 * part + c
                                at = slice(2 * chunk, 2 * chunk + 241, 16)
                                for hb in range(2):
                                    cols_of = slice(hb * P, (hb + 1) * P)
                                    o = bank[6 + kv][:, hb * 64:(hb + 1) * 64].rearrange("p (g n) -> p g n", g=GROUPS)
                                    product(o, hi[:, c, cols_of], lo[:, c, cols_of], xc_hi[:, kv, :, at], xc_lo[:, kv, :, at],
                                            chunk == 0 and hb == 0, chunk == 15, shared=True)
                                    o = bank[6 + kv][:, 128 + 2 * hb:130 + 2 * hb]
                                    nc.tensor.matmul(o, lo[:, c, cols_of], pos[:, 16 * kv + chunk, :], start=False, stop=False, skip_group_check=True)
                                    ins = nc.tensor.matmul(o, hi[:, c, cols_of], pos[:, 16 * kv + chunk, :], start=False, stop=chunk == 15,
                                                           skip_group_check=True)
                            ins.then_inc(slab_used, 1)
                    for kh in range(2):
                        token_slab(s0 + 6 + kh, kh, 512, slice(0, 512), lambda tt: bank[4 + tt][:]).then_inc(slab_used, 1)
                    pe.wait_ge(loaded_kv, 32)
                    pe.wait_ge(hid_ready, 4)
                    for hb in range(2):
                        ins = nc.tensor.matmul(bank[6][0:GROUPS * 16, 256:256 + HD], hid[:, 0, hb, :], cmp_w2[:, 0, hb, :], start=hb == 0, stop=hb == 1)
                    ins.then_inc(cmp_psum, 1)
                    pe.wait_ge(hid_v_ready, 1)
                    for g in range(GROUPS):
                        for hb in range(2):
                            ins = nc.tensor.matmul(bank[7][:, S + g * HD:S + (g + 1) * HD], hid_v[:, hb, g, :, :].rearrange("p r n -> p (r n)"),
                                                   cmp_w2[:, 1, hb, :], start=hb == 0, stop=hb == 1)
                    ins.then_inc(cmp_psum, 1)
                    for kh in range(2):
                        token_slab(s0 + 8 + kh, kh, 512, slice(0, 512), lambda tt: bank[2 + tt][:]).then_inc(slab_used, 1)
                    pe.wait_ge(kc_normed, 1)
                    nc.tensor.transpose(bank[6][:, 384:384 + GROUPS * 16], kc_n[:], ident[0:GROUPS * 16, 0:GROUPS * 16]).then_inc(kcT_psum, 1)

                    def transpose_keys(slot, b):
                        pe.wait_ge(key_normed, slot + 1)
                        for blk in range(2):
                            for tt in range(NT):
                                o = bank[b][:, blk * S + tt * P:blk * S + (tt + 1) * P]
                                ins = nc.tensor.transpose(o, key_n[:, slot, tt, blk * P:(blk + 1) * P], ident[:])
                        ins.then_inc(keyT_psum, 1)

                    pe.wait_ge(cmp_ready, 1)
                    transpose_keys(0, 7)
                    pe.wait_ge(cmp_ready, 2)
                if kind == NSA:
                    for j in range(2):
                        for kh in range(2):
                            token_slab(s0 + 2 * j + kh, kh, 512, slice(0, 512), lambda tt: bank[2 * j + tt][:]).then_inc(slab_used, 1)
                    pe.wait_ge(wg_ready, 1)
                    for c in range(KC):
                        for tt in range(NT):
                            toks = slice(tt * P, (tt + 1) * P)
                            ins = product(bank[4][:, tt * 3 * NQ:(tt + 1) * 3 * NQ], xT_hi[:, c, toks], xT_lo[:, c, toks], wg_hi[:, c, :], wg_lo[:, c, :],
                                          c == 0 and tt == 0, c == KC - 1, shared=True)
                    ins.then_inc(gates_psum, 1)
                    for j in range(2):
                        pe.wait_ge(q_normed, j + 1)
                        for rp in range(2):
                            for r in range(2):
                                for tt in range(NT):
                                    at = slice((2 * rp + r) * P, (2 * rp + r + 1) * P)
                                    o = bank[Q_T[j][rp]][:, r * S + tt * P:r * S + (tt + 1) * P]
                                    ins = nc.tensor.transpose(o, q_n[:, tt, j, at], ident[:])
                            ins.then_inc(qT_psum, 1)

                    def query(g, r, tt):
                        return qT[HD * (g % 2):HD * (g % 2 + 1), g // 2, r, tt * P:(tt + 1) * P]

                    def scores(w):
                        g, keys = w // 2, (k_sel, k_win)[w % 2]
                        key = keys[HD * (g % 2):HD * (g % 2 + 1), g // 2, :]
                        if w >= 2:
                            pe.wait_ge(selT_act, w - 1)
                            pe.wait_ge(selT_dve, w - 1)
                        banks = [bank[i] for i in SCORES[w % 2]]
                        for b in range(3):
                            heads = 4 if b == 0 else 2
                            o = banks[b][:].rearrange("p (r m) -> p r m", r=heads)[:, :, (S - P) * (b > 0):]
                            nc.tensor.matmul(o, ident_b[:], causal[:].unsqueeze(1).to_broadcast([P, heads, P]), start=True, stop=False,
                                             skip_group_check=True)
                        for tt in range(NT):
                            for r in range(PER_GROUP):
                                b, at = score_place(tt, r)
                                ins = nc.tensor.matmul(banks[b][:, at], query(g, r, tt), key[:, 0:P * (tt + 1)], start=False, stop=True,
                                                       skip_group_check=True)
                        ins.then_inc(sel_scored, 1)

                    def transpose_weights(w):
                        pe.wait_ge(sel_exped, w + 1)
                        for b in range(3):
                            for i in range(4):
                                at = slice(i * P, (i + 1) * P)
                                ins = nc.tensor.transpose(bank[SCORES[w % 2][b]][:, at], sel_p[:, w % 2, b, at], ident[:])
                        ins.then_inc(selT_psum, 1)

                    def outputs(w):
                        g, values = w // 2, (v_sel, v_win)[w % 2]
                        pe.wait_ge(selT_act, w + 1)
                        pe.wait_ge(selT_dve, w + 1)
                        if w >= 2:
                            pe.wait_ge(attended, w - 1)
                        for tt in range(NT):
                            for r in range(PER_GROUP):
                                b, at = score_place(tt, r)
                                o = bank[6 + w % 2][:, (tt * PER_GROUP + r) * HD:(tt * PER_GROUP + r + 1) * HD]
                                for key_tile in range(tt + 1):
                                    p = sel_pT[:, w % 2, b, at.start + key_tile * P:at.start + (key_tile + 1) * P]
                                    ins = nc.tensor.matmul(o, p, values[:, key_tile, g * HD:(g + 1) * HD], start=key_tile == 0, stop=key_tile == tt)
                        ins.then_inc(sel_out, 1)

                    pe.wait_ge(qT_ready, 4)
                    for tt in range(NT):
                        for hd in range(NQ):
                            g, r = hd // PER_GROUP, hd % PER_GROUP
                            at = tt * P + (g // 2 * PER_GROUP + r) * 16
                            o = bank[1 + g % 2][:, at:at + 16]
                            ins = nc.tensor.matmul(o, query(g, r, tt), k_cmp[HD * (g % 2):HD * (g % 2 + 1), 16 * g:16 * (g + 1)], start=True, stop=True)
                    ins.then_inc(cmp_scored, 1)
                    pe.wait_ge(branch_gates, 1)
                    pe.wait_ge(consts, 2)
                    scores(0)
                    pe.wait_ge(cmp_weighted, 1)
                    for tt in range(NT):
                        for g in range(GROUPS):
                            p = cmp_p[:, tt, PER_GROUP * g:PER_GROUP * (g + 1), :].rearrange("p r n -> p (r n)")
                            ins = nc.tensor.transpose(bank[2 * tt][:, g * P:(g + 1) * P], p, ident[:])
                        ins.then_inc(cmpT_psum, 1)
                    for tt in range(NT):
                        pe.wait_ge(cmpT_ready, tt + 1)
                        for g in range(GROUPS):
                            o = bank[CMP_OUT[tt][g // 2]][:, (g % 2) * S:(g % 2 + 1) * S]
                            ins = nc.tensor.matmul(o, cmp_pT[:, tt, g, :], v_cmp[:, g, :], start=True, stop=True)
                        ins.then_inc(cmp_out, 1)
                    pe.wait_ge(z_started, 2 * NT)
                    scores(1)
                    for w in range(UNITS):
                        transpose_weights(w)
                        if w > 0:
                            outputs(w - 1)
                        if w + 2 < UNITS:
                            scores(w + 2)
                    outputs(UNITS - 1)
                    transpose_input(z_sb, attended, lambda tt: UNITS)
                    pe.wait_ge(xT_ready, 4 * (inputs_before(n) + 2))
                    for d in range(KC // 2):
                        project_slab(s0 + 4 + d, d, KC // 2, xT_hi, xT_lo)
                if n < last:
                    transpose_input(operand(n + 1), normed, lambda tt: normed_before(n + 1) - NT + tt + 1)
                if kind == KV:
                    transpose_keys(1, 6)


_INS = ["x", "ln_g", "ln_b", "ffn_w_gate", "ffn_w_up", "ffn_w_down", "w_in", "b_gate", "diff_lambda", "diff_subln_g",
        "w_br_moba", "w_br_diff", "w_br_sb", "w_out", "ffn_norm_2", "ffn_w_gate_up_2", "ffn_w_down_2", "mix_norm_2",
        "conv_w_in_2", "conv_w_2", "conv_w_out_2", "kv_norm_2", "kv_w_2", "cmp_pos_2", "cmp_w1_2", "cmp_b1_2",
        "cmp_w2_2", "k_norm_2", "nsa_w_qg_2", "q_norm_2", "nsa_w_o_2"]


def kernel(**inputs):
    import numpy as _np
    import concourse.bacc as _bacc
    from concourse import mybir as _mybir
    from concourse.bass_utils import run_bass_kernel_spmd as _run

    nc = _bacc.Bacc("TRN2", target_bir_lowering=False, num_devices=1)
    arrays, t = {}, {}
    for name in _INS:
        a = _np.ascontiguousarray(inputs[name])
        arrays[f"in_{name}_dram"] = a
        t[name] = nc.dram_tensor(f"in_{name}_dram", a.shape, _mybir.dt.from_np(a.dtype), kind="ExternalInput").ap()
    out = nc.dram_tensor("out_0_dram", (1, S, D), _mybir.dt.float32, kind="ExternalOutput").ap()
    two_block_kernel(nc, t, out[0])
    r = _run(nc, [arrays], core_ids=[0])
    return r.results[0]["out_0_dram"]
```

```python
from contextlib import ExitStack

import concourse.bass as bass
from concourse import mybir

F32 = mybir.dt.float32
F32R = mybir.dt.float32r
BF16 = mybir.dt.bfloat16
ALU = mybir.AluOpType
ACT = mybir.ActivationFunctionType
AX = mybir.AxisListType

P = 128
D = 1024
KC = D // P
S = 256
NT = S // P
FF = 2816
FT = FF // 256
FC = FF // P
SLOTS = 4
SLAB = 2048
HD = 64
BW = 384
BC = BW // P
BRANCH_HEADS = BW // HD
ALPHA = 2.0 ** 0.25
LN_EPS = 1e-5
SUBLN_EPS = 1e-5
RMS_EPS = 1e-6
LAMBDA_INIT = 0.8 - 0.6
DIFF_SCALE = 32.0 ** -0.5
MASKED = -1e30
N_CMP = 15
GROUPS = 4
PER_GROUP = 4
CMP_HID = 256
CMP_ROWS = 16 * (GROUPS + 1)
XC = CMP_ROWS * 16 + 16

CONV_W, POS, CMP_B, Q_NORM, K_NORM, SUBLN, ROWS = 0, 24, 56, 60, 61, 64, 65

FFN, MIXER, CONV, KV, NSA = "ffn", "mixer", "conv", "kv", "nsa"
PHASES = [FFN, MIXER, FFN, FFN, CONV, FFN, KV, FFN, NSA, FFN]
LENGTH = {FFN: 33, MIXER: 36, CONV: 16, KV: 10, NSA: 8}
STOP = len(PHASES)


def alibi_slope(i):
    return 2.0 ** (-8.0 * (i + 1) / 12.0)


def two_block_kernel(nc, t, out):
    phases = PHASES[:STOP]
    first_slab = [sum(LENGTH[k] for k in phases[:n]) for n in range(len(phases) + 1)]
    TOTAL = first_slab[-1]
    ffn_number = [sum(k == FFN for k in phases[:n]) for n in range(len(phases))]

    with ExitStack() as ctx:
        def sb(name, shape, dt=F32):
            return ctx.enter_context(nc.sbuf_tensor(name, shape, dt))

        def sem(name):
            return ctx.enter_context(nc.semaphore(name))

        raw = sb("raw", [P, SLOTS, SLAB])
        w_hi = sb("w_hi", [P, SLOTS, SLAB], F32R)
        w_lo = sb("w_lo", [P, SLOTS, SLAB], F32R)
        x_sb = sb("x_sb", [P, NT, D])
        z_sb = sb("z_sb", [P, NT, D])
        xT_hi = sb("xT_hi", [P, KC, S], F32R)
        xT_lo = sb("xT_lo", [P, KC, S], F32R)
        gain = sb("gain", [P, 3, D])
        stats = sb("stats", [P, 64])
        bn = sb("bn", [P, NT, 2, 6])
        head_max = sb("head_max", [P, 2, 4])
        head_sum = sb("head_sum", [P, 2, 4])
        lam_col = sb("lam_col", [P, 8])
        near = sb("near", [P, P], BF16)
        causal = sb("causal", [P, P], BF16)
        same_head = sb("same_head", [P, P])
        minus_half = sb("minus_half", [P, 32])
        ident = sb("ident", [P, P])
        ident_b = sb("ident_b", [P, P], BF16)
        cols = sb("cols", [P, 80])

        bank = [ctx.enter_context(nc.psum_tensor(f"bank{i}", [P, 512], F32)) for i in range(8)]
        Y = [[bank[2], bank[3]], [bank[6], bank[7]]]
        TB = [[bank[0], bank[1]], [bank[4], bank[5]]]

        def layer_memory(tensors):
            with ExitStack() as own:
                return [own.enter_context(nc.sbuf_tensor(n, s, d)) for n, s, d in tensors]

        qk, v_mix, oT_hi, oT_lo, gates, b_gate, prob, probT, far, tmp, o_norm = layer_memory([
            ("qk", [P, 6 * BC, S], F32),
            ("v_mix", [P, NT, 3 * BW], F32),
            ("oT_hi", [P, BC, S], F32R), ("oT_lo", [P, BC, S], F32R),
            ("gates", [P, NT, D], F32), ("b_gate", [P, 3, D], F32),
            ("prob", [P, 2, BW], F32),
            ("probT", [P, 2, BW], F32),
            ("far", [P, BW], F32),
            ("tmp", [P, 512], F32), ("o_norm", [P, 2, S], F32)])
        ms_d, o_f, o_root = o_norm[:, 0, :], o_norm[:, 1, :], tmp[:, S:2 * S]
        stick = far
        k_sel = sb("k_sel", [P, 2, S])
        k_win = sb("k_win", [P, 2, S])
        v_sel = sb("v_sel", [P, NT, S])
        v_win = sb("v_win", [P, NT, S])
        k_cmp = sb("k_cmp", [P, GROUPS * 16])
        v_cmp = sb("v_cmp", [P, GROUPS, PER_GROUP * HD])
        xc_hi, xc_lo, hid_row, cmp_w2, hid, hid_v, key_sq, key_n, key_ms, cmp_bias, kc_sq, kc_n, kc_ms = layer_memory([
            ("xc_hi", [P, 2, XC], F32R), ("xc_lo", [P, 2, XC], F32R),
            ("hid_row", [CMP_ROWS, 2, CMP_HID], F32),
            ("cmp_w2", [P, 2, 2, HD], F32), ("hid", [P, 2, 2, GROUPS * 16], F32),
            ("hid_v", [P, 2, GROUPS, PER_GROUP, 32], F32),
            ("key_sq", [P, 2, NT, S], F32), ("key_n", [P, 2, NT, S], F32), ("key_ms", [P, 2, 2, NT * GROUPS], F32),
            ("cmp_bias", [P, 2, 2], F32), ("kc_sq", [GROUPS * 16, HD], F32), ("kc_n", [GROUPS * 16, 2 * HD], F32),
            ("kc_ms", [GROUPS * 16, 4], F32)])
        NQ = D // HD
        wg, wg_hi, wg_lo, branch_gate, q_ms, qT, sel_p, sel_pT, cmp_p, cmp_pT, cmp_mask, cmp_valid, cmp_row, sel_max, sel_sum, \
            sel_coef, sel_add = layer_memory([
                ("wg", [P, KC, 3 * NQ], F32), ("wg_hi", [P, KC, 3 * NQ], F32R), ("wg_lo", [P, KC, 3 * NQ], F32R),
                ("branch_gate", [P, NT, 3 * NQ], F32), ("q_ms", [P, 2, 2, NQ], F32),
                ("qT", [P, 2, PER_GROUP, S], F32),
                ("sel_p", [P, 2, 3, 512], F32), ("sel_pT", [P, 2, 3, 512], F32),
                ("cmp_p", [P, NT, NQ, 32], F32), ("cmp_pT", [P, NT, GROUPS, P], F32),
                ("cmp_mask", [P, NT, 16], F32), ("cmp_valid", [P, NT, 16], F32), ("cmp_row", [P, 2, NT, NQ], F32),
                ("sel_max", [P, 2, 8], F32), ("sel_sum", [P, 2, NT, PER_GROUP], F32), ("sel_coef", [P, 2, NT, PER_GROUP], F32),
                ("sel_add", [P, 512], F32)])
        q_n = sel_pT[:].rearrange("p a b c -> p (a b c)")[:, 0:NT * D].rearrange("p (t n c) -> p t n c", t=NT, n=2)
        cmp_l = sel_add[:].rearrange("p (t h n) -> p t h n", t=NT, h=NQ)
        hT_hi, hT_lo, silu, h = layer_memory([
            ("hT_hi", [P, FC, S], F32R), ("hT_lo", [P, FC, S], F32R),
            ("silu", [P, NT, 256], F32), ("h", [P, NT, 256], F32)])
        conv_v, conv_a, conv_c, conv_y, yT_hi, yT_lo = layer_memory([
            ("conv_v", [P, KC, S + 2], F32), ("conv_a", [P, KC, S], F32), ("conv_c", [P, 2, 512], F32),
            ("conv_y", [P, 2, 512], F32), ("yT_hi", [P, KC, S], F32R), ("yT_lo", [P, KC, S], F32R)])

        arrived = [sem(f"arrived{i}") for i in range(SLOTS)]
        high_ready = sem("high_ready")
        low_ready = sem("low_ready")
        slab_used = sem("slab_used")
        loaded_x = [sem(f"loaded_x{i}") for i in range(NT)]
        loaded_p = sem("loaded_p")
        loaded_mix = sem("loaded_mix")
        loaded_lam = sem("loaded_lam")
        lam_dots = sem("lam_dots")
        lam_exp = sem("lam_exp")
        pair_read = [sem("pair0_read"), sem("pair1_read")]
        far_ready = sem("far_ready")
        scored = sem("scored")
        score_read = sem("score_read")
        neg_ready = sem("neg_ready")
        exped = sem("exped")
        logs = sem("logs")
        prob_ready = sem("prob_ready")
        probT_psum = sem("probT_psum")
        probT_ready = sem("probT_ready")
        o_psum = sem("o_psum")
        o_copied = sem("o_copied")
        o_square = sem("o_square")
        o_sums = sem("o_sums")
        o_spread = sem("o_spread")
        o_log = sem("o_log")
        o_rstd = sem("o_rstd")
        o_normed = sem("o_normed")
        oT_high = sem("oT_high")
        oT_ready = sem("oT_ready")
        gate_sum = sem("gate_sum")
        gated = sem("gated")
        merged = sem("merged")
        conv_c_ready = sem("conv_c_ready")
        conv_v_ready = sem("conv_v_ready")
        conv_y_ready = sem("conv_y_ready")
        yT_high = sem("yT_high")
        yT_ready = sem("yT_ready")
        loaded_kv = sem("loaded_kv")
        xc_high = sem("xc_high")
        xc_ready = sem("xc_ready")
        xc_zero = sem("xc_zero")
        hid_rows = sem("hid_rows")
        hidT_psum = sem("hidT_psum")
        bias_ready = sem("bias_ready")
        hid_ready = sem("hid_ready")
        hid_v_ready = sem("hid_v_ready")
        cmp_psum = sem("cmp_psum")
        kc_squared = sem("kc_squared")
        kc_spread = sem("kc_spread")
        kc_rstd = sem("kc_rstd")
        kc_normed = sem("kc_normed")
        kcT_psum = sem("kcT_psum")
        cmp_ready = sem("cmp_ready")
        key_squared = sem("key_squared")
        key_spread = sem("key_spread")
        key_rstd = sem("key_rstd")
        key_normed = sem("key_normed")
        keyT_psum = sem("keyT_psum")
        keys_ready = sem("keys_ready")
        values_ready = sem("values_ready")
        loaded_wg = sem("loaded_wg")
        wg_high = sem("wg_high")
        wg_ready = sem("wg_ready")
        gates_psum = sem("gates_psum")
        branch_gates = sem("branch_gates")
        q_squared = sem("q_squared")
        q_spread = sem("q_spread")
        q_rstd = sem("q_rstd")
        q_normed = sem("q_normed")
        qT_psum = sem("qT_psum")
        qT_ready = sem("qT_ready")
        cmp_masks = sem("cmp_masks")
        cmp_scored = sem("cmp_scored")
        cmp_shifted = sem("cmp_shifted")
        cmp_exped = sem("cmp_exped")
        cmp_weighted = sem("cmp_weighted")
        cmpT_psum = sem("cmpT_psum")
        cmpT_ready = sem("cmpT_ready")
        cmp_out = sem("cmp_out")
        z_started = sem("z_started")
        sel_scored = sem("sel_scored")
        sel_neg = sem("sel_neg")
        sel_exped = sem("sel_exped")
        sel_weighed = sem("sel_weighed")
        selT_psum = sem("selT_psum")
        selT_act = sem("selT_act")
        selT_dve = sem("selT_dve")
        sel_out = sem("sel_out")
        attended = sem("attended")
        consts = sem("consts")
        cols_psum = sem("cols_psum")
        cols_ready = sem("cols_ready")
        gain_loaded = [sem(f"gain_loaded{i}") for i in range(3)]
        scaled = sem("scaled")
        y_ready = sem("y_ready")
        summed = sem("summed")
        squared = sem("squared")
        spread = sem("spread")
        rstd_ready = sem("rstd_ready")
        normed = sem("normed")
        xT_psum = sem("xT_psum")
        xT_high = sem("xT_high")
        xT_ready = sem("xT_ready")
        silu_ready = sem("silu_ready")
        h_ready = sem("h_ready")
        hT_psum = sem("hT_psum")
        hT_high = sem("hT_high")
        hT_ready = sem("hT_ready")
        act_step = sem("act_step")
        loaded_rows = sem("loaded_rows")
        dve_step = sem("dve_step")
        pool_step = sem("pool_step")
        stored = sem("stored")

        LN, RMS = "ln", "rms"
        ln_row = {0: 0, 1: 1, 2: 2}
        rms_of = {2: t["ffn_norm_2"][0, 0], 3: t["mix_norm_2"][0], 4: t["ffn_norm_2"][0, 1], 5: t["kv_norm_2"],
                  6: t["ffn_norm_2"][1, 0], 7: t["mix_norm_2"][1], 8: t["ffn_norm_2"][1, 1]}
        last = len(phases) - 1

        def has_ln(n):
            return n in ln_row

        def has_rms(n):
            return n in rms_of and n < last

        def operand(n):
            return x_sb if n in (0, 1, 2) else z_sb

        ln_uses = [sum(has_ln(m) for m in range(n)) for n in range(len(phases) + 1)]
        rms_uses = [sum(has_rms(m) for m in range(n)) for n in range(len(phases) + 1)]
        y_layers = [sum(k != KV for k in phases[:n]) for n in range(len(phases) + 1)]

        def normed_before(n):
            return NT * (ln_uses[n] + rms_uses[n])

        def summed_before(n):
            return NT * y_layers[n]

        HEADS = BRANCH_HEADS
        MOBA, DIFF, STICK = range(3)
        QKV = {"q, k of moba": ([(0, 256), (256, 256)], 4, 0), "k of moba, q of diff": ([(512, 256), (1152, 256)], 4, 4),
               "v of moba, sb": ([(768, 384), (3328, 128)], 0, 0), "q, k of diff": ([(1408, 256), (1664, 256)], 4, 8),
               "v of diff": ([(1920, 192), (2112, 192)], 0, 0), "q, k of sb": ([(2304, 256), (2560, 256)], 4, 12),
               "k, v of sb": ([(2816, 256), (3072, 256)], 2, 16)}
        GATE0 = 3 * 3 * BW
        TILES = [("q, k of moba",), ("k of moba, q of diff",), ("v of moba, sb",), ("q, k of diff",), ("v of diff",),
                 ("gate", MOBA, 0), ("gate", MOBA, 1), ("branch", MOBA, 0), ("branch", MOBA, 1),
                 ("q, k of sb",), ("k, v of sb",), ("gate", DIFF, 0), ("gate", DIFF, 1), ("branch", DIFF, 0), ("branch", DIFF, 1),
                 ("gate", STICK, 0), ("gate", STICK, 1), ("branch", STICK, 0), ("branch", STICK, 1)]
        MIX_SLABS = [(i, kh) for i, what in enumerate(TILES) for kh in range(1 if what[0] == "branch" else 2)]
        STEPS = [6] + [1] * 8 + [2] * 4 + [1, 1, 2, 1, 1, 1] + [3]
        ROUND = [range(sum(STEPS[:i]), sum(STEPS[:i + 1])) for i in range(len(STEPS))]
        assert ROUND[-1].stop == len(MIX_SLABS) and len(STEPS) == 3 * HEADS + 2

        def pair_of(tile):
            return [bank[2 * (tile % 2)], bank[2 * (tile % 2) + 1]]

        def pair_reads(tile):
            return 2 * (tile // 2)

        def ends(d):
            tile, kh = MIX_SLABS[d]
            return tile if kh == 1 or TILES[tile][0] == "branch" else None

        def branch_slab(b, half):
            return MIX_SLABS.index((TILES.index(("branch", b, half)), 0))

        def before(u):
            return u if u // HEADS == DIFF or u == 2 * HEADS else u - 1

        ROWS_A, ROWS_B = slice(0, P), slice(P, 3 * P)

        def tokens_of(x):
            return x[:, :, 0:16 * CMP_ROWS].rearrange("p a (g t) -> p a g t", t=S)

        def hidden_of(kv, hb):
            return bank[6 + kv][:, CMP_HID + hb * CMP_ROWS:CMP_HID + (hb + 1) * CMP_ROWS]

        UNITS = 2 * GROUPS
        Q_T = [[5, 6], [7, 0]]
        SCORES = [[3, 4, 5], [0, 1, 2]]
        CMP_OUT = [[6, 7], [1, 0]]

        def score_place(tt, r):
            return (0, slice(r * P, (r + 1) * P)) if tt == 0 else (1 + r // 2, slice((r % 2) * S, (r % 2 + 1) * S))

        def ffn_weights(f):
            if f < 2:
                return t["ffn_w_gate"][0, f], t["ffn_w_up"][0, f], t["ffn_w_down"][0, f]
            both = t["ffn_w_gate_up_2"][(f - 2) // 2, (f - 2) % 2]
            return both[:, 0:FF], both[:, FF:2 * FF], t["ffn_w_down_2"][(f - 2) // 2, (f - 2) % 2]

        def half_rows(w, kh):
            return w[kh * 512:(kh + 1) * 512, :].rearrange("(k p) n -> p k n", p=P)

        def inputs_before(n):
            return n + sum(k in (MIXER, NSA) for k in phases[:n])

        def width_of(k):
            n = max(m for m in range(len(phases)) if first_slab[m] <= k)
            d = k - first_slab[n]
            narrow = phases[n] == MIXER and d < len(MIX_SLABS) and TILES[MIX_SLABS[d][0]][0] in ("v of diff", "branch")
            return 4 * BW if narrow else SLAB

        block = ctx.enter_context(nc.Block())

        @block.sync
        def _(sp):
            def load(k, pieces, i=0):
                slot = k % SLOTS
                if k >= SLOTS:
                    sp.wait_ge(low_ready, k - SLOTS + 1 + 4 * i)
                for dst, src in pieces(slot):
                    sp.dma_start(dst, src).then_inc(arrived[slot], 32 // len(pieces(slot)))

            def columns(w, kh, spans, width=512):
                def pieces(slot):
                    dst = raw[:, slot, 0:4 * width].rearrange("p (k n) -> p k n", k=4)
                    at, found = 0, []
                    for c0, n in spans:
                        found.append((dst[:, :, at:at + n], half_rows(w, kh)[:, :, c0:c0 + n]))
                        at += n
                    return found
                return pieces

            def rows(w, c0, chunks=2):
                def pieces(slot):
                    return [(raw[:, slot, j * D:(j + 1) * D], w[(c0 + j) * P:(c0 + j + 1) * P, :]) for j in range(chunks)]
                return pieces

            def gain_row(row, src, n_before):
                sp.dma_start(gain[:, row, :], src.partition_broadcast(P)).then_inc(gain_loaded[row], 16)

            def gains(n):
                if n > 0:
                    sp.wait_ge(normed, normed_before(n))
                if has_ln(n):
                    gain_row(0, t["ln_g"][0, ln_row[n]], n)
                    gain_row(1, t["ln_b"][0, ln_row[n]], n)
                if has_rms(n):
                    gain_row(2, rms_of[n], n)

            for tt in range(NT):
                sp.dma_start(x_sb[:, tt, :], t["x"][0, tt * P:(tt + 1) * P, :]).then_inc(loaded_x[tt], 16)
            for n, kind in enumerate(phases):
                s0 = first_slab[n]
                if kind == FFN:
                    gate, up, down = ffn_weights(ffn_number[n])

                    def gate_up(j, kh, i=0):
                        def pieces(slot):
                            dst = raw[:, slot, :].rearrange("p (k n) -> p k n", k=4)
                            at = bass.ds(256 * j + 512 * i, 256)
                            return [(dst[:, :, 0:256], half_rows(gate, kh)[:, :, at]),
                                    (dst[:, :, 256:512], half_rows(up, kh)[:, :, at])]
                        load(s0 + 2 * j + kh, pieces, i)

                    for j in range(3):
                        for kh in range(2):
                            gate_up(j, kh)
                    with sp.Fori(0, (FT - 3) // 2) as i:
                        for j in range(3, 5):
                            for kh in range(2):
                                gate_up(j, kh, i)
                    gains(n)
                    for d in range(FC // 2):
                        load(s0 + 2 * FT + d, rows(down, 2 * d))
                elif kind == MIXER:
                    w = t["w_in"][0]
                    for d, (tile, kh) in enumerate(MIX_SLABS):
                        what = TILES[tile]
                        if d == ROUND[0].stop:
                            gains(n)
                            sp.wait_ge(normed, normed_before(n))
                            sp.dma_start(b_gate[:], t["b_gate"][0].partition_broadcast(P)).then_inc(loaded_mix, 16)
                        if what[0] == "gate":
                            c0 = GATE0 + what[1] * D + what[2] * 512
                            load(s0 + d, columns(w, kh, [(c0, 256), (c0 + 256, 256)]))
                        elif what[0] == "branch":
                            wb = t[("w_br_moba", "w_br_diff", "w_br_sb")[what[1]]][0]
                            src = wb[:, what[2] * 512:(what[2] + 1) * 512].rearrange("(k p) n -> p k n", p=P)

                            def pieces(slot):
                                dst = raw[:, slot, 0:BC * 512].rearrange("p (k n) -> p k n", k=BC)
                                return [(dst[:, :, 0:256], src[:, :, 0:256]), (dst[:, :, 256:512], src[:, :, 256:512])]
                            load(s0 + d, pieces)
                        else:
                            spans = QKV[what[0]][0]
                            load(s0 + d, columns(w, kh, spans, sum(c for _, c in spans)))
                    for d in range(KC // 2):
                        load(s0 + 32 + d, rows(t["w_out"][0], 2 * d))
                elif kind == CONV:
                    w = t["conv_w_in_2"][0]
                    for j in range(4):
                        for kh in range(2):
                            load(s0 + 2 * j + kh, columns(w, kh, [(D + 256 * j, 256), (2 * D + 256 * j, 256)]))
                    for j in range(2):
                        for kh in range(2):
                            load(s0 + 8 + 2 * j + kh, columns(w, kh, [(512 * j, 256), (512 * j + 256, 256)]))
                    gains(n)
                    for d in range(KC // 2):
                        load(s0 + 12 + d, rows(t["conv_w_out_2"][0], 2 * d))
                elif kind == KV:
                    w = t["kv_w_2"]
                    for kh in range(2):
                        load(s0 + kh, columns(w, kh, [(0, 256), (256, 256)]))
                    for kv in range(2):
                        for part in range(2):
                            src = t["cmp_w1_2"][kv, part * 1024:(part + 1) * 1024, :].rearrange("(k p) n -> p k n", p=P)

                            def pieces(slot):
                                dst = raw[:, slot, :].rearrange("p (k n) -> p k n", k=8)
                                return [(dst[:, 0:4, :], src[:, 0:4, :]), (dst[:, 4:8, :], src[:, 4:8, :])]
                            load(s0 + 2 + 2 * kv + part, pieces)
                    gains(n)
                    for kv in range(2):
                        sp.dma_start(cmp_w2[:, kv, :, :], t["cmp_w2_2"][kv].rearrange("(b p) d -> p b d", p=P)).then_inc(loaded_kv, 16)
                    for slot in range(2):
                        for kh in range(2):
                            load(s0 + 6 + 2 * slot + kh, columns(w, kh, [(512 * (slot + 1), 256), (512 * (slot + 1) + 256, 256)]))
                elif kind == NSA:
                    w = t["nsa_w_qg_2"][0]
                    for j in range(2):
                        for kh in range(2):
                            load(s0 + 2 * j + kh, columns(w, kh, [(512 * j, 256), (512 * j + 256, 256)]))
                    gains(n)
                    sp.dma_start(wg[:], w[:, D:D + 3 * NQ].rearrange("(k p) n -> p k n", p=P)).then_inc(loaded_wg, 16)
                    for d in range(KC // 2):
                        load(s0 + 4 + d, rows(t["nsa_w_o_2"][0], 2 * d))
            if has_ln(last):
                sp.wait_ge(normed, normed_before(len(phases)))
            else:
                sp.wait_ge(summed, summed_before(len(phases)))
            for tt in range(NT):
                sp.dma_start(out[tt * P:(tt + 1) * P, :], x_sb[:, tt, :]).then_inc(stored, 16)
            sp.wait_ge(stored, 16 * NT)

        @block.gpsimd
        def _(pool):
            pool.memset(ident[:], 0.0).then_inc(pool_step, 1)
            pool.wait_ge(pool_step, 1)
            pool.affine_select(out=ident[:], in_=ident[:], compare_op=ALU.not_equal, fill=1.0, base=0,
                               pattern=[[-1, P]], channel_multiplier=1).then_inc(pool_step, 1)
            pool.wait_ge(pool_step, 2)
            pool.tensor_copy(ident_b[:], ident[:]).then_inc(consts, 1)
            pool.memset(minus_half[:], -0.5).then_inc(pool_step, 1)
            pool.wait_ge(pool_step, 3)
            made = [3]

            def step(ins):
                made[0] += 1
                ins.then_inc(pool_step, 1)
                pool.wait_ge(pool_step, made[0])

            for m, first in ((near, 1), (causal, 0)):
                step(pool.memset(m[:], 0.0))
                step(pool.affine_select(out=m[:], in_=m[:], compare_op=ALU.is_ge, fill=MASKED, base=-first,
                                        pattern=[[-1, P]], channel_multiplier=1))
            step(pool.memset(same_head[:], 0.0))
            step(pool.memset(same_head[0:HD, 0:HD], 1.0))
            step(pool.memset(same_head[HD:P, HD:P], 1.0))
            pool.engine_nop().then_inc(consts, 1)

            def root(first, tt, col):
                pool.wait_ge(spread, first + tt + 1)
                pool.tensor_tensor(stats[:, col + 1:col + 2], stats[:, col:col + 1], minus_half[:, 0:1], ALU.pow).then_inc(rstd_ready, 1)

            for n, kind in enumerate(phases):
                if kind == MIXER:
                    pool.wait_ge(normed, normed_before(n))
                    for at, off in ((ROWS_A, 0), (ROWS_B, P)):
                        size = at.stop - at.start
                        step(pool.iota(far[:, at], pattern=[[1, size]], base=-off, channel_multiplier=-1,
                                       allow_small_or_imprecise_dtypes=True))
                        ins = pool.affine_select(out=far[:, at], in_=far[:, at], compare_op=ALU.is_ge, fill=MASKED, base=off,
                                                 pattern=[[-1, size]], channel_multiplier=1)
                    step(ins)
                    pool.engine_nop().then_inc(far_ready, 1)
                if kind == NSA:
                    pool.wait_ge(normed, normed_before(n))
                    step(pool.memset(cmp_mask[:], 0.0))
                    step(pool.memset(cmp_valid[:], 1.0))
                    step(pool.memset(cmp_p[:], 0.0))
                    for m, out_of in ((cmp_mask, MASKED), (cmp_valid, 0.0)):
                        for tt in range(NT):
                            step(pool.affine_select(out=m[:, tt, :], in_=m[:, tt, :], compare_op=ALU.is_ge, fill=out_of,
                                                    base=tt * P - 31, pattern=[[-16, 16]], channel_multiplier=1))
                    pool.engine_nop().then_inc(cmp_masks, 1)
                    for j in range(2):
                        pool.wait_ge(q_spread, j + 1)
                        pool.tensor_tensor(q_ms[:, j, 1, :], q_ms[:, j, 0, :], minus_half[:, 0:NQ], ALU.pow).then_inc(q_rstd, 1)
                if has_ln(n):
                    pool.wait_ge(xT_psum, 4 * (inputs_before(n) + 1))
                    pool.tensor_scalar(x_sb[:].rearrange("p t d -> p (t d)"), x_sb[:].rearrange("p t d -> p (t d)"),
                                       ALPHA, None, ALU.mult).then_inc(scaled, 1)
                    for tt in range(NT):
                        root(normed_before(n), tt, 4 * tt + 2)
                if has_rms(n):
                    for tt in range(NT):
                        root(normed_before(n) + NT * has_ln(n), tt, 10 + 2 * tt)
                if kind == KV:
                    for slot in range(2):
                        if slot == 1:
                            pool.wait_ge(kc_spread, 1)
                            pool.tensor_tensor(kc_ms[:, 2:3], kc_ms[:, 1:2], minus_half[0:GROUPS * 16, 0:1], ALU.pow).then_inc(kc_rstd, 1)
                        pool.wait_ge(key_spread, slot + 1)
                        pool.tensor_tensor(key_ms[:, slot, 1, :], key_ms[:, slot, 0, :], minus_half[:, 0:NT * GROUPS],
                                           ALU.pow).then_inc(key_rstd, 1)

        @block.scalar
        def _(act):
            def split(k, i=0):
                if k >= TOTAL:
                    return
                slot, width = k % SLOTS, width_of(k)
                act.wait_ge(arrived[slot], 32 * (k // SLOTS + 1) + 32 * i)
                if k >= SLOTS:
                    act.wait_ge(slab_used, k - SLOTS + 1 + 4 * i)
                nc.scalar.activation(w_hi[:, slot, 0:width], raw[:, slot, 0:width], ACT.Copy).then_inc(high_ready, 1)

            def evacuate_input(index):
                for b in range(4):
                    tt, q = b // 2, b % 2
                    act.wait_ge(xT_psum, 4 * index + b + 1)
                    nc.scalar.activation(xT_hi[:, 4 * q:4 * q + 4, tt * P:(tt + 1) * P],
                                         TB[tt][q][:].rearrange("p (k m) -> p k m", k=4), ACT.Copy).then_inc(xT_high, 1)

            def norm(n):
                if has_rms(n):
                    for tt in range(NT):
                        if has_ln(n):
                            act.wait_ge(normed, normed_before(n) + tt + 1)
                        else:
                            act.wait_ge(summed, summed_before(n) + (tt + 1 if kind != KV else 0))
                        nc.scalar.activation(z_sb[:, tt, :], x_sb[:, tt, :], ACT.Square,
                                             accum_out=stats[:, 8 + tt:9 + tt]).then_inc(squared, 1)

            def boundary(n):
                norm(n)
                if n < last:
                    evacuate_input(inputs_before(n + 1))

            rows_sb = z_sb[0:ROWS, 0, 0:P]
            for at, src in ((CONV_W, t["conv_w_2"][0].rearrange("w (k p) -> (w k) p", p=P)),
                            (POS, t["cmp_pos_2"].rearrange("a (c q) d -> (a c) (q d)", q=2)),
                            (CMP_B, t["cmp_b1_2"].rearrange("a (b p) -> (a b) p", p=P))):
                act.dma_start(z_sb[at:at + src.shape[0], 0, 0:P], src).then_inc(loaded_rows, 16)
            for at, src in ((Q_NORM, t["q_norm_2"]), (K_NORM, t["k_norm_2"]), (SUBLN, t["diff_subln_g"])):
                for twice in range(2):
                    act.dma_start(z_sb[at:at + src.shape[0], 0, twice * HD:(twice + 1) * HD], src).then_inc(loaded_rows, 16)

            act.dma_start(z_sb[:, 1, 0:P], t["diff_lambda"][0].rearrange("a d -> (a d)").partition_broadcast(P)).then_inc(loaded_lam, 16)
            evacuate_input(0)
            for k in range(SLOTS):
                split(k)
            for n, kind in enumerate(phases):
                s0 = first_slab[n]
                if kind == MIXER:
                    def tile_out(tile):
                        what = TILES[tile]
                        if what[0] in QKV:
                            _, blocks, first = QKV[what[0]]
                            act.wait_ge(slab_used, s0 + MIX_SLABS.index((tile, 1)) + 1)
                            for i in range(blocks // 2):
                                nc.scalar.activation(qk[:, first + 2 * i:first + 2 * i + 2, :],
                                                     pair_of(tile)[i][:].rearrange("p (k m) -> p k m", k=2),
                                                     ACT.Copy).then_inc(pair_read[tile % 2], 1)
                        if what[0] == "gate" and what[2] == 1:
                            b = what[1]
                            for half in range(2):
                                for tt in range(NT):
                                    g = gates[:, tt, half * 512:(half + 1) * 512]
                                    act.wait_ge(gate_sum, 4 * b + 2 * half + tt + 1)
                                    nc.scalar.activation(g, g, ACT.Sigmoid).then_inc(gated, 1)
                            nc.scalar.preload_act_table_set("natural_log_exp_and_others")

                    def logs_of(u):
                        p, z, k = prob[:, u % 2, :], bank[4 + u % 2][:, 0:BW], 3 * (u - 2 * HEADS)
                        act.wait_ge(scored, u + 1)
                        act.wait_ge(probT_psum, before(u))
                        nc.scalar.activation(p, z, ACT.Abs).then_inc(logs, 1)
                        act.wait_ge(logs, k + 1)
                        nc.scalar.activation(p, p, ACT.Exp, scale=-(HD ** -0.5)).then_inc(logs, 1)
                        act.wait_ge(logs, k + 2)
                        nc.scalar.activation(p, p, ACT.Ln, bias=1.0).then_inc(logs, 1)

                    def weights_of(u):
                        b = u // HEADS
                        if b == STICK:
                            p = prob[:, u % 2, :]
                            act.wait_ge(score_read, u + 1)
                            nc.scalar.activation(p, p, ACT.Exp).then_inc(prob_ready, 1)
                            return
                        scale = HD ** -0.5 if b == MOBA else DIFF_SCALE
                        act.wait_ge(neg_ready, u + 1)
                        for m in range(1 if b == MOBA else 2):
                            side = u % 2 if b == MOBA else m
                            for i, at in enumerate((ROWS_A, ROWS_B)):
                                c = 2 * m + i
                                ins = nc.scalar.activation(prob[:, side, at], prob[:, side, at], ACT.Exp, scale=scale,
                                                           bias=head_max[:, u % 2, c:c + 1],
                                                           accum_out=head_sum[:, u % 2, c:c + 1])
                        ins.then_inc(exped, 1)

                    def transposed(u):
                        act.wait_ge(probT_psum, u + 1)
                        if u >= 2:
                            act.wait_ge(o_psum, u - 1)
                        nc.scalar.activation(probT[:, u % 2, :], bank[6][:, 0:BW], ACT.Copy).then_inc(probT_ready, 1)

                    def pair_out(p, src):
                        b = p // BC
                        if b > 0:
                            act.wait_ge(slab_used, s0 + branch_slab(b - 1, 1) + 1)
                        nc.scalar.activation(oT_hi[:, p % BC, :], src, ACT.Copy).then_inc(oT_high, 1)

                    def pair_begins(p):
                        act.wait_ge(o_psum, 2 * p + 2)
                        if p // BC != DIFF:
                            pair_out(p, bank[7][:, 0:S])
                            return
                        k = p - BC
                        act.wait_ge(oT_ready, p)
                        nc.scalar.activation(o_f, bank[7][:, 0:S], ACT.Copy).then_inc(o_copied, 1)
                        act.wait_ge(o_copied, k + 1)
                        nc.scalar.activation(ms_d, o_f, ACT.Square).then_inc(o_square, 1)

                    def pair_roots(p):
                        k = p - BC
                        act.wait_ge(o_spread, k + 1)
                        nc.scalar.activation(o_root, ms_d, ACT.Ln).then_inc(o_log, 1)
                        act.wait_ge(o_log, k + 1)
                        nc.scalar.activation(o_root, o_root, ACT.Exp, scale=-0.5).then_inc(o_rstd, 1)

                    def slabs(i):
                        for d in ROUND[i]:
                            split(s0 + d + 4)

                    def tiles(i):
                        for d in ROUND[i]:
                            if ends(d) is not None:
                                tile_out(ends(d))

                    for d in ROUND[0]:
                        split(s0 + d + 4)
                        if ends(d) is not None:
                            tile_out(ends(d))
                    nc.scalar.preload_act_table_set("natural_log_exp_and_others")
                    for u in range(3 * HEADS):
                        weights_of(u)
                        slabs(u + 1)
                        transposed(u)
                        tiles(u + 1)
                        if u % 2 == 0 and u > 0:
                            pair_begins(u // 2 - 1)
                        if u % 2 == 1 and (u - 3) // 2 // BC == DIFF:
                            pair_roots((u - 3) // 2)
                            act.wait_ge(o_normed, (u - 3) // 2 - BC + 1)
                            pair_out((u - 3) // 2, o_f)
                        if u + 1 >= 2 * HEADS and u + 1 < 3 * HEADS:
                            logs_of(u + 1)
                    pair_begins(3 * BC - 1)
                    for d in ROUND[-1]:
                        split(s0 + d + 4)
                        if ends(d) is not None:
                            tile_out(ends(d))
                    evacuate_input(inputs_before(n) + 1)
                    for d in range(KC // 2 - 1):
                        split(s0 + 32 + d + 4)
                    boundary(n)
                    split(s0 + 32 + KC // 2 - 1 + 4)
                if kind == CONV:
                    for j in range(6):
                        split(s0 + 2 * j + 4)
                        act.wait_ge(slab_used, s0 + 2 * j + 2)
                        if j < 4:
                            if j >= 2:
                                act.wait_ge(conv_v_ready, j - 1)
                            nc.scalar.activation(conv_c[:, j % 2, :], bank[4 * (j % 2)][:], ACT.Copy).then_inc(conv_c_ready, 1)
                        else:
                            for b in range(2):
                                act.wait_ge(conv_y_ready, 2 * (j - 4) + b + 1)
                                k = 4 * (j - 4) + 2 * b
                                nc.scalar.activation(yT_hi[:, k:k + 2, :], conv_y[:, b, :].rearrange("p (k m) -> p k m", k=2),
                                                     ACT.Copy).then_inc(yT_high, 1)
                        split(s0 + 2 * j + 5)
                    for d in range(KC // 2 - 1):
                        split(s0 + 12 + d + 4)
                    boundary(n)
                    split(s0 + 12 + KC // 2 - 1 + 4)
                if kind == KV:
                    split(s0 + 4)
                    act.wait_ge(xc_zero, 1)
                    nc.scalar.activation(tokens_of(xc_hi)[:, :, GROUPS, 0:32:2], cols[:, POS:POS + 32].rearrange("p (a c) -> p a c", a=2),
                                         ACT.Copy).then_inc(xc_high, 1)
                    act.wait_ge(slab_used, s0 + 2)
                    for kv in range(2):
                        for gp in range(2):
                            src = bank[kv][HD * gp:HD * (gp + 1), :].rearrange("p (b m) -> p b m", b=2)
                            for on in range(2):
                                nc.scalar.activation(tokens_of(xc_hi)[HD * on:HD * (on + 1), kv, gp:GROUPS:2, 0:S - on], src[:, :, on:S],
                                                     ACT.Copy).then_inc(xc_high, 1)
                    split(s0 + 5)
                    norm(n)
                    for kv in range(2):
                        split(s0 + 6 + 2 * kv)
                        act.wait_ge(slab_used, s0 + 4 + 2 * kv)
                        nc.scalar.activation(hid_row[:, kv, :], bank[6 + kv][0:CMP_ROWS, 0:CMP_HID], ACT.Copy).then_inc(hid_rows, 1)
                        act.wait_ge(bias_ready, kv + 1)
                        for hb in range(2):
                            nc.scalar.activation(hid[:, kv, hb, :], hidden_of(kv, hb)[:, 0:GROUPS * 16], ACT.Gelu_apprx_tanh,
                                                 bias=cmp_bias[:, kv, hb:hb + 1]).then_inc(hid_ready, 1)
                        split(s0 + 7 + 2 * kv)
                    for slot, (pair, v) in enumerate((([4, 5], v_sel), ([2, 3], v_win))):
                        split(s0 + 10 + 2 * slot)
                        act.wait_ge(slab_used, s0 + 8 + 2 * slot)
                        for tt in range(NT):
                            nc.scalar.activation(key_sq[:, slot, tt, :], bank[pair[tt]][:, 0:S], ACT.Square).then_inc(key_squared, 1)
                        for tt in range(NT):
                            nc.scalar.activation(v[:, tt, :], bank[pair[tt]][:, S:2 * S], ACT.Copy).then_inc(values_ready, 1)
                        if slot == 0:
                            split(s0 + 11)
                            act.wait_ge(cmp_psum, 1)
                            nc.scalar.activation(kc_sq[:], bank[6][0:GROUPS * 16, 0:HD], ACT.Square,
                                                 accum_out=kc_ms[:, 0:1]).then_inc(kc_squared, 1)
                    evacuate_input(inputs_before(n + 1))
                    split(s0 + 13)
                if kind == NSA:
                    act.wait_ge(loaded_wg, 16)
                    nc.scalar.activation(wg_hi[:], wg[:], ACT.Copy).then_inc(wg_high, 1)
                    for j in range(2):
                        split(s0 + 2 * j + 4)
                        act.wait_ge(slab_used, s0 + 2 * j + 2)
                        for tt in range(NT):
                            nc.scalar.activation(z_sb[:, tt, 512 * j:512 * (j + 1)], bank[2 * j + tt][:], ACT.Square).then_inc(q_squared, 1)
                        split(s0 + 2 * j + 5)
                    act.wait_ge(gates_psum, 1)
                    nc.scalar.activation(branch_gate[:].rearrange("p t n -> p (t n)"), bank[4][:, 0:NT * 3 * NQ],
                                         ACT.Sigmoid).then_inc(branch_gates, 1)
                    act.wait_ge(cmp_shifted, 1)
                    nc.scalar.activation(cmp_l, cmp_l, ACT.Exp).then_inc(cmp_exped, 1)

                    def exponentials(w):
                        act.wait_ge(sel_neg, w + 1)
                        if w >= 2:
                            act.wait_ge(selT_psum, w - 1)
                            act.wait_ge(sel_weighed, w - 1)
                        for tt in range(NT):
                            for r in range(PER_GROUP):
                                b, at = score_place(tt, r)
                                ins = nc.scalar.activation(sel_p[:, w % 2, b, at], bank[SCORES[w % 2][b]][:, at], ACT.Exp,
                                                           bias=sel_max[:, w % 2, tt * PER_GROUP + r:tt * PER_GROUP + r + 1],
                                                           accum_out=sel_sum[:, w % 2, tt, r:r + 1])
                        ins.then_inc(sel_exped, 1)

                    def transposed_weights(w):
                        act.wait_ge(selT_psum, w + 1)
                        if w >= 2:
                            act.wait_ge(sel_out, w - 1)
                        for b in range(2):
                            ins = nc.scalar.activation(sel_pT[:, w % 2, b, :], bank[SCORES[w % 2][b]][:], ACT.Copy)
                        ins.then_inc(selT_act, 1)

                    exponentials(0)
                    for tt in range(NT):
                        act.wait_ge(cmpT_psum, tt + 1)
                        nc.scalar.activation(cmp_pT[:, tt, :, :].rearrange("p g m -> p (g m)"), bank[2 * tt][:], ACT.Copy)\
                            .then_inc(cmpT_ready, 1)
                    for tt in range(NT):
                        act.wait_ge(cmp_out, tt + 1)
                        for half in range(2):
                            nc.scalar.activation(z_sb[:, tt, 512 * half:512 * (half + 1)], bank[CMP_OUT[tt][half]][:], ACT.Copy)\
                                .then_inc(z_started, 1)
                    for w in range(UNITS):
                        if w > 0:
                            exponentials(w)
                        transposed_weights(w)
                    evacuate_input(inputs_before(n) + 1)
                    for d in range(KC // 2 - 1):
                        split(s0 + 4 + d + 4)
                    boundary(n)
                    split(s0 + 4 + KC // 2 - 1 + 4)
                if kind == FFN:
                    f = ffn_number[n]

                    def hidden(j, i=0):
                        act.wait_ge(hT_psum, FT * f + j + 1 + 2 * i)
                        nc.scalar.activation(hT_hi[:, bass.ds(2 * j + 4 * i, 2), :],
                                             bank[4 + j % 2][:].rearrange("p (c m) -> p c m", c=2),
                                             ACT.Copy).then_inc(hT_high, 1)

                    def tile(j, i=0):
                        if not (isinstance(i, int) and j == 0):
                            hidden(j - 1, i)
                        split(s0 + 2 * j + 4, i)
                        act.wait_ge(slab_used, s0 + 2 * j + 2 + 4 * i)
                        for tt in range(NT):
                            if not (isinstance(i, int) and j == 0):
                                act.wait_ge(h_ready, 2 * FT * f + 2 * j - 1 + tt + 4 * i)
                            nc.scalar.activation(silu[:, tt, :], bank[2 * (j % 2) + tt][:, 0:256],
                                                 ACT.Silu).then_inc(silu_ready, 1)
                        split(s0 + 2 * j + 5, i)

                    for j in range(3):
                        tile(j)
                    if n == 0:
                        act.wait_ge(lam_dots, 1)
                        nc.scalar.activation(lam_col[:, 2:4], lam_col[:, 0:2], ACT.Exp).then_inc(lam_exp, 1)
                    with act.Fori(0, (FT - 3) // 2) as i:
                        for j in range(3, 5):
                            tile(j, i)
                    for d in range(FC // 2):
                        if d == 1:
                            hidden(FT - 1)
                        if d < FC // 2 - 1:
                            split(s0 + 2 * FT + d + 4)
                    boundary(n)
                    split(s0 + 2 * FT + FC // 2 - 1 + 4)

        @block.vector
        def _(dve):
            steps = [0]

            def step(ins):
                steps[0] += 1
                ins.then_inc(dve_step, 1)
                dve.wait_ge(dve_step, steps[0])

            def split(k, i=0):
                if k >= TOTAL:
                    return
                slot, width = k % SLOTS, width_of(k)
                dve.wait_ge(high_ready, k + 1 + 4 * i)
                nc.vector.tensor_tensor(w_lo[:, slot, 0:width], raw[:, slot, 0:width],
                                        w_hi[:, slot, 0:width].bitcast(F32), ALU.subtract).then_inc(low_ready, 1)

            def evacuate_input(index):
                for b in range(4):
                    tt, q = b // 2, b % 2
                    dve.wait_ge(xT_high, 4 * index + b + 1)
                    nc.vector.tensor_tensor(xT_lo[:, 4 * q:4 * q + 4, tt * P:(tt + 1) * P],
                                            TB[tt][q][:].rearrange("p (k m) -> p k m", k=4),
                                            xT_hi[:, 4 * q:4 * q + 4, tt * P:(tt + 1) * P].bitcast(F32),
                                            ALU.subtract).then_inc(xT_ready, 1)

            def add_output(n, tt, factor, y_at):
                if tt == 0:
                    dve.wait_ge(y_ready, y_layers[n] + 1)
                    if has_ln(n):
                        dve.wait_ge(scaled, ln_uses[n] + 1)
                else:
                    dve.wait_ge(slab_used, y_at)
                for half in range(2):
                    part = x_sb[:, tt, half * 512:(half + 1) * 512]
                    ins = nc.vector.scalar_tensor_tensor(out=part, in0=Y[tt][half][:], scalar=factor, in1=part,
                                                         op0=ALU.mult, op1=ALU.add)
                ins.then_inc(summed, 1)

            def layer_norm(n, tt):
                dve.wait_ge(summed, summed_before(n) + tt + 1)
                for half in range(2):
                    ins = nc.vector.bn_stats(bn[:, tt, half, :], x_sb[:, tt, half * 512:(half + 1) * 512])
                step(ins)
                step(nc.vector.bn_aggr(stats[:, 4 * tt:4 * tt + 2], bn[:, tt, :, :]))
                nc.vector.tensor_scalar(stats[:, 4 * tt + 2:4 * tt + 3], stats[:, 4 * tt + 1:4 * tt + 2], LN_EPS, None,
                                        ALU.add).then_inc(spread, 1)

            def layer_norm_apply(n, tt):
                xt, mean, rstd = x_sb[:, tt, :], stats[:, 4 * tt:4 * tt + 1], stats[:, 4 * tt + 3:4 * tt + 4]
                dve.wait_ge(rstd_ready, normed_before(n) + tt + 1)
                dve.wait_ge(gain_loaded[0], 16 * (ln_uses[n] + 1))
                dve.wait_ge(gain_loaded[1], 16 * (ln_uses[n] + 1))
                step(nc.vector.scalar_tensor_tensor(out=xt, in0=xt, scalar=mean, in1=gain[:, 0, :],
                                                    op0=ALU.subtract, op1=ALU.mult))
                nc.vector.scalar_tensor_tensor(out=xt, in0=xt, scalar=rstd, in1=gain[:, 1, :],
                                               op0=ALU.mult, op1=ALU.add).then_inc(normed, 1)

            def rms_norm(n, tt):
                dve.wait_ge(squared, NT * rms_uses[n] + tt + 1)
                nc.vector.tensor_scalar(stats[:, 10 + 2 * tt:11 + 2 * tt], stats[:, 8 + tt:9 + tt], 1.0 / D, RMS_EPS,
                                        ALU.mult, ALU.add).then_inc(spread, 1)

            def rms_norm_apply(n, tt):
                dve.wait_ge(rstd_ready, normed_before(n) + NT * has_ln(n) + tt + 1)
                dve.wait_ge(gain_loaded[2], 16 * (rms_uses[n] + 1))
                nc.vector.scalar_tensor_tensor(out=z_sb[:, tt, :], in0=x_sb[:, tt, :], scalar=stats[:, 11 + 2 * tt:12 + 2 * tt],
                                               in1=gain[:, 2, :], op0=ALU.mult, op1=ALU.mult).then_inc(normed, 1)

            def boundary(n, factor, y_at):
                for tt in range(NT):
                    add_output(n, tt, factor, y_at)
                    if has_ln(n):
                        layer_norm(n, tt)
                norm(n)
                if n < last:
                    evacuate_input(inputs_before(n + 1))

            def norm(n):
                if has_ln(n):
                    for tt in range(NT):
                        layer_norm_apply(n, tt)
                if has_rms(n):
                    for tt in range(NT):
                        rms_norm(n, tt)
                    for tt in range(NT):
                        rms_norm_apply(n, tt)

            evacuate_input(0)
            for k in range(SLOTS):
                split(k)
            def small_parameters():
                dve.wait_ge(cols_psum, 1)
                nc.vector.tensor_copy(cols[:, 0:ROWS], bank[7][:, 0:ROWS]).then_inc(cols_ready, 1)
                dve.wait_ge(cols_ready, 1)
                dve.wait_ge(loaded_lam, 16)
                lf = z_sb[:, 1, 0:P].rearrange("p (a b d) -> p a b d", a=2, b=2)
                dots = z_sb[:, 1, P:P + HD].rearrange("p (a d) -> p a d", a=2)
                step(nc.vector.tensor_tensor(dots, lf[:, :, 0, :], lf[:, :, 1, :], ALU.mult))
                nc.vector.tensor_reduce(lam_col[:, 0:2], dots, AX.X, ALU.add).then_inc(lam_dots, 1)
                dve.wait_ge(lam_exp, 1)
                step(nc.vector.tensor_tensor(lam_col[:, 4:5], lam_col[:, 3:4], lam_col[:, 2:3], ALU.subtract))
                step(nc.vector.tensor_scalar(lam_col[:, 5:6], lam_col[:, 4:5], -LAMBDA_INIT, None, ALU.add))
                step(nc.vector.tensor_scalar(lam_col[:, 6:7], cols[:, SUBLN:SUBLN + 1], 1.0 - LAMBDA_INIT, None, ALU.mult))

            minus_lam, out_gain = lam_col[:, 5:6], lam_col[:, 6:7]
            for n, kind in enumerate(phases):
                s0 = first_slab[n]
                if kind == MIXER:
                    def tile_out(tile):
                        what, src = TILES[tile], pair_of(tile)
                        if what[0] == "k, v of sb":
                            dve.wait_ge(slab_used, s0 + MIX_SLABS.index((tile, 1)) + 1)
                            nc.vector.tensor_copy(v_mix[:, :, 2 * BW:2 * BW + 256], src[1][:].rearrange("p (t n) -> p t n", t=NT))\
                                .then_inc(pair_read[tile % 2], 1)
                        elif what[0] in QKV and QKV[what[0]][1] == 0:
                            dve.wait_ge(slab_used, s0 + MIX_SLABS.index((tile, 1)) + 1)
                            for tt in range(NT):
                                if what[0] == "v of moba, sb":
                                    nc.vector.tensor_copy(v_mix[:, tt, 2 * BW + 256:3 * BW], src[tt][:, BW:512])
                                c0 = 0 if what[0] == "v of moba, sb" else BW
                                nc.vector.tensor_copy(v_mix[:, tt, c0:c0 + BW], src[tt][:, 0:BW]).then_inc(pair_read[tile % 2], 1)
                        elif what[0] == "gate":
                            _, b, half = what
                            at = slice(half * 512, (half + 1) * 512)
                            dve.wait_ge(loaded_mix, 16)
                            dve.wait_ge(slab_used, s0 + MIX_SLABS.index((tile, 1)) + 1)
                            if b > 0:
                                dve.wait_ge(merged, 4 * b)
                            for tt in range(NT):
                                nc.vector.tensor_tensor(gates[:, tt, at], src[tt][:], b_gate[:, b, at], ALU.add).then_inc(gate_sum, 1)
                            dve.wait_ge(gate_sum, 4 * b + 2 * half + 2)
                            nc.vector.engine_nop().then_inc(pair_read[tile % 2], 2)
                        elif what[0] == "branch":
                            _, b, half = what
                            at = slice(half * 512, (half + 1) * 512)
                            dve.wait_ge(slab_used, s0 + branch_slab(b, half) + 1)
                            for tt in range(NT):
                                dve.wait_ge(gated, 4 * b + 2 * half + tt + 1)
                                y = z_sb[:, tt, at]
                                if b == 0:
                                    nc.vector.tensor_tensor(y, gates[:, tt, at], src[tt][:], ALU.mult).then_inc(merged, 1)
                                else:
                                    step(nc.vector.tensor_tensor(tmp[:], gates[:, tt, at], src[tt][:], ALU.mult))
                                    nc.vector.tensor_tensor(y, y, tmp[:], ALU.add).then_inc(merged, 1)
                                dve.wait_ge(merged, 4 * b + 2 * half + tt + 1)
                            nc.vector.engine_nop().then_inc(pair_read[tile % 2], 2)

                    def maxima_of(u):
                        b, hd = u // HEADS, u % HEADS
                        dve.wait_ge(scored, u + 1)
                        if before(u) > 0:
                            dve.wait_ge(probT_psum, before(u))
                        scale = HD ** -0.5 if b == MOBA else DIFF_SCALE
                        slope = alibi_slope(2 * hd if b == MOBA else 2 * hd + 1)
                        maps = 1 if b == MOBA else 2
                        for m in range(maps):
                            side = u % 2 if b == MOBA else m
                            ins = nc.vector.scalar_tensor_tensor(out=prob[:, side, :], in0=far[:], scalar=slope / scale,
                                                                 in1=bank[4 + side][:, 0:BW], op0=ALU.mult, op1=ALU.add)
                        ins.then_inc(score_read, 1)
                        dve.wait_ge(score_read, u + 1)
                        mx = head_max[:, u % 2, 0:2 * maps]
                        for m in range(maps):
                            side = u % 2 if b == MOBA else m
                            for i, at in enumerate((ROWS_A, ROWS_B)):
                                ins = nc.vector.tensor_reduce(head_max[:, u % 2, 2 * m + i:2 * m + i + 1], prob[:, side, at], AX.X, ALU.max)
                        step(ins)
                        nc.vector.tensor_scalar(mx, mx, -scale, None, ALU.mult).then_inc(neg_ready, 1)

                    def weights_of(u):
                        b = u // HEADS
                        if b == STICK:
                            p, z = prob[:, u % 2, :], bank[4 + u % 2][:, 0:BW]
                            dve.wait_ge(logs, 3 * (u - 2 * HEADS) + 3)
                            soft = tmp[:, 0:BW]
                            step(nc.vector.tensor_scalar(soft, z, 0.0, HD ** -0.5, ALU.max, ALU.mult))
                            step(nc.vector.tensor_tensor(soft, soft, p, ALU.add))
                            for at in (ROWS_A, ROWS_B):
                                part, to = soft[:, at], stick[:, at]
                                ins = nc.vector.tensor_tensor_scan(to[:, ::-1], part[:, ::-1], part[:, ::-1], 0.0, ALU.add, ALU.max)
                            step(ins)
                            nc.vector.scalar_tensor_tensor(out=p, in0=z, scalar=HD ** -0.5, in1=stick[:], op0=ALU.mult,
                                                           op1=ALU.subtract).then_inc(score_read, 1)
                            dve.wait_ge(score_read, u + 1)
                            return
                        sm = head_sum[:, u % 2, 0:2 if b == MOBA else 4]
                        dve.wait_ge(exped, u + 1)
                        step(nc.vector.reciprocal(sm, sm))
                        if b == DIFF:
                            step(nc.vector.tensor_scalar(sm[:, 2:4], sm[:, 2:4], minus_lam, None, ALU.mult))
                        side = u % 2 if b == MOBA else 0
                        for i, at in enumerate((ROWS_A, ROWS_B)):
                            ins = nc.vector.tensor_scalar(prob[:, side, at], prob[:, side, at], sm[:, i:i + 1], None, ALU.mult)
                        if b == DIFF:
                            step(ins)
                            for i, at in enumerate((ROWS_A, ROWS_B)):
                                ins = nc.vector.scalar_tensor_tensor(out=prob[:, 0, at], in0=prob[:, 1, at], scalar=sm[:, 2 + i:3 + i],
                                                                     in1=prob[:, 0, at], op0=ALU.mult, op1=ALU.add)
                        ins.then_inc(prob_ready, 1)
                        dve.wait_ge(prob_ready, u + 1)

                    def pair_spread(p):
                        dve.wait_ge(o_sums, p - BC + 1)
                        nc.vector.tensor_scalar(ms_d, bank[7][:, S:2 * S], 1.0 / HD, SUBLN_EPS, ALU.mult, ALU.add).then_inc(o_spread, 1)

                    def pair_norm(p):
                        near_one = tmp[:, 0:S]
                        dve.wait_ge(o_rstd, p - BC + 1)
                        step(nc.vector.tensor_tensor(near_one, o_root, o_root, ALU.mult))
                        step(nc.vector.tensor_tensor(near_one, near_one, ms_d, ALU.mult))
                        step(nc.vector.tensor_scalar(near_one, near_one, -0.5, 1.5, ALU.mult, ALU.add))
                        step(nc.vector.tensor_tensor(near_one, near_one, o_root, ALU.mult))
                        nc.vector.scalar_tensor_tensor(out=o_f, in0=o_f, scalar=out_gain, in1=near_one,
                                                       op0=ALU.mult, op1=ALU.mult).then_inc(o_normed, 1)

                    def pair_out(p, src):
                        dve.wait_ge(oT_high, p + 1)
                        nc.vector.tensor_tensor(oT_lo[:, p % BC, :], src, oT_hi[:, p % BC, :].bitcast(F32), ALU.subtract)\
                            .then_inc(oT_ready, 1)

                    def slabs(i):
                        for d in ROUND[i]:
                            split(s0 + d + 4)

                    def tiles(i):
                        for d in ROUND[i]:
                            if ends(d) is not None:
                                tile_out(ends(d))

                    for d in ROUND[0]:
                        split(s0 + d + 4)
                        if ends(d) is not None:
                            tile_out(ends(d))
                    dve.wait_ge(far_ready, 1)
                    maxima_of(0)
                    for u in range(3 * HEADS):
                        weights_of(u)
                        delayed = (u - 3) // 2 if u % 2 == 1 and (u - 3) // 2 // BC == DIFF else None
                        if delayed is not None:
                            pair_spread(delayed)
                        slabs(u + 1)
                        if u + 1 < 2 * HEADS:
                            maxima_of(u + 1)
                        tiles(u + 1)
                        if u % 2 == 0 and u > 0 and (u // 2 - 1) // BC != DIFF:
                            pair_out(u // 2 - 1, bank[7][:, 0:S])
                        if delayed is not None:
                            pair_norm(delayed)
                            pair_out(delayed, o_f)
                    pair_out(3 * BC - 1, bank[7][:, 0:S])
                    for d in ROUND[-1]:
                        split(s0 + d + 4)
                        if ends(d) is not None:
                            tile_out(ends(d))
                    evacuate_input(inputs_before(n) + 1)
                    for d in range(KC // 2 - 1):
                        split(s0 + 32 + d + 4)
                    boundary(n, 1.0, s0 + 36)
                    split(s0 + 32 + KC // 2 - 1 + 4)
                if kind == CONV:
                    nc.vector.memset(conv_v[:, :, 0:2], 0.0)
                    for j in range(6):
                        split(s0 + 2 * j + 4)
                        if j < 4:
                            dve.wait_ge(conv_c_ready, j + 1)
                            nc.vector.tensor_tensor(conv_v[:, 2 * j:2 * j + 2, 2:S + 2],
                                                    conv_c[:, j % 2, :].rearrange("p (k m) -> p k m", k=2),
                                                    bank[4 * (j % 2) + 1][:].rearrange("p (k m) -> p k m", k=2),
                                                    ALU.mult).then_inc(conv_v_ready, 1)
                            dve.wait_ge(conv_v_ready, j + 1)
                            for k in (2 * j, 2 * j + 1):
                                a = conv_a[:, k, :]
                                w = [cols[:, CONV_W + tap * KC + k:CONV_W + tap * KC + k + 1] for tap in range(3)]
                                step(nc.vector.tensor_scalar(a, conv_v[:, k, 2:S + 2], w[2], None, ALU.mult))
                                for tap in (1, 0):
                                    step(nc.vector.scalar_tensor_tensor(out=a, in0=conv_v[:, k, tap:tap + S], scalar=w[tap],
                                                                        in1=a, op0=ALU.mult, op1=ALU.add))
                        else:
                            dve.wait_ge(slab_used, s0 + 2 * j + 2)
                            for b in range(2):
                                k, done = 4 * (j - 4) + 2 * b, 2 * (j - 4) + b + 1
                                if j == 5:
                                    dve.wait_ge(yT_ready, done - 2)
                                nc.vector.tensor_tensor(conv_y[:, b, :], bank[4 * (j % 2) + b][:],
                                                        conv_a[:, k:k + 2, :].rearrange("p k m -> p (k m)"),
                                                        ALU.mult).then_inc(conv_y_ready, 1)
                            for b in range(2):
                                k, done = 4 * (j - 4) + 2 * b, 2 * (j - 4) + b + 1
                                dve.wait_ge(yT_high, done)
                                nc.vector.tensor_tensor(yT_lo[:, k:k + 2, :], conv_y[:, b, :].rearrange("p (k m) -> p k m", k=2),
                                                        yT_hi[:, k:k + 2, :].bitcast(F32), ALU.subtract).then_inc(yT_ready, 1)
                        split(s0 + 2 * j + 5)
                    for d in range(KC // 2 - 1):
                        split(s0 + 12 + d + 4)
                    boundary(n, 1.0, s0 + 16)
                    split(s0 + 12 + KC // 2 - 1 + 4)
                if kind == KV:
                    zero = ident[:].rearrange("p (a g t) -> p a g t", a=2, g=GROUPS)
                    for x in (xc_hi, xc_lo):
                        last_token = tokens_of(x)[HD:P, :, 0:GROUPS, S - 1:S]
                        nc.vector.tensor_tensor(last_token, zero[HD:P, :, :, 0:1], zero[HD:P, :, :, 0:1], ALU.subtract)
                        for kv in range(2):
                            ins = nc.vector.tensor_tensor(x[:, kv, GROUPS * S:], x_sb[:, 0, 0:XC - GROUPS * S], x_sb[:, 0, 0:XC - GROUPS * S],
                                                          ALU.subtract)
                    step(ins)
                    nc.vector.engine_nop().then_inc(xc_zero, 1)
                    step(nc.vector.memset(v_cmp[:], 0.0))
                    step(nc.vector.memset(hid_v[:], 0.0))
                    split(s0 + 4)
                    dve.wait_ge(xc_high, 1)
                    nc.vector.tensor_tensor(tokens_of(xc_lo)[:, :, GROUPS, 0:32:2], cols[:, POS:POS + 32].rearrange("p (a c) -> p a c", a=2),
                                            tokens_of(xc_hi)[:, :, GROUPS, 0:32:2].bitcast(F32), ALU.subtract).then_inc(xc_ready, 1)
                    for kv in range(2):
                        dve.wait_ge(xc_high, 1 + 4 * (kv + 1))
                        for gp in range(2):
                            src = bank[kv][HD * gp:HD * (gp + 1), :].rearrange("p (b m) -> p b m", b=2)
                            for on in range(2):
                                part = slice(HD * on, HD * (on + 1))
                                nc.vector.tensor_tensor(tokens_of(xc_lo)[part, kv, gp:GROUPS:2, 0:S - on], src[:, :, on:S],
                                                        tokens_of(xc_hi)[part, kv, gp:GROUPS:2, 0:S - on].bitcast(F32), ALU.subtract).then_inc(xc_ready, 1)
                    split(s0 + 5)
                    norm(n)
                    for kv in range(2):
                        split(s0 + 6 + 2 * kv)
                        dve.wait_ge(hidT_psum, kv + 1)
                        for hb in range(2):
                            c0 = CMP_B + 2 * kv + hb
                            ins = nc.vector.tensor_tensor(cmp_bias[:, kv, hb:hb + 1], hidden_of(kv, hb)[:, GROUPS * 16:GROUPS * 16 + 1],
                                                          cols[:, c0:c0 + 1], ALU.add)
                        ins.then_inc(bias_ready, 1)
                        split(s0 + 7 + 2 * kv)
                    dve.wait_ge(hid_ready, 4)
                    for hb in range(2):
                        for r in range(PER_GROUP):
                            ins = nc.vector.tensor_copy(hid_v[:, hb, :, r, 0:16], hid[:, 1, hb, :].rearrange("p (g n) -> p g n", g=GROUPS))
                    ins.then_inc(hid_v_ready, 1)
                    for slot, pair in enumerate(([4, 5], [2, 3])):
                        split(s0 + 10 + 2 * slot)
                        dve.wait_ge(key_squared, NT * (slot + 1))
                        ms, rstd = key_ms[:, slot, 0, :], key_ms[:, slot, 1, :]
                        step(nc.vector.tensor_reduce(ms, key_sq[:, slot, :, :].rearrange("p t (g d) -> p (t g) d", g=GROUPS), AX.X, ALU.add))
                        nc.vector.tensor_scalar(ms, ms, 1.0 / HD, RMS_EPS, ALU.mult, ALU.add).then_inc(key_spread, 1)
                        dve.wait_ge(key_rstd, slot + 1)
                        dve.wait_ge(values_ready, NT * (slot + 1))
                        for tt in range(NT):
                            each = rstd[:, tt * GROUPS:(tt + 1) * GROUPS].unsqueeze(2).to_broadcast([P, GROUPS, HD])
                            ins = nc.vector.tensor_tensor(key_n[:, slot, tt, :].rearrange("p (g d) -> p g d", g=GROUPS),
                                                          bank[pair[tt]][:, 0:S].rearrange("p (g d) -> p g d", g=GROUPS), each, ALU.mult)
                        ins.then_inc(key_normed, 1)
                        if slot == 0:
                            split(s0 + 11)
                            dve.wait_ge(cmp_psum, 2)
                            for r in range(PER_GROUP):
                                part = slice(32 * r, 32 * (r + 1))
                                ins = nc.vector.tensor_copy(v_cmp[part, :, HD * r:HD * (r + 1)],
                                                            bank[7][part, 0:S].rearrange("p (g d) -> p g d", g=GROUPS))
                            ins.then_inc(cmp_ready, 1)
                            dve.wait_ge(kc_squared, 1)
                            nc.vector.tensor_scalar(kc_ms[:, 1:2], kc_ms[:, 0:1], 1.0 / HD, RMS_EPS, ALU.mult, ALU.add).then_inc(kc_spread, 1)
                            dve.wait_ge(kc_rstd, 1)
                            for twice in range(2):
                                ins = nc.vector.tensor_scalar(kc_n[:, twice * HD:(twice + 1) * HD], bank[6][0:GROUPS * 16, 0:HD],
                                                              kc_ms[:, 2:3], None, ALU.mult)
                            ins.then_inc(kc_normed, 1)
                            dve.wait_ge(kcT_psum, 1)
                            nc.vector.tensor_scalar(k_cmp[:], bank[6][:, P:P + GROUPS * 16], cols[:, K_NORM:K_NORM + 1], None,
                                                    ALU.mult).then_inc(cmp_ready, 1)
                    evacuate_input(inputs_before(n + 1))
                    split(s0 + 13)
                    for slot, (b, keys) in enumerate(((7, k_sel), (6, k_win))):
                        dve.wait_ge(keyT_psum, slot + 1)
                        nc.vector.tensor_scalar(keys[:].rearrange("p b m -> p (b m)"), bank[b][:], cols[:, K_NORM + 1 + slot:K_NORM + 2 + slot],
                                                None, ALU.mult).then_inc(keys_ready, 1)
                if kind == NSA:
                    dve.wait_ge(wg_high, 1)
                    nc.vector.tensor_tensor(wg_lo[:], wg[:], wg_hi[:].bitcast(F32), ALU.subtract).then_inc(wg_ready, 1)
                    for j in range(2):
                        split(s0 + 2 * j + 4)
                        dve.wait_ge(q_squared, NT * (j + 1))
                        ms, rstd = q_ms[:, j, 0, :], q_ms[:, j, 1, :]
                        squares = z_sb[:, :, 512 * j:512 * (j + 1)].rearrange("p t (h d) -> p t h d", h=8)
                        step(nc.vector.tensor_reduce(ms.rearrange("p (t h) -> p t h", t=NT), squares, AX.X, ALU.add))
                        nc.vector.tensor_scalar(ms, ms, 1.0 / HD, RMS_EPS, ALU.mult, ALU.add).then_inc(q_spread, 1)
                        split(s0 + 2 * j + 5)
                        dve.wait_ge(q_rstd, j + 1)
                        for tt in range(NT):
                            for gp in range(2):
                                at = 256 * gp
                                each = rstd[:, 8 * tt + 4 * gp:8 * tt + 4 * gp + 4].unsqueeze(2).to_broadcast([P, PER_GROUP, HD])
                                ins = nc.vector.tensor_tensor(q_n[:, tt, j, :].rearrange("p (r g d) -> p r g d", r=PER_GROUP, g=2)[:, :, gp, :],
                                                              bank[2 * j + tt][:, at:at + 256].rearrange("p (r d) -> p r d", r=PER_GROUP),
                                                              each, ALU.mult)
                        ins.then_inc(q_normed, 1)
                    for j in range(2):
                        for rp in range(2):
                            dve.wait_ge(qT_psum, 2 * j + rp + 1)
                            nc.vector.tensor_scalar(qT[:, j, 2 * rp:2 * rp + 2, :].rearrange("p r m -> p (r m)"), bank[Q_T[j][rp]][:],
                                                    cols[:, Q_NORM:Q_NORM + 1], HD ** -0.5, ALU.mult, ALU.mult).then_inc(qT_ready, 1)

                    def per_query(x):
                        return x[:].unsqueeze(2).to_broadcast([P, NT, NQ, 16])

                    def per_head(x):
                        return x.unsqueeze(3).to_broadcast([P, NT, NQ, 16])

                    def row_maxima(w):
                        dve.wait_ge(sel_scored, w + 1)
                        if w >= 2:
                            dve.wait_ge(sel_exped, w - 1)
                        for b in range(3):
                            heads = 4 if b == 0 else 2
                            to = sel_max[:, w % 2, 0:4] if b == 0 else sel_max[:, w % 2, 2 + 2 * b:4 + 2 * b]
                            ins = nc.vector.tensor_reduce(to, bank[SCORES[w % 2][b]][:].rearrange("p (r m) -> p r m", r=heads), AX.X, ALU.max)
                        step(ins)
                        nc.vector.tensor_scalar(sel_max[:, w % 2, :], sel_max[:, w % 2, :], -1.0, None, ALU.mult).then_inc(sel_neg, 1)

                    def transposed_weights(w):
                        dve.wait_ge(selT_psum, w + 1)
                        if w >= 2:
                            dve.wait_ge(sel_out, w - 1)
                        nc.vector.tensor_copy(sel_pT[:, w % 2, 2, :], bank[SCORES[w % 2][2]][:]).then_inc(selT_dve, 1)

                    def weigh(w):
                        g, branch = w // 2, 1 + w % 2
                        dve.wait_ge(sel_exped, w + 1)
                        step(nc.vector.reciprocal(sel_sum[:, w % 2, :, :], sel_sum[:, w % 2, :, :]))
                        gate = branch_gate[:].rearrange("p t (h c) -> p t h c", c=3)[:, :, PER_GROUP * g:PER_GROUP * (g + 1), branch]
                        nc.vector.tensor_tensor(sel_coef[:, w % 2, :, :], sel_sum[:, w % 2, :, :], gate, ALU.mult).then_inc(sel_weighed, 1)

                    def add_unit(w):
                        g = w // 2
                        dve.wait_ge(sel_weighed, w + 1)
                        dve.wait_ge(sel_out, w + 1)
                        each = sel_coef[:, w % 2, :, :].rearrange("p t r -> p (t r)").unsqueeze(2).to_broadcast([P, NT * PER_GROUP, HD])
                        step(nc.vector.tensor_tensor(sel_add[:].rearrange("p (r d) -> p r d", d=HD),
                                                     bank[6 + w % 2][:].rearrange("p (r d) -> p r d", d=HD), each, ALU.mult))
                        zg = z_sb[:, :, 256 * g:256 * (g + 1)]
                        nc.vector.tensor_tensor(zg, zg, sel_add[:].rearrange("p (t n) -> p t n", t=NT), ALU.add).then_inc(attended, 1)
                        dve.wait_ge(attended, w + 1)

                    dve.wait_ge(cmp_masks, 1)
                    dve.wait_ge(cmp_scored, 1)
                    top, total = cmp_row[:, 0, :, :], cmp_row[:, 1, :, :]
                    for gp in range(2):
                        for tt in range(NT):
                            o = cmp_l[:, tt, :, :].rearrange("p (j g r) n -> p j g r n", j=2, g=2)[:, :, gp, :, :]
                            mask = cmp_mask[:, tt, :].unsqueeze(1).unsqueeze(1).to_broadcast([P, 2, PER_GROUP, 16])
                            ins = nc.vector.tensor_tensor(o, bank[1 + gp][:, tt * P:(tt + 1) * P].rearrange("p (j r n) -> p j r n", j=2, r=PER_GROUP),
                                                          mask, ALU.add)
                    step(ins)
                    step(nc.vector.tensor_reduce(top, cmp_l, AX.X, ALU.max))
                    nc.vector.tensor_tensor(cmp_l, cmp_l, per_head(top), ALU.subtract).then_inc(cmp_shifted, 1)
                    row_maxima(0)
                    dve.wait_ge(cmp_exped, 1)
                    step(nc.vector.tensor_reduce(total, cmp_l, AX.X, ALU.add))
                    step(nc.vector.reciprocal(total, total))
                    dve.wait_ge(branch_gates, 1)
                    gate = branch_gate[:].rearrange("p t (h c) -> p t h c", c=3)[:, :, :, 0]
                    step(nc.vector.tensor_tensor(total, total, gate, ALU.mult))
                    step(nc.vector.tensor_tensor(cmp_l, cmp_l, per_query(cmp_valid), ALU.mult))
                    nc.vector.tensor_tensor(cmp_p[:, :, :, 0:16], cmp_l, per_head(total), ALU.mult).then_inc(cmp_weighted, 1)
                    row_maxima(1)
                    dve.wait_ge(z_started, 2 * NT)
                    for w in range(UNITS):
                        transposed_weights(w)
                        weigh(w)
                        if w > 0:
                            add_unit(w - 1)
                        if w + 2 < UNITS:
                            row_maxima(w + 2)
                    add_unit(UNITS - 1)
                    evacuate_input(inputs_before(n) + 1)
                    for d in range(KC // 2 - 1):
                        split(s0 + 4 + d + 4)
                    boundary(n, 1.0, s0 + 8)
                    split(s0 + 4 + KC // 2 - 1 + 4)
                if kind == FFN:
                    f = ffn_number[n]

                    def hidden(j, i=0):
                        dve.wait_ge(hT_high, FT * f + j + 1 + 2 * i)
                        nc.vector.tensor_tensor(hT_lo[:, bass.ds(2 * j + 4 * i, 2), :],
                                                bank[4 + j % 2][:].rearrange("p (c m) -> p c m", c=2),
                                                hT_hi[:, bass.ds(2 * j + 4 * i, 2), :].bitcast(F32),
                                                ALU.subtract).then_inc(hT_ready, 1)

                    def tile(j, i=0):
                        if not (isinstance(i, int) and j == 0):
                            hidden(j - 1, i)
                        split(s0 + 2 * j + 4, i)
                        for tt in range(NT):
                            dve.wait_ge(silu_ready, 2 * FT * f + 2 * j + tt + 1 + 4 * i)
                            nc.vector.tensor_tensor(h[:, tt, :], silu[:, tt, :], bank[2 * (j % 2) + tt][:, 256:512],
                                                    ALU.mult).then_inc(h_ready, 1)
                        split(s0 + 2 * j + 5, i)

                    for j in range(3):
                        tile(j)
                    if n == 0:
                        small_parameters()
                    with dve.Fori(0, (FT - 3) // 2) as i:
                        for j in range(3, 5):
                            tile(j, i)
                    for d in range(FC // 2):
                        if d == 1:
                            hidden(FT - 1)
                        if d < FC // 2 - 1:
                            split(s0 + 2 * FT + d + 4)
                    boundary(n, 0.5, s0 + 33)
                    split(s0 + 2 * FT + FC // 2 - 1 + 4)

        @block.tensor
        def _(pe):
            def product(o, x_hi, x_lo, wh, wl, first, last_one, shared=False):
                nc.tensor.matmul(o, x_lo, wh, start=first, stop=False, skip_group_check=shared)
                nc.tensor.matmul(o, x_hi, wl, start=False, stop=False, skip_group_check=shared)
                return nc.tensor.matmul(o, x_hi, wh, start=False, stop=last_one, skip_group_check=shared)

            def transpose_input(src, tt):
                for q in range(2):
                    for c in range(4):
                        k = 4 * q + c
                        ins = nc.tensor.transpose(TB[tt][q][:, c * P:(c + 1) * P], src[:, tt, k * P:(k + 1) * P], ident[:])
                    ins.then_inc(xT_psum, 1)

            def next_input(n, tt):
                if n == 0:
                    pe.wait_ge(loaded_x[tt], 16)
                else:
                    pe.wait_ge(normed, normed_before(n) - NT + tt + 1)
                transpose_input(operand(n), tt)

            def slab_view(slot, chunks, width):
                hi = w_hi[:, slot, 0:chunks * width].rearrange("p (k n) -> p k n", k=chunks)
                lo = w_lo[:, slot, 0:chunks * width].rearrange("p (k n) -> p k n", k=chunks)
                return hi, lo

            def project_slab(k, d, slabs, lhs_hi, lhs_lo):
                pe.wait_ge(low_ready, k + 1)
                hi, lo = slab_view(k % SLOTS, 2, D)
                last_slab = d == slabs - 1
                order = [(c, tt) for tt in range(NT) for c in range(2)] if last_slab else [(c, tt) for c in range(2) for tt in range(NT)]
                for c, tt in order:
                    for half in range(2):
                        at = slice(half * 512, (half + 1) * 512)
                        toks = slice(tt * P, (tt + 1) * P)
                        ins = product(Y[tt][half][:], lhs_hi[:, 2 * d + c, toks], lhs_lo[:, 2 * d + c, toks],
                                      hi[:, c, at], lo[:, c, at], d == 0 and c == 0, last_slab and c == 1)
                    if last_slab and c == 1 and tt == 0:
                        ins.then_inc(y_ready, 1)
                ins.then_inc(slab_used, 1)

            def feature_slab(k, kh, banks, blocks):
                pe.wait_ge(low_ready, k + 1)
                hi, lo = slab_view(k % SLOTS, 4, 512)
                for c in range(4):
                    for fb in range(blocks):
                        at = slice(fb * P, (fb + 1) * P)
                        ins = product(banks[fb // 2][:, (fb % 2) * S:(fb % 2 + 1) * S], hi[:, c, at], lo[:, c, at],
                                      xT_hi[:, 4 * kh + c, :], xT_lo[:, 4 * kh + c, :],
                                      kh == 0 and c == 0 and fb % 2 == 0, kh == 1 and c == 3, shared=True)
                return ins

            def token_slab(k, kh, width, at, dst, shared=False):
                pe.wait_ge(low_ready, k + 1)
                hi, lo = slab_view(k % SLOTS, 4, width)
                for c in range(4):
                    for tt in range(NT):
                        toks = slice(tt * P, (tt + 1) * P)
                        ins = product(dst(tt), xT_hi[:, 4 * kh + c, toks], xT_lo[:, 4 * kh + c, toks], hi[:, c, at], lo[:, c, at],
                                      kh == 0 and c == 0 and not (shared and tt), kh == 1 and c == 3, shared=shared)
                return ins

            pe.wait_ge(consts, 1)
            for tt in range(NT):
                next_input(0, tt)
            for n, kind in enumerate(phases):
                s0 = first_slab[n]
                if kind != FFN:
                    pe.wait_ge(xT_ready, 4 * (inputs_before(n) + 1))
                if kind == FFN:
                    f = ffn_number[n]

                    def gate_up(j, kh, i=0, tiles=range(NT)):
                        k = s0 + 2 * j + kh
                        pe.wait_ge(low_ready, k + 1 + 4 * i)
                        hi, lo = slab_view(k % SLOTS, 4, 512)
                        for c in range(4):
                            for tt in tiles:
                                toks = slice(tt * P, (tt + 1) * P)
                                ins = product(bank[2 * (j % 2) + tt][:], xT_hi[:, 4 * kh + c, toks], xT_lo[:, 4 * kh + c, toks],
                                              hi[:, c, :], lo[:, c, :], kh == 0 and c == 0, kh == 1 and c == 3)
                        if NT - 1 in tiles:
                            ins.then_inc(slab_used, 1)

                    def hidden(j, i=0, free=True):
                        pe.wait_ge(h_ready, 2 * FT * f + 2 * j + 2 + 4 * i)
                        if j >= 2:
                            pe.wait_ge(hT_ready, FT * f + j - 1 + 2 * i)
                        dst = bank[4 + j % 2][:].rearrange("p (c m) -> p c m", c=2)
                        for c in range(2):
                            for tt in range(NT):
                                ins = nc.tensor.transpose(dst[:, c, tt * P:(tt + 1) * P], h[:, tt, c * P:(c + 1) * P], ident[:])
                        ins.then_inc(hT_psum, 1)

                    def tile(j, i=0):
                        gate_up(j, 0, i)
                        hidden(j - 1, i)
                        gate_up(j, 1, i)

                    for tt in range(NT):
                        for kh in range(2):
                            pe.wait_ge(xT_ready, 4 * inputs_before(n) + 2 * tt + kh + 1)
                            gate_up(0, kh, tiles=[tt])
                            if tt == 0 and kh == 0 and n > 0:
                                next_input(n, 1)
                    for j in range(1, 3):
                        tile(j)
                    if n == 0:
                        pe.wait_ge(loaded_rows, 16 * 9)
                        nc.tensor.transpose(bank[7][:, 0:ROWS], z_sb[0:ROWS, 0, 0:P], ident[0:ROWS, 0:ROWS]).then_inc(cols_psum, 1)
                    with pe.Fori(0, (FT - 3) // 2) as i:
                        for j in range(3, 5):
                            tile(j, i)
                    if n == 0:
                        pe.wait_ge(cols_ready, 1)
                    if n > 0 and phases[n - 1] == KV:
                        pe.wait_ge(keys_ready, 2)
                    for d in range(FC // 2):
                        pe.wait_ge(hT_ready, FT * f + d + 1)
                        project_slab(s0 + 2 * FT + d, d, FC // 2, hT_hi, hT_lo)
                        if d == 0:
                            hidden(FT - 1)
                if kind == MIXER:
                    def slab(d):
                        tile, kh = MIX_SLABS[d]
                        what, k, banks = TILES[tile], s0 + d, pair_of(tile)
                        if kh == 0 and tile >= 2:
                            pe.wait_ge(pair_read[tile % 2], pair_reads(tile))
                        if what[0] == "gate":
                            ins = token_slab(k, kh, 512, slice(0, 512), lambda tt: banks[tt][:])
                        elif what[0] == "branch":
                            pe.wait_ge(oT_ready, BC * (what[1] + 1))
                            pe.wait_ge(low_ready, k + 1)
                            hi, lo = slab_view(k % SLOTS, BC, 512)
                            for c in range(BC):
                                for tt in range(NT):
                                    toks = slice(tt * P, (tt + 1) * P)
                                    ins = product(banks[tt][:], oT_hi[:, c, toks], oT_lo[:, c, toks], hi[:, c, :], lo[:, c, :],
                                                  c == 0, c == BC - 1)
                        else:
                            spans, blocks, _ = QKV[what[0]]
                            width = sum(c for _, c in spans)
                            if blocks:
                                ins = feature_slab(k, kh, banks, blocks)
                            if blocks == 2:
                                ins = token_slab(k, kh, width, slice(256, 512), lambda tt: banks[1][:, tt * 256:(tt + 1) * 256], True)
                            if blocks == 0:
                                ins = token_slab(k, kh, width, slice(0, width), lambda tt: banks[tt][:, 0:width])
                        ins.then_inc(slab_used, 1)

                    def projected(name):
                        tile = TILES.index((name,))
                        pe.wait_ge(pair_read[tile % 2], pair_reads(tile) + 2)

                    def scores(u):
                        b, hd = u // HEADS, u % HEADS
                        if before(u) > 0:
                            pe.wait_ge(score_read, before(u))
                        for m in range(2 if b == DIFF else 1):
                            dst = bank[4 + (m if b == DIFF else u % 2)]
                            size = 32 if b == DIFF else HD
                            rows_at = slice(HD * (hd % 2) + 32 * m, HD * (hd % 2) + 32 * m + size)
                            q, key = qk[rows_at, 2 * BC * b + hd // 2, :], qk[rows_at, 2 * BC * b + BC + hd // 2, :]
                            if b == STICK:
                                for tt in range(NT):
                                    toks = slice(tt * P, (tt + 1) * P)
                                    o = dst[:, 2 * tt * P:(2 * tt + 1) * P]
                                    nc.tensor.matmul(o, q[:, toks], key[:, toks], start=True, stop=False)
                                    nc.tensor.matmul(o, ident_b[:], near[:], start=False, stop=True)
                                ins = nc.tensor.matmul(dst[:, P:2 * P], q[:, P:S], key[:, 0:P], start=True, stop=True)
                            else:
                                nc.tensor.matmul(dst[:, ROWS_A], q[:, 0:P], key[:, 0:P], start=True, stop=True)
                                ins = nc.tensor.matmul(dst[:, ROWS_B], q[:, P:S], key, start=True, stop=True)
                        ins.then_inc(scored, 1)

                    def transpose_weights(u):
                        side = 0 if u // HEADS == DIFF else u % 2
                        pe.wait_ge(prob_ready, u + 1)
                        if u > 0:
                            pe.wait_ge(probT_ready, u)
                        for i in range(3):
                            ins = nc.tensor.transpose(bank[6][:, i * P:(i + 1) * P], prob[:, side, i * P:(i + 1) * P], ident[:])
                        ins.then_inc(probT_psum, 1)

                    def outputs(u):
                        b, hd = u // HEADS, u % HEADS
                        pe.wait_ge(probT_ready, u + 1)
                        if hd == 0:
                            for name in (["v of moba, sb"], ["v of diff"], ["k, v of sb"])[b]:
                                projected(name)
                        if u % 2 == 0 and u > 0:
                            p = u // 2 - 1
                            if p // BC == DIFF:
                                pe.wait_ge(o_spread, p - BC + 1)
                            else:
                                pe.wait_ge(oT_ready, p + 1)
                        dst = bank[7][HD * (hd % 2):HD * (hd % 2 + 1), :]
                        v = [v_mix[:, tt, b * BW + hd * HD:b * BW + (hd + 1) * HD] for tt in range(NT)]
                        p = probT[:, u % 2, :]
                        nc.tensor.matmul(dst[:, 0:P], v[0], p[:, 0:P], start=True, stop=True)
                        nc.tensor.matmul(dst[:, P:S], v[0], p[:, P:2 * P], start=True, stop=False)
                        nc.tensor.matmul(dst[:, P:S], v[1], p[:, 2 * P:3 * P], start=False, stop=True).then_inc(o_psum, 1)

                    def square_sums(p):
                        pe.wait_ge(o_square, p - BC + 1)
                        nc.tensor.matmul(bank[7][:, S:2 * S], same_head[:], ms_d, start=True, stop=True).then_inc(o_sums, 1)

                    for d in ROUND[0]:
                        slab(d)
                    projected("q, k of moba")
                    projected("k of moba, q of diff")
                    pe.wait_ge(consts, 2)
                    scores(0)
                    scores(1)
                    for u in range(3 * HEADS):
                        b, hd = u // HEADS, u % HEADS
                        for d in ROUND[u + 1]:
                            slab(d)
                        if u % 2 == 1 and (u - 3) // 2 // BC == DIFF:
                            square_sums((u - 3) // 2)
                        transpose_weights(u)
                        for ahead in {MOBA: [u + 2] if hd < 4 else [u + 1] if hd == 5 else [],
                                      DIFF: [u + 1] if hd < 5 else [u + 1, u + 2],
                                      STICK: [u + 2] if hd < 4 else []}[b]:
                            if ahead == HEADS:
                                projected("q, k of diff")
                            if ahead == 2 * HEADS:
                                projected("q, k of sb")
                                projected("k, v of sb")
                            scores(ahead)
                        if u > 0:
                            outputs(u - 1)
                    outputs(3 * HEADS - 1)
                    for d in ROUND[-1]:
                        slab(d)
                    for tt in range(NT):
                        pe.wait_ge(merged, 12)
                        transpose_input(z_sb, tt)
                    pe.wait_ge(xT_ready, 4 * (inputs_before(n) + 2))
                    for d in range(KC // 2):
                        project_slab(s0 + 32 + d, d, KC // 2, xT_hi, xT_lo)
                if kind == CONV:
                    for j in range(6):
                        if j >= 2:
                            pe.wait_ge(conv_v_ready, j - 1)
                        for kh in range(2):
                            feature_slab(s0 + 2 * j + kh, kh, [bank[4 * (j % 2)], bank[4 * (j % 2) + 1]], 4)\
                                .then_inc(slab_used, 1)
                    for d in range(KC // 2):
                        pe.wait_ge(yT_ready, d + 1)
                        project_slab(s0 + 12 + d, d, KC // 2, yT_hi, yT_lo)
                if kind == KV:
                    for kh in range(2):
                        feature_slab(s0 + kh, kh, [bank[0], bank[1]], 4).then_inc(slab_used, 1)
                    for kv in range(2):
                        pe.wait_ge(xc_ready, 1 + 4 * (kv + 1))
                        for part in range(2):
                            k = s0 + 2 + 2 * kv + part
                            pe.wait_ge(low_ready, k + 1)
                            hi, lo = slab_view(k % SLOTS, 8, 256)
                            for c in range(8):
                                chunk = 8 * part + c
                                at = slice(2 * chunk, 2 * chunk + 16 * CMP_ROWS - 15, 16)
                                ins = product(bank[6 + kv][0:CMP_ROWS, 0:CMP_HID], xc_hi[:, kv, at], xc_lo[:, kv, at],
                                              hi[:, c, :], lo[:, c, :], chunk == 0, chunk == 15)
                            ins.then_inc(slab_used, 1)
                    def transpose_hidden(kv):
                        pe.wait_ge(hid_rows, kv + 1)
                        for hb in range(2):
                            ins = nc.tensor.transpose(hidden_of(kv, hb), hid_row[:, kv, hb * P:(hb + 1) * P], ident[0:CMP_ROWS, 0:CMP_ROWS])
                        ins.then_inc(hidT_psum, 1)

                    transpose_hidden(0)
                    for kh in range(2):
                        token_slab(s0 + 6 + kh, kh, 512, slice(0, 512), lambda tt: bank[4 + tt][:]).then_inc(slab_used, 1)
                        if kh == 0:
                            transpose_hidden(1)
                    pe.wait_ge(loaded_kv, 32)
                    pe.wait_ge(hid_ready, 4)
                    for hb in range(2):
                        ins = nc.tensor.matmul(bank[6][0:GROUPS * 16, 0:HD], hid[:, 0, hb, :], cmp_w2[:, 0, hb, :], start=hb == 0, stop=hb == 1)
                    ins.then_inc(cmp_psum, 1)
                    pe.wait_ge(hid_v_ready, 1)
                    for g in range(GROUPS):
                        for hb in range(2):
                            ins = nc.tensor.matmul(bank[7][:, g * HD:(g + 1) * HD], hid_v[:, hb, g, :, :].rearrange("p r n -> p (r n)"),
                                                   cmp_w2[:, 1, hb, :], start=hb == 0, stop=hb == 1)
                    ins.then_inc(cmp_psum, 1)
                    for kh in range(2):
                        token_slab(s0 + 8 + kh, kh, 512, slice(0, 512), lambda tt: bank[2 + tt][:]).then_inc(slab_used, 1)
                    pe.wait_ge(kc_normed, 1)
                    nc.tensor.transpose(bank[6][:, P:P + GROUPS * 16], kc_n[:], ident[0:GROUPS * 16, 0:GROUPS * 16]).then_inc(kcT_psum, 1)

                    def transpose_keys(slot, b):
                        pe.wait_ge(key_normed, slot + 1)
                        for blk in range(2):
                            for tt in range(NT):
                                o = bank[b][:, blk * S + tt * P:blk * S + (tt + 1) * P]
                                ins = nc.tensor.transpose(o, key_n[:, slot, tt, blk * P:(blk + 1) * P], ident[:])
                        ins.then_inc(keyT_psum, 1)

                    pe.wait_ge(cmp_ready, 1)
                    transpose_keys(0, 7)
                    pe.wait_ge(cmp_ready, 2)
                if kind == NSA:
                    for j in range(2):
                        for kh in range(2):
                            token_slab(s0 + 2 * j + kh, kh, 512, slice(0, 512), lambda tt: bank[2 * j + tt][:]).then_inc(slab_used, 1)
                    pe.wait_ge(wg_ready, 1)
                    for c in range(KC):
                        for tt in range(NT):
                            toks = slice(tt * P, (tt + 1) * P)
                            ins = product(bank[4][:, tt * 3 * NQ:(tt + 1) * 3 * NQ], xT_hi[:, c, toks], xT_lo[:, c, toks], wg_hi[:, c, :], wg_lo[:, c, :],
                                          c == 0 and tt == 0, c == KC - 1, shared=True)
                    ins.then_inc(gates_psum, 1)
                    for j in range(2):
                        pe.wait_ge(q_normed, j + 1)
                        for rp in range(2):
                            for r in range(2):
                                for tt in range(NT):
                                    at = slice((2 * rp + r) * P, (2 * rp + r + 1) * P)
                                    o = bank[Q_T[j][rp]][:, r * S + tt * P:r * S + (tt + 1) * P]
                                    ins = nc.tensor.transpose(o, q_n[:, tt, j, at], ident[:])
                            ins.then_inc(qT_psum, 1)

                    def query(g, r, tt):
                        return qT[HD * (g % 2):HD * (g % 2 + 1), g // 2, r, tt * P:(tt + 1) * P]

                    def scores(w):
                        g, keys = w // 2, (k_sel, k_win)[w % 2]
                        key = keys[HD * (g % 2):HD * (g % 2 + 1), g // 2, :]
                        if w >= 2:
                            pe.wait_ge(selT_act, w - 1)
                            pe.wait_ge(selT_dve, w - 1)
                        banks = [bank[i] for i in SCORES[w % 2]]
                        for b in range(3):
                            heads = 4 if b == 0 else 2
                            o = banks[b][:].rearrange("p (r m) -> p r m", r=heads)[:, :, (S - P) * (b > 0):]
                            nc.tensor.matmul(o, ident_b[:], causal[:].unsqueeze(1).to_broadcast([P, heads, P]), start=True, stop=False,
                                             skip_group_check=True)
                        for tt in range(NT):
                            for r in range(PER_GROUP):
                                b, at = score_place(tt, r)
                                ins = nc.tensor.matmul(banks[b][:, at], query(g, r, tt), key[:, 0:P * (tt + 1)], start=False, stop=True,
                                                       skip_group_check=True)
                        ins.then_inc(sel_scored, 1)

                    def transpose_weights(w):
                        pe.wait_ge(sel_exped, w + 1)
                        for b in range(3):
                            for i in range(4):
                                at = slice(i * P, (i + 1) * P)
                                ins = nc.tensor.transpose(bank[SCORES[w % 2][b]][:, at], sel_p[:, w % 2, b, at], ident[:])
                        ins.then_inc(selT_psum, 1)

                    def outputs(w):
                        g, values = w // 2, (v_sel, v_win)[w % 2]
                        pe.wait_ge(selT_act, w + 1)
                        pe.wait_ge(selT_dve, w + 1)
                        if w >= 2:
                            pe.wait_ge(attended, w - 1)
                        for tt in range(NT):
                            for r in range(PER_GROUP):
                                b, at = score_place(tt, r)
                                o = bank[6 + w % 2][:, (tt * PER_GROUP + r) * HD:(tt * PER_GROUP + r + 1) * HD]
                                for key_tile in range(tt + 1):
                                    p = sel_pT[:, w % 2, b, at.start + key_tile * P:at.start + (key_tile + 1) * P]
                                    ins = nc.tensor.matmul(o, p, values[:, key_tile, g * HD:(g + 1) * HD], start=key_tile == 0, stop=key_tile == tt)
                        ins.then_inc(sel_out, 1)

                    pe.wait_ge(qT_ready, 4)
                    for tt in range(NT):
                        for hd in range(NQ):
                            g, r = hd // PER_GROUP, hd % PER_GROUP
                            at = tt * P + (g // 2 * PER_GROUP + r) * 16
                            o = bank[1 + g % 2][:, at:at + 16]
                            ins = nc.tensor.matmul(o, query(g, r, tt), k_cmp[HD * (g % 2):HD * (g % 2 + 1), 16 * g:16 * (g + 1)], start=True, stop=True)
                    ins.then_inc(cmp_scored, 1)
                    pe.wait_ge(branch_gates, 1)
                    pe.wait_ge(consts, 2)
                    scores(0)
                    pe.wait_ge(cmp_weighted, 1)
                    for tt in range(NT):
                        for g in range(GROUPS):
                            p = cmp_p[:, tt, PER_GROUP * g:PER_GROUP * (g + 1), :].rearrange("p r n -> p (r n)")
                            ins = nc.tensor.transpose(bank[2 * tt][:, g * P:(g + 1) * P], p, ident[:])
                        ins.then_inc(cmpT_psum, 1)
                    for tt in range(NT):
                        pe.wait_ge(cmpT_ready, tt + 1)
                        for g in range(GROUPS):
                            o = bank[CMP_OUT[tt][g // 2]][:, (g % 2) * S:(g % 2 + 1) * S]
                            ins = nc.tensor.matmul(o, cmp_pT[:, tt, g, :], v_cmp[:, g, :], start=True, stop=True)
                        ins.then_inc(cmp_out, 1)
                    pe.wait_ge(z_started, 2 * NT)
                    scores(1)
                    for w in range(UNITS):
                        transpose_weights(w)
                        if w > 0:
                            outputs(w - 1)
                        if w + 2 < UNITS:
                            scores(w + 2)
                    outputs(UNITS - 1)
                    for tt in range(NT):
                        pe.wait_ge(attended, UNITS)
                        transpose_input(z_sb, tt)
                    pe.wait_ge(xT_ready, 4 * (inputs_before(n) + 2))
                    for d in range(KC // 2):
                        project_slab(s0 + 4 + d, d, KC // 2, xT_hi, xT_lo)
                if n < last:
                    for tt in range(1 if phases[n + 1] == FFN else NT):
                        next_input(n + 1, tt)
                if kind == KV:
                    transpose_keys(1, 6)


_INS = ["x", "ln_g", "ln_b", "ffn_w_gate", "ffn_w_up", "ffn_w_down", "w_in", "b_gate", "diff_lambda", "diff_subln_g",
        "w_br_moba", "w_br_diff", "w_br_sb", "w_out", "ffn_norm_2", "ffn_w_gate_up_2", "ffn_w_down_2", "mix_norm_2",
        "conv_w_in_2", "conv_w_2", "conv_w_out_2", "kv_norm_2", "kv_w_2", "cmp_pos_2", "cmp_w1_2", "cmp_b1_2",
        "cmp_w2_2", "k_norm_2", "nsa_w_qg_2", "q_norm_2", "nsa_w_o_2"]


def kernel(**inputs):
    import numpy as _np
    import concourse.bacc as _bacc
    from concourse import mybir as _mybir
    from concourse.bass_utils import run_bass_kernel_spmd as _run

    nc = _bacc.Bacc("TRN2", target_bir_lowering=False, num_devices=1)
    arrays, t = {}, {}
    for name in _INS:
        a = _np.ascontiguousarray(inputs[name])
        arrays[f"in_{name}_dram"] = a
        t[name] = nc.dram_tensor(f"in_{name}_dram", a.shape, _mybir.dt.from_np(a.dtype), kind="ExternalInput").ap()
    out = nc.dram_tensor("out_0_dram", (1, S, D), _mybir.dt.float32, kind="ExternalOutput").ap()
    two_block_kernel(nc, t, out[0])
    r = _run(nc, [arrays], core_ids=[0])
    return r.results[0]["out_0_dram"]
```

```python
from contextlib import ExitStack

import concourse.bass as bass
from concourse import mybir

F32 = mybir.dt.float32
F32R = mybir.dt.float32r
BF16 = mybir.dt.bfloat16
ALU = mybir.AluOpType
ACT = mybir.ActivationFunctionType
AX = mybir.AxisListType

P = 128
D = 1024
KC = D // P
S = 256
NT = S // P
FF = 2816
FT = FF // 256
FC = FF // P
SLOTS = 4
SLAB = 2048
HD = 64
BW = 384
BC = BW // P
BRANCH_HEADS = BW // HD
ALPHA = 2.0 ** 0.25
LN_EPS = 1e-5
SUBLN_EPS = 1e-5
RMS_EPS = 1e-6
LAMBDA_INIT = 0.8 - 0.6
DIFF_SCALE = 32.0 ** -0.5
MASKED = -1e30
N_CMP = 15
GROUPS = 4
PER_GROUP = 4
CMP_HID = 256
CMP_ROWS = 16 * (GROUPS + 1)
XC = CMP_ROWS * 16 + 16

CONV_W, POS, CMP_B, Q_NORM, K_NORM, SUBLN, ROWS = 0, 24, 56, 60, 61, 64, 65

FFN, MIXER, CONV, KV, NSA = "ffn", "mixer", "conv", "kv", "nsa"
PHASES = [FFN, MIXER, FFN, FFN, CONV, FFN, KV, FFN, NSA, FFN]
LENGTH = {FFN: 33, MIXER: 36, CONV: 16, KV: 10, NSA: 8}
STOP = len(PHASES)


def alibi_slope(i):
    return 2.0 ** (-8.0 * (i + 1) / 12.0)


def two_block_kernel(nc, t, out):
    phases = PHASES[:STOP]
    first_slab = [sum(LENGTH[k] for k in phases[:n]) for n in range(len(phases) + 1)]
    TOTAL = first_slab[-1]
    ffn_number = [sum(k == FFN for k in phases[:n]) for n in range(len(phases))]

    with ExitStack() as ctx:
        def sb(name, shape, dt=F32):
            return ctx.enter_context(nc.sbuf_tensor(name, shape, dt))

        def sem(name):
            return ctx.enter_context(nc.semaphore(name))

        raw = sb("raw", [P, SLOTS, SLAB])
        w_hi = sb("w_hi", [P, SLOTS, SLAB], F32R)
        w_lo = sb("w_lo", [P, SLOTS, SLAB], F32R)
        x_sb = sb("x_sb", [P, NT, D])
        z_sb = sb("z_sb", [P, NT, D])
        xT_hi = sb("xT_hi", [P, KC, S], F32R)
        xT_lo = sb("xT_lo", [P, KC, S], F32R)
        gain = sb("gain", [P, 3, D])
        stats = sb("stats", [P, 64])
        bn = sb("bn", [P, NT, 2, 6])
        head_max = sb("head_max", [P, 2, 4])
        head_sum = sb("head_sum", [P, 2, 4])
        lam_col = sb("lam_col", [P, 8])
        near = sb("near", [P, P], BF16)
        causal = sb("causal", [P, P], BF16)
        same_head = sb("same_head", [P, P])
        minus_half = sb("minus_half", [P, 32])
        ident = sb("ident", [P, P])
        ident_b = sb("ident_b", [P, P], BF16)
        cols = sb("cols", [P, 80])

        bank = [ctx.enter_context(nc.psum_tensor(f"bank{i}", [P, 512], F32)) for i in range(8)]
        Y = [[bank[2], bank[3]], [bank[6], bank[7]]]
        TOKENS_FIRST = [(0, 0, bank[0]), (0, 1, bank[1]), (1, 0, bank[4]), (1, 1, bank[5])]
        HALVES_FIRST = [(0, 0, bank[4]), (1, 0, bank[5]), (0, 1, bank[0]), (1, 1, bank[1])]

        def layer_memory(tensors):
            with ExitStack() as own:
                return [own.enter_context(nc.sbuf_tensor(n, s, d)) for n, s, d in tensors]

        qk, v_mix, oT_hi, oT_lo, gates, b_gate, prob, probT, far, tmp, o_norm = layer_memory([
            ("qk", [P, 6 * BC, S], F32),
            ("v_mix", [P, NT, 3 * BW], F32),
            ("oT_hi", [P, BC, S], F32R), ("oT_lo", [P, BC, S], F32R),
            ("gates", [P, NT, D], F32), ("b_gate", [P, 3, D], F32),
            ("prob", [P, 2, BW], F32),
            ("probT", [P, 2, BW], F32),
            ("far", [P, BW], F32),
            ("tmp", [P, 512], F32), ("o_norm", [P, 2, S], F32)])
        ms_d, o_f, o_root = o_norm[:, 0, :], o_norm[:, 1, :], tmp[:, S:2 * S]
        stick = far
        k_sel = sb("k_sel", [P, 2, S])
        k_win = sb("k_win", [P, 2, S])
        v_sel = sb("v_sel", [P, NT, S])
        v_win = sb("v_win", [P, NT, S])
        k_cmp = sb("k_cmp", [P, GROUPS * 16])
        key_n = sb("key_n", [P, 2, NT, S])
        kc_n = sb("kc_n", [GROUPS * 16, 2 * HD])
        v_cmp = sb("v_cmp", [P, GROUPS, PER_GROUP * HD])
        xc_hi, xc_lo, hid_row, cmp_w2, hid, hid_v, key_sq, key_ms, cmp_bias, kc_sq, kc_ms = layer_memory([
            ("xc_hi", [P, 2, XC], F32R), ("xc_lo", [P, 2, XC], F32R),
            ("hid_row", [CMP_ROWS, 2, CMP_HID], F32),
            ("cmp_w2", [P, 2, 2, HD], F32), ("hid", [P, 2, 2, GROUPS * 16], F32),
            ("hid_v", [P, 2, GROUPS, PER_GROUP, 32], F32),
            ("key_sq", [P, 2, NT, S], F32), ("key_ms", [P, 2, 2, NT * GROUPS], F32),
            ("cmp_bias", [P, 2, 2], F32), ("kc_sq", [GROUPS * 16, HD], F32),
            ("kc_ms", [GROUPS * 16, 4], F32)])
        NQ = D // HD
        wg, wg_hi, wg_lo, branch_gate, q_ms, qT, sel_p, sel_pT, cmp_p, cmp_pT, cmp_mask, cmp_valid, cmp_row, sel_max, sel_sum, \
            sel_coef, sel_add = layer_memory([
                ("wg", [P, KC, 3 * NQ], F32), ("wg_hi", [P, KC, 3 * NQ], F32R), ("wg_lo", [P, KC, 3 * NQ], F32R),
                ("branch_gate", [P, NT, 3 * NQ], F32), ("q_ms", [P, 2, 2, NQ], F32),
                ("qT", [P, 2, PER_GROUP, S], F32),
                ("sel_p", [P, 2, 3, 512], F32), ("sel_pT", [P, 2, 3, 512], F32),
                ("cmp_p", [P, NT, NQ, 32], F32), ("cmp_pT", [P, NT, GROUPS, P], F32),
                ("cmp_mask", [P, NT, 16], F32), ("cmp_valid", [P, NT, 16], F32), ("cmp_row", [P, 2, NT, NQ], F32),
                ("sel_max", [P, 2, 8], F32), ("sel_sum", [P, 2, NT, PER_GROUP], F32), ("sel_coef", [P, 2, NT, PER_GROUP], F32),
                ("sel_add", [P, 512], F32)])
        q_n = sel_pT[:].rearrange("p a b c -> p (a b c)")[:, 0:NT * D].rearrange("p (t n c) -> p t n c", t=NT, n=2)
        cmp_l = sel_add[:].rearrange("p (t h n) -> p t h n", t=NT, h=NQ)
        hT_hi, hT_lo, silu, h = layer_memory([
            ("hT_hi", [P, FC, S], F32R), ("hT_lo", [P, FC, S], F32R),
            ("silu", [P, NT, 256], F32), ("h", [P, NT, 256], F32)])
        conv_v, conv_a, conv_c, conv_y, yT_hi, yT_lo = layer_memory([
            ("conv_v", [P, KC, S + 2], F32), ("conv_a", [P, KC, S], F32), ("conv_c", [P, 2, 512], F32),
            ("conv_y", [P, 2, 512], F32), ("yT_hi", [P, KC, S], F32R), ("yT_lo", [P, KC, S], F32R)])

        arrived = [sem(f"arrived{i}") for i in range(SLOTS)]
        high_ready = sem("high_ready")
        low_ready = sem("low_ready")
        slab_used = sem("slab_used")
        loaded_x = [sem(f"loaded_x{i}") for i in range(NT)]
        loaded_p = sem("loaded_p")
        loaded_mix = sem("loaded_mix")
        loaded_lam = sem("loaded_lam")
        lam_dots = sem("lam_dots")
        lam_exp = sem("lam_exp")
        pair_read = [sem("pair0_read"), sem("pair1_read")]
        far_ready = sem("far_ready")
        scored = sem("scored")
        score_read = sem("score_read")
        neg_ready = sem("neg_ready")
        exped = sem("exped")
        logs = sem("logs")
        prob_ready = sem("prob_ready")
        probT_psum = sem("probT_psum")
        probT_ready = sem("probT_ready")
        o_psum = sem("o_psum")
        o_copied = sem("o_copied")
        o_square = sem("o_square")
        o_sums = sem("o_sums")
        o_spread = sem("o_spread")
        o_log = sem("o_log")
        o_rstd = sem("o_rstd")
        o_normed = sem("o_normed")
        oT_high = sem("oT_high")
        oT_ready = sem("oT_ready")
        gate_sum = sem("gate_sum")
        gated = sem("gated")
        multiplied = sem("multiplied")
        merged = sem("merged")
        conv_c_ready = sem("conv_c_ready")
        conv_v_ready = sem("conv_v_ready")
        conv_y_ready = sem("conv_y_ready")
        yT_high = sem("yT_high")
        yT_ready = sem("yT_ready")
        loaded_kv = sem("loaded_kv")
        xc_high = sem("xc_high")
        xc_ready = sem("xc_ready")
        xc_zero = sem("xc_zero")
        hid_rows = sem("hid_rows")
        hidT_psum = sem("hidT_psum")
        bias_ready = sem("bias_ready")
        hid_ready = sem("hid_ready")
        hid_v_ready = sem("hid_v_ready")
        cmp_psum = sem("cmp_psum")
        kc_squared = sem("kc_squared")
        kc_spread = sem("kc_spread")
        kc_rstd = sem("kc_rstd")
        kc_normed = sem("kc_normed")
        kcT_psum = sem("kcT_psum")
        cmp_ready = sem("cmp_ready")
        key_squared = sem("key_squared")
        key_spread = sem("key_spread")
        key_rstd = sem("key_rstd")
        key_normed = sem("key_normed")
        keyT_psum = sem("keyT_psum")
        keys_ready = sem("keys_ready")
        values_ready = sem("values_ready")
        loaded_wg = sem("loaded_wg")
        wg_high = sem("wg_high")
        wg_ready = sem("wg_ready")
        gates_psum = sem("gates_psum")
        branch_gates = sem("branch_gates")
        q_squared = sem("q_squared")
        q_spread = sem("q_spread")
        q_rstd = sem("q_rstd")
        q_normed = sem("q_normed")
        qT_psum = sem("qT_psum")
        qT_ready = sem("qT_ready")
        cmp_masks = sem("cmp_masks")
        cmp_scored = sem("cmp_scored")
        cmp_shifted = sem("cmp_shifted")
        cmp_exped = sem("cmp_exped")
        cmp_weighted = sem("cmp_weighted")
        cmpT_psum = sem("cmpT_psum")
        cmpT_ready = sem("cmpT_ready")
        cmp_out = sem("cmp_out")
        z_started = sem("z_started")
        sel_scored = sem("sel_scored")
        sel_neg = sem("sel_neg")
        sel_exped = sem("sel_exped")
        sel_weighed = sem("sel_weighed")
        selT_psum = sem("selT_psum")
        selT_act = sem("selT_act")
        selT_dve = sem("selT_dve")
        sel_out = sem("sel_out")
        attended = sem("attended")
        consts = sem("consts")
        cols_psum = sem("cols_psum")
        cols_ready = sem("cols_ready")
        gain_loaded = [sem(f"gain_loaded{i}") for i in range(3)]
        scaled = sem("scaled")
        y_ready = sem("y_ready")
        summed = sem("summed")
        squared = sem("squared")
        spread = sem("spread")
        rstd_ready = sem("rstd_ready")
        normed = sem("normed")
        xT_psum = sem("xT_psum")
        xT_high = sem("xT_high")
        xT_ready = sem("xT_ready")
        silu_ready = sem("silu_ready")
        h_ready = sem("h_ready")
        hT_psum = sem("hT_psum")
        hT_high = sem("hT_high")
        hT_ready = sem("hT_ready")
        act_step = sem("act_step")
        loaded_rows = sem("loaded_rows")
        dve_step = sem("dve_step")
        pool_step = sem("pool_step")
        stored = sem("stored")

        LN, RMS = "ln", "rms"
        def apart(n):
            return n < last and phases[n] != KV and phases[n + 1] == FFN and not has_ln(n)

        def behind_kv(n):
            return n > 0 and phases[n - 1] == KV

        ln_row = {0: 0, 1: 1, 2: 2}
        rms_of = {2: t["ffn_norm_2"][0, 0], 3: t["mix_norm_2"][0], 4: t["ffn_norm_2"][0, 1], 5: t["kv_norm_2"],
                  6: t["ffn_norm_2"][1, 0], 7: t["mix_norm_2"][1], 8: t["ffn_norm_2"][1, 1]}
        last = len(phases) - 1

        def has_ln(n):
            return n in ln_row

        def has_rms(n):
            return n in rms_of and n < last

        def operand(n):
            return x_sb if n in (0, 1, 2) else z_sb

        ln_uses = [sum(has_ln(m) for m in range(n)) for n in range(len(phases) + 1)]
        rms_uses = [sum(has_rms(m) for m in range(n)) for n in range(len(phases) + 1)]
        y_layers = [sum(k != KV for k in phases[:n]) for n in range(len(phases) + 1)]

        def normed_before(n):
            return NT * (ln_uses[n] + rms_uses[n])

        def norm_index(n, tt, which):
            return normed_before(n) + tt + (NT if which == RMS and has_ln(n) else 0)

        def last_norm(n, tt):
            return norm_index(n, tt, RMS if has_rms(n) else LN) + 1

        def summed_before(n):
            return NT * y_layers[n]

        HEADS = BRANCH_HEADS
        MOBA, DIFF, STICK = range(3)
        QKV = {"q, k of moba": ([(0, 256), (256, 256)], 4, 0), "k of moba, q of diff": ([(512, 256), (1152, 256)], 4, 4),
               "v of moba, sb": ([(768, 384), (3328, 128)], 0, 0), "q, k of diff": ([(1408, 256), (1664, 256)], 4, 8),
               "v of diff": ([(1920, 192), (2112, 192)], 0, 0), "q, k of sb": ([(2304, 256), (2560, 256)], 4, 12),
               "k, v of sb": ([(2816, 256), (3072, 256)], 2, 16)}
        GATE0 = 3 * 3 * BW
        TILES = [("q, k of moba",), ("k of moba, q of diff",), ("v of moba, sb",), ("q, k of diff",), ("v of diff",),
                 ("gate", MOBA, 0), ("gate", MOBA, 1), ("branch", MOBA, 0), ("branch", MOBA, 1),
                 ("q, k of sb",), ("k, v of sb",), ("gate", DIFF, 0), ("gate", DIFF, 1), ("branch", DIFF, 0), ("branch", DIFF, 1),
                 ("gate", STICK, 0), ("gate", STICK, 1), ("branch", STICK, 0), ("branch", STICK, 1)]
        MIX_SLABS = [(i, kh) for i, what in enumerate(TILES) for kh in range(1 if what[0] == "branch" else 2)]
        STEPS = [6] + [1] * 8 + [2] * 3 + [1] * 4 + [2, 1, 1] + [4]
        ROUND = [range(sum(STEPS[:i]), sum(STEPS[:i + 1])) for i in range(len(STEPS))]
        assert ROUND[-1].stop == len(MIX_SLABS) and len(STEPS) == 3 * HEADS + 2

        def pair_of(tile):
            return [bank[2 * (tile % 2)], bank[2 * (tile % 2) + 1]]

        def pair_reads(tile):
            return 2 * (tile // 2)

        def ends(d):
            tile, kh = MIX_SLABS[d]
            return tile if kh == 1 or TILES[tile][0] == "branch" else None

        def branch_slab(b, half):
            return MIX_SLABS.index((TILES.index(("branch", b, half)), 0))

        def before(u):
            return u if u // HEADS == DIFF or u == 2 * HEADS else u - 1

        ROWS_A, ROWS_B = slice(0, P), slice(P, 3 * P)

        def tokens_of(x):
            return x[:, :, 0:16 * CMP_ROWS].rearrange("p a (g t) -> p a g t", t=S)

        def hidden_of(kv, hb):
            return bank[6 + kv][:, CMP_HID + hb * CMP_ROWS:CMP_HID + (hb + 1) * CMP_ROWS]

        UNITS = 2 * GROUPS
        Q_IN = [[0, 1], [6, 7]]
        Q_T = [[1, 2], [0, 1]]
        SCORES = [[3, 4, 5], [0, 1, 2]]
        CMP_OUT = [6, 7]

        def score_place(tt, r):
            return (0, slice(r * P, (r + 1) * P)) if tt == 0 else (1 + r // 2, slice((r % 2) * S, (r % 2 + 1) * S))

        def ffn_weights(f):
            if f < 2:
                return t["ffn_w_gate"][0, f], t["ffn_w_up"][0, f], t["ffn_w_down"][0, f]
            both = t["ffn_w_gate_up_2"][(f - 2) // 2, (f - 2) % 2]
            return both[:, 0:FF], both[:, FF:2 * FF], t["ffn_w_down_2"][(f - 2) // 2, (f - 2) % 2]

        def half_rows(w, kh):
            return w[kh * 512:(kh + 1) * 512, :].rearrange("(k p) n -> p k n", p=P)

        def inputs_before(n):
            return n + sum(k in (MIXER, NSA) for k in phases[:n])

        def width_of(k):
            n = max(m for m in range(len(phases)) if first_slab[m] <= k)
            d = k - first_slab[n]
            narrow = phases[n] == MIXER and d < len(MIX_SLABS) and TILES[MIX_SLABS[d][0]][0] in ("v of diff", "branch")
            return 4 * BW if narrow else SLAB

        block = ctx.enter_context(nc.Block())

        @block.sync
        def _(sp):
            def load(k, pieces, i=0):
                slot = k % SLOTS
                if k >= SLOTS:
                    sp.wait_ge(low_ready, k - SLOTS + 1 + 4 * i)
                for dst, src in pieces(slot):
                    sp.dma_start(dst, src).then_inc(arrived[slot], 32 // len(pieces(slot)))

            def columns(w, kh, spans, width=512):
                def pieces(slot):
                    dst = raw[:, slot, 0:4 * width].rearrange("p (k n) -> p k n", k=4)
                    at, found = 0, []
                    for c0, n in spans:
                        found.append((dst[:, :, at:at + n], half_rows(w, kh)[:, :, c0:c0 + n]))
                        at += n
                    return found
                return pieces

            def rows(w, c0, chunks=2):
                def pieces(slot):
                    return [(raw[:, slot, j * D:(j + 1) * D], w[(c0 + j) * P:(c0 + j + 1) * P, :]) for j in range(chunks)]
                return pieces

            def gain_row(row, src, n_before):
                sp.dma_start(gain[:, row, :], src.partition_broadcast(P)).then_inc(gain_loaded[row], 16)

            def gains(n):
                if n > 0:
                    sp.wait_ge(normed, normed_before(n))
                if has_ln(n):
                    gain_row(0, t["ln_g"][0, ln_row[n]], n)
                    gain_row(1, t["ln_b"][0, ln_row[n]], n)
                if has_rms(n):
                    gain_row(2, rms_of[n], n)

            for tt in range(NT):
                sp.dma_start(x_sb[:, tt, :], t["x"][0, tt * P:(tt + 1) * P, :]).then_inc(loaded_x[tt], 16)
            for n, kind in enumerate(phases):
                s0 = first_slab[n]
                if kind == FFN:
                    gate, up, down = ffn_weights(ffn_number[n])

                    def gate_up(j, kh, i=0):
                        def pieces(slot):
                            dst = raw[:, slot, :].rearrange("p (k n) -> p k n", k=4)
                            at = bass.ds(256 * j + 512 * i, 256)
                            return [(dst[:, :, 0:256], half_rows(gate, kh)[:, :, at]),
                                    (dst[:, :, 256:512], half_rows(up, kh)[:, :, at])]
                        load(s0 + 2 * j + kh, pieces, i)

                    for j in range(3):
                        for kh in range(2):
                            gate_up(j, kh)
                    if n == 0:
                        for at, src in ((CONV_W, t["conv_w_2"][0].rearrange("w (k p) -> (w k) p", p=P)),
                                        (POS, t["cmp_pos_2"].rearrange("a (c q) d -> (a c) (q d)", q=2)),
                                        (CMP_B, t["cmp_b1_2"].rearrange("a (b p) -> (a b) p", p=P))):
                            sp.dma_start(z_sb[at:at + src.shape[0], 0, 0:P], src).then_inc(loaded_rows, 16)
                        for at, src in ((Q_NORM, t["q_norm_2"]), (K_NORM, t["k_norm_2"]), (SUBLN, t["diff_subln_g"])):
                            for twice in range(2):
                                sp.dma_start(z_sb[at:at + src.shape[0], 0, twice * HD:(twice + 1) * HD], src).then_inc(loaded_rows, 16)
                        sp.dma_start(z_sb[:, 1, 0:P], t["diff_lambda"][0].rearrange("a d -> (a d)").partition_broadcast(P)).then_inc(loaded_lam, 16)
                    with sp.Fori(0, (FT - 3) // 2) as i:
                        for j in range(3, 5):
                            for kh in range(2):
                                gate_up(j, kh, i)
                    gains(n)
                    for d in range(FC // 2):
                        load(s0 + 2 * FT + d, rows(down, 2 * d))
                elif kind == MIXER:
                    w = t["w_in"][0]
                    for d, (tile, kh) in enumerate(MIX_SLABS):
                        what = TILES[tile]
                        if d == ROUND[0].stop:
                            gains(n)
                            sp.wait_ge(normed, normed_before(n))
                            sp.dma_start(b_gate[:], t["b_gate"][0].partition_broadcast(P)).then_inc(loaded_mix, 16)
                        if what[0] == "gate":
                            c0 = GATE0 + what[1] * D + what[2] * 512
                            load(s0 + d, columns(w, kh, [(c0, 256), (c0 + 256, 256)]))
                        elif what[0] == "branch":
                            wb = t[("w_br_moba", "w_br_diff", "w_br_sb")[what[1]]][0]
                            src = wb[:, what[2] * 512:(what[2] + 1) * 512].rearrange("(k p) n -> p k n", p=P)

                            def pieces(slot):
                                dst = raw[:, slot, 0:BC * 512].rearrange("p (k n) -> p k n", k=BC)
                                return [(dst[:, :, 0:256], src[:, :, 0:256]), (dst[:, :, 256:512], src[:, :, 256:512])]
                            load(s0 + d, pieces)
                        else:
                            spans = QKV[what[0]][0]
                            load(s0 + d, columns(w, kh, spans, sum(c for _, c in spans)))
                    for d in range(KC // 2):
                        load(s0 + 32 + d, rows(t["w_out"][0], 2 * d))
                elif kind == CONV:
                    w = t["conv_w_in_2"][0]
                    for j in range(4):
                        for kh in range(2):
                            load(s0 + 2 * j + kh, columns(w, kh, [(D + 256 * j, 256), (2 * D + 256 * j, 256)]))
                    for j in range(2):
                        for kh in range(2):
                            load(s0 + 8 + 2 * j + kh, columns(w, kh, [(512 * j, 256), (512 * j + 256, 256)]))
                    gains(n)
                    for d in range(KC // 2):
                        load(s0 + 12 + d, rows(t["conv_w_out_2"][0], 2 * d))
                elif kind == KV:
                    w = t["kv_w_2"]

                    def two_slots(slab, pair):
                        for kh in range(2):
                            load(s0 + slab + kh, columns(w, kh, [(512 * pair, 256), (512 * pair + 256, 256)]))

                    two_slots(0, 0)
                    two_slots(2, 1)
                    for kv in range(2):
                        for part in range(2):
                            src = t["cmp_w1_2"][kv, part * 1024:(part + 1) * 1024, :].rearrange("(k p) n -> p k n", p=P)

                            def pieces(slot):
                                dst = raw[:, slot, :].rearrange("p (k n) -> p k n", k=8)
                                return [(dst[:, 0:4, :], src[:, 0:4, :]), (dst[:, 4:8, :], src[:, 4:8, :])]
                            load(s0 + 4 + 2 * kv + part, pieces)
                        if kv == 0:
                            gains(n)
                            for a in range(2):
                                sp.dma_start(cmp_w2[:, a, :, :], t["cmp_w2_2"][a].rearrange("(b p) d -> p b d", p=P)).then_inc(loaded_kv, 16)
                    two_slots(8, 2)
                elif kind == NSA:
                    w = t["nsa_w_qg_2"][0]
                    for j in range(2):
                        for kh in range(2):
                            load(s0 + 2 * j + kh, columns(w, kh, [(512 * j, 256), (512 * j + 256, 256)]))
                    sp.wait_ge(normed, normed_before(n))
                    sp.dma_start(wg[:], w[:, D:D + 3 * NQ].rearrange("(k p) n -> p k n", p=P)).then_inc(loaded_wg, 16)
                    gains(n)
                    for d in range(KC // 2):
                        load(s0 + 4 + d, rows(t["nsa_w_o_2"][0], 2 * d))
            if has_ln(last):
                sp.wait_ge(normed, normed_before(len(phases)))
            else:
                sp.wait_ge(summed, summed_before(len(phases)))
            for tt in range(NT):
                sp.dma_start(out[tt * P:(tt + 1) * P, :], x_sb[:, tt, :]).then_inc(stored, 16)
            sp.wait_ge(stored, 16 * NT)

        @block.gpsimd
        def _(pool):
            pool.memset(ident[:], 0.0).then_inc(pool_step, 1)
            pool.wait_ge(pool_step, 1)
            pool.affine_select(out=ident[:], in_=ident[:], compare_op=ALU.not_equal, fill=1.0, base=0,
                               pattern=[[-1, P]], channel_multiplier=1).then_inc(pool_step, 1)
            pool.wait_ge(pool_step, 2)
            pool.tensor_copy(ident_b[:], ident[:]).then_inc(consts, 1)
            pool.memset(minus_half[:], -0.5).then_inc(pool_step, 1)
            pool.wait_ge(pool_step, 3)
            made = [3]

            def step(ins):
                made[0] += 1
                ins.then_inc(pool_step, 1)
                pool.wait_ge(pool_step, made[0])

            for m, first in ((near, 1), (causal, 0)):
                step(pool.memset(m[:], 0.0))
                step(pool.affine_select(out=m[:], in_=m[:], compare_op=ALU.is_ge, fill=MASKED, base=-first,
                                        pattern=[[-1, P]], channel_multiplier=1))
            step(pool.memset(same_head[:], 0.0))
            step(pool.memset(same_head[0:HD, 0:HD], 1.0))
            step(pool.memset(same_head[HD:P, HD:P], 1.0))
            pool.engine_nop().then_inc(consts, 1)

            def split(k):
                if k >= TOTAL:
                    return
                slot, width = k % SLOTS, width_of(k)
                pool.wait_ge(high_ready, k + 1)
                pool.tensor_tensor(w_lo[:, slot, 0:width], raw[:, slot, 0:width], w_hi[:, slot, 0:width].bitcast(F32),
                                   ALU.subtract).then_inc(low_ready, 1)

            def root(index, col):
                pool.wait_ge(spread, index + 1)
                pool.tensor_tensor(stats[:, col + 1:col + 2], stats[:, col:col + 1], minus_half[:, 0:1], ALU.pow).then_inc(rstd_ready, 1)

            for n, kind in enumerate(phases):
                if kind == MIXER:
                    pool.wait_ge(normed, normed_before(n))
                    for at, off in ((ROWS_A, 0), (ROWS_B, P)):
                        size = at.stop - at.start
                        step(pool.iota(far[:, at], pattern=[[1, size]], base=-off, channel_multiplier=-1,
                                       allow_small_or_imprecise_dtypes=True))
                        ins = pool.affine_select(out=far[:, at], in_=far[:, at], compare_op=ALU.is_ge, fill=MASKED, base=off,
                                                 pattern=[[-1, size]], channel_multiplier=1)
                    step(ins)
                    pool.engine_nop().then_inc(far_ready, 1)
                    s0 = first_slab[n]
                    pool.wait_ge(low_ready, s0 + ROUND[0].stop + 4)
                    for steps in ROUND[1:]:
                        if branch_slab(DIFF, 1) in steps:
                            for half in range(2):
                                for tt in range(NT):
                                    pool.wait_ge(merged, 4)
                                    pool.wait_ge(multiplied, 2 * half + tt + 1)
                                    y = z_sb[:, tt, half * 512:(half + 1) * 512]
                                    pool.tensor_tensor(y, y, gates[:, tt, half * 512:(half + 1) * 512], ALU.add).then_inc(merged, 1)
                        for d in steps:
                            split(s0 + d + 4)
                if kind == NSA:
                    pool.wait_ge(normed, normed_before(n))
                    step(pool.memset(cmp_mask[:], 0.0))
                    step(pool.memset(cmp_valid[:], 1.0))
                    step(pool.memset(cmp_p[:], 0.0))
                    for m, out_of in ((cmp_mask, MASKED), (cmp_valid, 0.0)):
                        for tt in range(NT):
                            step(pool.affine_select(out=m[:, tt, :], in_=m[:, tt, :], compare_op=ALU.is_ge, fill=out_of,
                                                    base=tt * P - 31, pattern=[[-16, 16]], channel_multiplier=1))
                    pool.engine_nop().then_inc(cmp_masks, 1)
                    for j in range(2):
                        pool.wait_ge(q_spread, j + 1)
                        pool.tensor_tensor(q_ms[:, j, 1, :], q_ms[:, j, 0, :], minus_half[:, 0:NQ], ALU.pow).then_inc(q_rstd, 1)
                if kind == KV:
                    def key_roots(slot):
                        pool.wait_ge(key_spread, slot + 1)
                        pool.tensor_tensor(key_ms[:, slot, 1, :], key_ms[:, slot, 0, :], minus_half[:, 0:NT * GROUPS],
                                           ALU.pow).then_inc(key_rstd, 1)
                    key_roots(0)
                if has_ln(n):
                    pool.wait_ge(xT_psum, 4 * (inputs_before(n) + 1))
                    pool.tensor_scalar(x_sb[:].rearrange("p t d -> p (t d)"), x_sb[:].rearrange("p t d -> p (t d)"),
                                       ALPHA, None, ALU.mult).then_inc(scaled, 1)
                    for tt in range(NT):
                        root(norm_index(n, tt, LN), 4 * tt + 2)
                if has_rms(n):
                    for tt in range(NT):
                        root(norm_index(n, tt, RMS), 10 + 2 * tt)
                if kind == KV:
                    key_roots(1)
                    pool.wait_ge(kc_spread, 1)
                    pool.tensor_tensor(kc_ms[:, 2:3], kc_ms[:, 1:2], minus_half[0:GROUPS * 16, 0:1], ALU.pow).then_inc(kc_rstd, 1)

        @block.scalar
        def _(act):
            def split(k, i=0):
                if k >= TOTAL:
                    return
                slot, width = k % SLOTS, width_of(k)
                act.wait_ge(arrived[slot], 32 * (k // SLOTS + 1) + 32 * i)
                if k >= SLOTS:
                    act.wait_ge(slab_used, k - SLOTS + 1 + 4 * i)
                nc.scalar.activation(w_hi[:, slot, 0:width], raw[:, slot, 0:width], ACT.Copy).then_inc(high_ready, 1)

            def evacuate_input(index, order=TOKENS_FIRST, first=0):
                for place, (tt, q, src) in enumerate(order, first):
                    act.wait_ge(xT_psum, 4 * index + place + 1)
                    nc.scalar.activation(xT_hi[:, 4 * q:4 * q + 4, tt * P:(tt + 1) * P],
                                         src[:].rearrange("p (k m) -> p k m", k=4), ACT.Copy).then_inc(xT_high, 1)

            def norm(n, tiles=range(NT)):
                if has_rms(n):
                    for tt in tiles:
                        if has_ln(n):
                            act.wait_ge(normed, norm_index(n, tt, LN) + 1)
                        else:
                            act.wait_ge(summed, summed_before(n) + (tt + 1 if kind != KV else 0))
                        nc.scalar.activation(z_sb[:, tt, :], x_sb[:, tt, :], ACT.Square,
                                             accum_out=stats[:, 8 + tt:9 + tt]).then_inc(squared, 1)

            def boundary(n):
                if apart(n):
                    for tt in range(NT):
                        norm(n, [tt])
                        evacuate_input(inputs_before(n + 1), TOKENS_FIRST[2 * tt:2 * tt + 2], 2 * tt)
                else:
                    norm(n)
                    if n < last:
                        evacuate_input(inputs_before(n + 1))

            evacuate_input(0)
            for k in range(SLOTS):
                split(k)
            for n, kind in enumerate(phases):
                s0 = first_slab[n]
                if kind == MIXER:
                    def tile_out(tile):
                        what = TILES[tile]
                        if what[0] in QKV:
                            _, blocks, first = QKV[what[0]]
                            act.wait_ge(slab_used, s0 + MIX_SLABS.index((tile, 1)) + 1)
                            for i in range(blocks // 2):
                                at, src = first + 2 * i, pair_of(tile)[i][:].rearrange("p (k m) -> p k m", k=2)
                                queries = min(2, max(0, 4 * BC + BC - at)) if at >= 4 * BC else 0
                                if 0 < queries < 2:
                                    nc.scalar.activation(qk[:, at:at + queries, :], src[:, 0:queries, :], ACT.Copy, scale=HD ** -0.5)
                                    at, src, queries = at + queries, src[:, queries:, :], 0
                                nc.scalar.activation(qk[:, at:first + 2 * i + 2, :], src, ACT.Copy,
                                                     scale=HD ** -0.5 if queries else 1.0).then_inc(pair_read[tile % 2], 1)

                    def sigmoids(tile):
                        what = TILES[tile]
                        if what[0] == "gate" and what[2] == 1:
                            b = what[1]
                            for half in range(2):
                                for tt in range(NT):
                                    g = gates[:, tt, half * 512:(half + 1) * 512]
                                    act.wait_ge(gate_sum, 4 * b + 2 * half + tt + 1)
                                    nc.scalar.activation(g, g, ACT.Sigmoid).then_inc(gated, 1)
                            nc.scalar.preload_act_table_set("natural_log_exp_and_others")

                    def logs_of(u):
                        p, z, k = prob[:, u % 2, :], bank[4 + u % 2][:, 0:BW], 3 * (u - 2 * HEADS)
                        act.wait_ge(scored, u + 1)
                        act.wait_ge(probT_psum, before(u))
                        nc.scalar.activation(p, z, ACT.Abs).then_inc(logs, 1)
                        act.wait_ge(logs, k + 1)
                        nc.scalar.activation(p, p, ACT.Exp, scale=-1.0).then_inc(logs, 1)
                        act.wait_ge(logs, k + 2)
                        nc.scalar.activation(p, p, ACT.Ln, bias=1.0).then_inc(logs, 1)

                    def weights_of(u):
                        b = u // HEADS
                        if b == STICK:
                            p = prob[:, u % 2, :]
                            act.wait_ge(score_read, u + 1)
                            nc.scalar.activation(p, p, ACT.Exp).then_inc(prob_ready, 1)
                            return
                        scale = HD ** -0.5 if b == MOBA else DIFF_SCALE
                        act.wait_ge(neg_ready, u + 1)
                        for m in range(1 if b == MOBA else 2):
                            side = u % 2 if b == MOBA else m
                            for i, at in enumerate((ROWS_A, ROWS_B)):
                                c = 2 * m + i
                                ins = nc.scalar.activation(prob[:, side, at], prob[:, side, at], ACT.Exp, scale=scale,
                                                           bias=head_max[:, u % 2, c:c + 1],
                                                           accum_out=head_sum[:, u % 2, c:c + 1])
                        ins.then_inc(exped, 1)

                    def transposed(u):
                        act.wait_ge(probT_psum, u + 1)
                        if u >= 2:
                            act.wait_ge(o_psum, u - 1)
                        nc.scalar.activation(probT[:, u % 2, :], bank[6][:, 0:BW], ACT.Copy).then_inc(probT_ready, 1)

                    def pair_out(p, src):
                        b = p // BC
                        if b > 0:
                            act.wait_ge(slab_used, s0 + branch_slab(b - 1, 1) + 1)
                        nc.scalar.activation(oT_hi[:, p % BC, :], src, ACT.Copy).then_inc(oT_high, 1)

                    def pair_begins(p):
                        act.wait_ge(o_psum, 2 * p + 2)
                        if p // BC != DIFF:
                            pair_out(p, bank[7][:, 0:S])
                            return
                        k = p - BC
                        act.wait_ge(oT_ready, p)
                        nc.scalar.activation(o_f, bank[7][:, 0:S], ACT.Copy).then_inc(o_copied, 1)
                        act.wait_ge(o_copied, k + 1)
                        nc.scalar.activation(ms_d, o_f, ACT.Square).then_inc(o_square, 1)

                    def pair_roots(p):
                        k = p - BC
                        act.wait_ge(o_spread, k + 1)
                        nc.scalar.activation(o_root, ms_d, ACT.Ln).then_inc(o_log, 1)
                        act.wait_ge(o_log, k + 1)
                        nc.scalar.activation(o_root, o_root, ACT.Exp, scale=-0.5).then_inc(o_rstd, 1)

                    def slabs(i):
                        for d in ROUND[i]:
                            split(s0 + d + 4)

                    def tiles(i, leave):
                        for d in ROUND[i]:
                            if ends(d) is not None:
                                leave(ends(d))

                    for d in ROUND[0]:
                        split(s0 + d + 4)
                        if ends(d) is not None:
                            tile_out(ends(d))
                    nc.scalar.preload_act_table_set("natural_log_exp_and_others")
                    weights_of(0)
                    for u in range(3 * HEADS):
                        delayed = (u - 3) // 2 if u % 2 == 1 and (u - 3) // 2 // BC == DIFF else None
                        tiles(u + 1, tile_out)
                        transposed(u)
                        if 2 * HEADS <= u + 1 < 3 * HEADS:
                            logs_of(u + 1)
                        if u + 1 < 3 * HEADS:
                            weights_of(u + 1)
                        if u % 2 == 0 and u > 0:
                            pair_begins(u // 2 - 1)
                        if delayed is not None:
                            pair_roots(delayed)
                            act.wait_ge(o_normed, delayed - BC + 1)
                            pair_out(delayed, o_f)
                        tiles(u + 1, sigmoids)
                        slabs(u + 1)
                    pair_begins(3 * BC - 1)
                    for d in ROUND[-1]:
                        if ends(d) is not None:
                            sigmoids(ends(d))
                        split(s0 + d + 4)
                    evacuate_input(inputs_before(n) + 1, HALVES_FIRST)
                    for d in range(KC // 2 - 2):
                        split(s0 + 32 + d + 4)
                    boundary(n)
                    for d in range(KC // 2 - 2, KC // 2):
                        split(s0 + 32 + d + 4)
                if kind == CONV:
                    for j in range(6):
                        split(s0 + 2 * j + 4)
                        act.wait_ge(slab_used, s0 + 2 * j + 2)
                        if j < 4:
                            if j >= 2:
                                act.wait_ge(conv_v_ready, j - 1)
                            nc.scalar.activation(conv_c[:, j % 2, :], bank[4 * (j % 2)][:], ACT.Copy).then_inc(conv_c_ready, 1)
                        else:
                            for b in range(2):
                                act.wait_ge(conv_y_ready, 2 * (j - 4) + b + 1)
                                k = 4 * (j - 4) + 2 * b
                                nc.scalar.activation(yT_hi[:, k:k + 2, :], conv_y[:, b, :].rearrange("p (k m) -> p k m", k=2),
                                                     ACT.Copy).then_inc(yT_high, 1)
                        split(s0 + 2 * j + 5)
                    for d in range(KC // 2 - 2):
                        split(s0 + 12 + d + 4)
                    boundary(n)
                    for d in range(KC // 2 - 2, KC // 2):
                        split(s0 + 12 + d + 4)
                if kind == KV:
                    split(s0 + 4)
                    act.wait_ge(xc_zero, 1)
                    nc.scalar.activation(tokens_of(xc_hi)[:, :, GROUPS, 0:32:2], cols[:, POS:POS + 32].rearrange("p (a c) -> p a c", a=2),
                                         ACT.Copy).then_inc(xc_high, 1)
                    act.wait_ge(slab_used, s0 + 2)
                    for kv in range(2):
                        for gp in range(2):
                            src = bank[kv][HD * gp:HD * (gp + 1), :].rearrange("p (b m) -> p b m", b=2)
                            for on in range(2):
                                nc.scalar.activation(tokens_of(xc_hi)[HD * on:HD * (on + 1), kv, gp:GROUPS:2, 0:S - on], src[:, :, on:S],
                                                     ACT.Copy).then_inc(xc_high, 1)
                    split(s0 + 5)

                    def keys_out(slot):
                        k, pair, v = s0 + (2, 8)[slot], ([4, 5], [2, 3])[slot], (v_sel, v_win)[slot]
                        split(k + 4)
                        act.wait_ge(slab_used, k + 2)
                        for tt in range(NT):
                            nc.scalar.activation(key_sq[:, slot, tt, :], bank[pair[tt]][:, 0:S], ACT.Square).then_inc(key_squared, 1)
                        for tt in range(NT):
                            nc.scalar.activation(v[:, tt, :], bank[pair[tt]][:, S:2 * S], ACT.Copy).then_inc(values_ready, 1)

                    keys_out(0)
                    split(s0 + 7)
                    norm(n)
                    for kv in range(2):
                        split(s0 + 8 + 2 * kv)
                        act.wait_ge(slab_used, s0 + 6 + 2 * kv)
                        nc.scalar.activation(hid_row[:, kv, :], bank[6 + kv][0:CMP_ROWS, 0:CMP_HID], ACT.Copy).then_inc(hid_rows, 1)
                        split(s0 + 9 + 2 * kv)
                        act.wait_ge(bias_ready, kv + 1)
                        for hb in range(2):
                            nc.scalar.activation(hid[:, kv, hb, :], hidden_of(kv, hb)[:, 0:GROUPS * 16], ACT.Gelu_apprx_tanh,
                                                 bias=cmp_bias[:, kv, hb:hb + 1]).then_inc(hid_ready, 1)
                    keys_out(1)
                    act.wait_ge(cmp_psum, 1)
                    nc.scalar.activation(kc_sq[:], bank[6][0:GROUPS * 16, 0:HD], ACT.Square, accum_out=kc_ms[:, 0:1]).then_inc(kc_squared, 1)
                    evacuate_input(inputs_before(n + 1))
                    split(s0 + 13)
                if kind == NSA:
                    act.wait_ge(loaded_wg, 16)
                    nc.scalar.activation(wg_hi[:], wg[:], ACT.Copy).then_inc(wg_high, 1)
                    for j in range(2):
                        split(s0 + 2 * j + 4)
                        act.wait_ge(slab_used, s0 + 2 * j + 2)
                        for tt in range(NT):
                            nc.scalar.activation(z_sb[:, tt, 512 * j:512 * (j + 1)], bank[Q_IN[j][tt]][:], ACT.Square).then_inc(q_squared, 1)
                        if j == 0:
                            act.wait_ge(gates_psum, 1)
                            nc.scalar.activation(branch_gate[:].rearrange("p t n -> p (t n)"), bank[2][:, 0:NT * 3 * NQ],
                                                 ACT.Sigmoid).then_inc(branch_gates, 1)
                        split(s0 + 2 * j + 5)

                    def exponentials(w):
                        act.wait_ge(sel_neg, w + 1)
                        if w >= 2:
                            act.wait_ge(selT_psum, w - 1)
                            act.wait_ge(sel_weighed, w - 1)
                        for tt in range(NT):
                            for r in range(PER_GROUP):
                                b, at = score_place(tt, r)
                                ins = nc.scalar.activation(sel_p[:, w % 2, b, at], bank[SCORES[w % 2][b]][:, at], ACT.Exp,
                                                           bias=sel_max[:, w % 2, tt * PER_GROUP + r:tt * PER_GROUP + r + 1],
                                                           accum_out=sel_sum[:, w % 2, tt, r:r + 1])
                        ins.then_inc(sel_exped, 1)

                    def transposed_weights(w):
                        act.wait_ge(selT_psum, w + 1)
                        if w >= 2:
                            act.wait_ge(sel_out, w - 1)
                        for b in range(2):
                            ins = nc.scalar.activation(sel_pT[:, w % 2, b, :], bank[SCORES[w % 2][b]][:], ACT.Copy)
                        ins.then_inc(selT_act, 1)

                    exponentials(0)
                    act.wait_ge(cmp_shifted, 1)
                    nc.scalar.activation(cmp_l, cmp_l, ACT.Exp).then_inc(cmp_exped, 1)
                    for tt in range(NT):
                        act.wait_ge(cmpT_psum, tt + 1)
                        nc.scalar.activation(cmp_pT[:, tt, :, :].rearrange("p g m -> p (g m)"), bank[CMP_OUT[tt]][:], ACT.Copy)\
                            .then_inc(cmpT_ready, 1)
                    transposed_weights(0)
                    for tt in range(NT):
                        act.wait_ge(cmp_out, tt + 1)
                        for half in range(2):
                            nc.scalar.activation(z_sb[:, tt, 512 * half:512 * (half + 1)], bank[CMP_OUT[half]][:], ACT.Copy)\
                                .then_inc(z_started, 1)
                    for w in range(1, UNITS):
                        exponentials(w)
                        transposed_weights(w)
                    evacuate_input(inputs_before(n) + 1, HALVES_FIRST)
                    for d in range(KC // 2 - 2):
                        split(s0 + 4 + d + 4)
                    boundary(n)
                    for d in range(KC // 2 - 2, KC // 2):
                        split(s0 + 4 + d + 4)
                if kind == FFN:
                    f = ffn_number[n]

                    def hidden(j, i=0):
                        act.wait_ge(hT_psum, FT * f + j + 1 + 2 * i)
                        nc.scalar.activation(hT_hi[:, bass.ds(2 * j + 4 * i, 2), :],
                                             bank[4 + j % 2][:].rearrange("p (c m) -> p c m", c=2),
                                             ACT.Copy).then_inc(hT_high, 1)

                    def tile(j, i=0):
                        if not (isinstance(i, int) and j == 0):
                            hidden(j - 1, i)
                        split(s0 + 2 * j + 4, i)
                        act.wait_ge(slab_used, s0 + 2 * j + 2 + 4 * i)
                        for tt in range(NT):
                            if not (isinstance(i, int) and j == 0):
                                act.wait_ge(h_ready, 2 * FT * f + 2 * j - 1 + tt + 4 * i)
                            nc.scalar.activation(silu[:, tt, :], bank[2 * (j % 2) + tt][:, 0:256],
                                                 ACT.Silu).then_inc(silu_ready, 1)
                        split(s0 + 2 * j + 5, i)

                    for j in range(3):
                        tile(j)
                    if n == 0:
                        act.wait_ge(lam_dots, 1)
                        nc.scalar.activation(lam_col[:, 2:4], lam_col[:, 0:2], ACT.Exp).then_inc(lam_exp, 1)
                    with act.Fori(0, (FT - 3) // 2) as i:
                        for j in range(3, 5):
                            tile(j, i)
                    for d in range(FC // 2):
                        if d == 1:
                            hidden(FT - 1)
                        if d < FC // 2 - 2:
                            split(s0 + 2 * FT + d + 4)
                    boundary(n)
                    for d in range(FC // 2 - 2, FC // 2):
                        split(s0 + 2 * FT + d + 4)

        @block.vector
        def _(dve):
            steps = [0]

            def step(ins):
                steps[0] += 1
                ins.then_inc(dve_step, 1)
                dve.wait_ge(dve_step, steps[0])

            def split(k, i=0):
                if k >= TOTAL:
                    return
                slot, width = k % SLOTS, width_of(k)
                dve.wait_ge(high_ready, k + 1 + 4 * i)
                nc.vector.tensor_tensor(w_lo[:, slot, 0:width], raw[:, slot, 0:width],
                                        w_hi[:, slot, 0:width].bitcast(F32), ALU.subtract).then_inc(low_ready, 1)

            def evacuate_input(index, order=TOKENS_FIRST, first=0):
                for place, (tt, q, src) in enumerate(order, first):
                    dve.wait_ge(xT_high, 4 * index + place + 1)
                    nc.vector.tensor_tensor(xT_lo[:, 4 * q:4 * q + 4, tt * P:(tt + 1) * P],
                                            src[:].rearrange("p (k m) -> p k m", k=4),
                                            xT_hi[:, 4 * q:4 * q + 4, tt * P:(tt + 1) * P].bitcast(F32),
                                            ALU.subtract).then_inc(xT_ready, 1)

            def add_output(n, tt, factor, y_at):
                if tt == 0:
                    dve.wait_ge(y_ready, y_layers[n] + 1)
                    if has_ln(n):
                        dve.wait_ge(scaled, ln_uses[n] + 1)
                else:
                    dve.wait_ge(slab_used, y_at)
                for half in range(2):
                    part = x_sb[:, tt, half * 512:(half + 1) * 512]
                    ins = nc.vector.scalar_tensor_tensor(out=part, in0=Y[tt][half][:], scalar=factor, in1=part,
                                                         op0=ALU.mult, op1=ALU.add)
                ins.then_inc(summed, 1)

            def layer_norm(n, tt):
                dve.wait_ge(summed, summed_before(n) + tt + 1)
                for half in range(2):
                    ins = nc.vector.bn_stats(bn[:, tt, half, :], x_sb[:, tt, half * 512:(half + 1) * 512])
                step(ins)
                step(nc.vector.bn_aggr(stats[:, 4 * tt:4 * tt + 2], bn[:, tt, :, :]))
                nc.vector.tensor_scalar(stats[:, 4 * tt + 2:4 * tt + 3], stats[:, 4 * tt + 1:4 * tt + 2], LN_EPS, None,
                                        ALU.add).then_inc(spread, 1)

            def layer_norm_apply(n, tt):
                xt, mean, rstd = x_sb[:, tt, :], stats[:, 4 * tt:4 * tt + 1], stats[:, 4 * tt + 3:4 * tt + 4]
                dve.wait_ge(rstd_ready, norm_index(n, tt, LN) + 1)
                dve.wait_ge(gain_loaded[0], 16 * (ln_uses[n] + 1))
                dve.wait_ge(gain_loaded[1], 16 * (ln_uses[n] + 1))
                step(nc.vector.scalar_tensor_tensor(out=xt, in0=xt, scalar=mean, in1=gain[:, 0, :],
                                                    op0=ALU.subtract, op1=ALU.mult))
                nc.vector.scalar_tensor_tensor(out=xt, in0=xt, scalar=rstd, in1=gain[:, 1, :],
                                               op0=ALU.mult, op1=ALU.add).then_inc(normed, 1)

            def rms_norm(n, tt):
                dve.wait_ge(squared, NT * rms_uses[n] + tt + 1)
                nc.vector.tensor_scalar(stats[:, 10 + 2 * tt:11 + 2 * tt], stats[:, 8 + tt:9 + tt], 1.0 / D, RMS_EPS,
                                        ALU.mult, ALU.add).then_inc(spread, 1)
                dve.wait_ge(rstd_ready, norm_index(n, tt, RMS) + 1)
                dve.wait_ge(gain_loaded[2], 16 * (rms_uses[n] + 1))
                nc.vector.scalar_tensor_tensor(out=z_sb[:, tt, :], in0=x_sb[:, tt, :], scalar=stats[:, 11 + 2 * tt:12 + 2 * tt],
                                               in1=gain[:, 2, :], op0=ALU.mult, op1=ALU.mult).then_inc(normed, 1)

            def boundary(n, factor, y_at):
                if apart(n):
                    add_output(n, 0, factor, y_at)
                    rms_norm(n, 0)
                    add_output(n, 1, factor, y_at)
                    for tt in range(NT):
                        evacuate_input(inputs_before(n + 1), TOKENS_FIRST[2 * tt:2 * tt + 2], 2 * tt)
                        if tt == 0:
                            rms_norm(n, 1)
                    return
                for tt in range(NT):
                    add_output(n, tt, factor, y_at)
                    if has_ln(n):
                        layer_norm(n, tt)
                if has_ln(n):
                    for tt in range(NT):
                        layer_norm_apply(n, tt)
                if has_rms(n):
                    for tt in range(NT):
                        rms_norm(n, tt)
                if n < last:
                    evacuate_input(inputs_before(n + 1))

            evacuate_input(0)
            for k in range(SLOTS):
                split(k)
            def small_parameters():
                dve.wait_ge(cols_psum, 1)
                nc.vector.tensor_copy(cols[:, 0:ROWS], bank[7][:, 0:ROWS]).then_inc(cols_ready, 1)
                dve.wait_ge(cols_ready, 1)
                dve.wait_ge(loaded_lam, 16)
                lf = z_sb[:, 1, 0:P].rearrange("p (a b d) -> p a b d", a=2, b=2)
                dots = z_sb[:, 1, P:P + HD].rearrange("p (a d) -> p a d", a=2)
                step(nc.vector.tensor_tensor(dots, lf[:, :, 0, :], lf[:, :, 1, :], ALU.mult))
                nc.vector.tensor_reduce(lam_col[:, 0:2], dots, AX.X, ALU.add).then_inc(lam_dots, 1)
                dve.wait_ge(lam_exp, 1)
                step(nc.vector.tensor_tensor(lam_col[:, 4:5], lam_col[:, 3:4], lam_col[:, 2:3], ALU.subtract))
                step(nc.vector.tensor_scalar(lam_col[:, 5:6], lam_col[:, 4:5], -LAMBDA_INIT, None, ALU.add))
                step(nc.vector.tensor_scalar(lam_col[:, 6:7], cols[:, SUBLN:SUBLN + 1], 1.0 - LAMBDA_INIT, None, ALU.mult))

            minus_lam, out_gain = lam_col[:, 5:6], lam_col[:, 6:7]
            for n, kind in enumerate(phases):
                s0 = first_slab[n]
                if kind == MIXER:
                    def tile_out(tile):
                        what, src = TILES[tile], pair_of(tile)
                        if what[0] == "k, v of sb":
                            dve.wait_ge(slab_used, s0 + MIX_SLABS.index((tile, 1)) + 1)
                            nc.vector.tensor_copy(v_mix[:, :, 2 * BW:2 * BW + 256], src[1][:].rearrange("p (t n) -> p t n", t=NT))\
                                .then_inc(pair_read[tile % 2], 1)
                        elif what[0] in QKV and QKV[what[0]][1] == 0:
                            dve.wait_ge(slab_used, s0 + MIX_SLABS.index((tile, 1)) + 1)
                            for tt in range(NT):
                                if what[0] == "v of moba, sb":
                                    nc.vector.tensor_copy(v_mix[:, tt, 2 * BW + 256:3 * BW], src[tt][:, BW:512])
                                c0 = 0 if what[0] == "v of moba, sb" else BW
                                nc.vector.tensor_copy(v_mix[:, tt, c0:c0 + BW], src[tt][:, 0:BW]).then_inc(pair_read[tile % 2], 1)
                        elif what[0] == "gate":
                            _, b, half = what
                            at = slice(half * 512, (half + 1) * 512)
                            dve.wait_ge(loaded_mix, 16)
                            dve.wait_ge(slab_used, s0 + MIX_SLABS.index((tile, 1)) + 1)
                            if b > 0:
                                dve.wait_ge(merged, 4 * b)
                            for tt in range(NT):
                                nc.vector.tensor_tensor(gates[:, tt, at], src[tt][:], b_gate[:, b, at], ALU.add).then_inc(gate_sum, 1)
                            dve.wait_ge(gate_sum, 4 * b + 2 * half + 2)
                            nc.vector.engine_nop().then_inc(pair_read[tile % 2], 2)
                        elif what[0] == "branch":
                            _, b, half = what
                            at = slice(half * 512, (half + 1) * 512)
                            dve.wait_ge(slab_used, s0 + branch_slab(b, half) + 1)
                            for tt in range(NT):
                                dve.wait_ge(gated, 4 * b + 2 * half + tt + 1)
                                y = z_sb[:, tt, at]
                                if b == MOBA:
                                    nc.vector.tensor_tensor(y, gates[:, tt, at], src[tt][:], ALU.mult).then_inc(merged, 1)
                                elif b == DIFF:
                                    nc.vector.tensor_tensor(gates[:, tt, at], gates[:, tt, at], src[tt][:], ALU.mult).then_inc(multiplied, 1)
                                else:
                                    dve.wait_ge(merged, 8)
                                    step(nc.vector.tensor_tensor(gates[:, tt, at], gates[:, tt, at], src[tt][:], ALU.mult))
                                    nc.vector.tensor_tensor(y, y, gates[:, tt, at], ALU.add).then_inc(merged, 1)
                            if b == DIFF:
                                dve.wait_ge(multiplied, 2 * half + 2)
                            else:
                                dve.wait_ge(merged, 4 * b + 2 * half + 2)
                            nc.vector.engine_nop().then_inc(pair_read[tile % 2], 2)

                    def maxima_of(u):
                        b, hd = u // HEADS, u % HEADS
                        dve.wait_ge(scored, u + 1)
                        if before(u) > 0:
                            dve.wait_ge(probT_psum, before(u))
                        scale = HD ** -0.5 if b == MOBA else DIFF_SCALE
                        slope = alibi_slope(2 * hd if b == MOBA else 2 * hd + 1)
                        maps = 1 if b == MOBA else 2
                        for m in range(maps):
                            side = u % 2 if b == MOBA else m
                            ins = nc.vector.scalar_tensor_tensor(out=prob[:, side, :], in0=far[:], scalar=slope / scale,
                                                                 in1=bank[4 + side][:, 0:BW], op0=ALU.mult, op1=ALU.add)
                        ins.then_inc(score_read, 1)
                        dve.wait_ge(score_read, u + 1)
                        mx = head_max[:, u % 2, 0:2 * maps]
                        for m in range(maps):
                            side = u % 2 if b == MOBA else m
                            for i, at in enumerate((ROWS_A, ROWS_B)):
                                ins = nc.vector.tensor_reduce(head_max[:, u % 2, 2 * m + i:2 * m + i + 1], prob[:, side, at], AX.X, ALU.max)
                        step(ins)
                        nc.vector.tensor_scalar(mx, mx, -scale, None, ALU.mult).then_inc(neg_ready, 1)

                    def weights_of(u):
                        b = u // HEADS
                        if b == STICK:
                            p, z = prob[:, u % 2, :], bank[4 + u % 2][:, 0:BW]
                            dve.wait_ge(logs, 3 * (u - 2 * HEADS) + 3)
                            soft = tmp[:, 0:BW]
                            step(nc.vector.scalar_tensor_tensor(out=soft, in0=z, scalar=0.0, in1=p, op0=ALU.max, op1=ALU.add))
                            for at in (ROWS_A, ROWS_B):
                                part, to = soft[:, at], stick[:, at]
                                ins = nc.vector.tensor_tensor_scan(to[:, ::-1], part[:, ::-1], part[:, ::-1], 0.0, ALU.add, ALU.max)
                            step(ins)
                            nc.vector.tensor_tensor(p, z, stick[:], ALU.subtract).then_inc(score_read, 1)
                            dve.wait_ge(score_read, u + 1)
                            return
                        sm = head_sum[:, u % 2, 0:2 if b == MOBA else 4]
                        dve.wait_ge(exped, u + 1)
                        step(nc.vector.reciprocal(sm, sm))
                        if b == DIFF:
                            step(nc.vector.tensor_scalar(sm[:, 2:4], sm[:, 2:4], minus_lam, None, ALU.mult))
                        side = u % 2 if b == MOBA else 0
                        for i, at in enumerate((ROWS_A, ROWS_B)):
                            ins = nc.vector.tensor_scalar(prob[:, side, at], prob[:, side, at], sm[:, i:i + 1], None, ALU.mult)
                        if b == DIFF:
                            step(ins)
                            for i, at in enumerate((ROWS_A, ROWS_B)):
                                ins = nc.vector.scalar_tensor_tensor(out=prob[:, 0, at], in0=prob[:, 1, at], scalar=sm[:, 2 + i:3 + i],
                                                                     in1=prob[:, 0, at], op0=ALU.mult, op1=ALU.add)
                        ins.then_inc(prob_ready, 1)
                        dve.wait_ge(prob_ready, u + 1)

                    def pair_spread(p):
                        dve.wait_ge(o_sums, p - BC + 1)
                        nc.vector.tensor_scalar(ms_d, bank[7][:, S:2 * S], 1.0 / HD, SUBLN_EPS, ALU.mult, ALU.add).then_inc(o_spread, 1)

                    def pair_norm(p):
                        near_one = tmp[:, 0:S]
                        dve.wait_ge(o_rstd, p - BC + 1)
                        step(nc.vector.tensor_tensor(near_one, o_root, o_root, ALU.mult))
                        step(nc.vector.tensor_tensor(near_one, near_one, ms_d, ALU.mult))
                        step(nc.vector.tensor_scalar(near_one, near_one, -0.5, 1.5, ALU.mult, ALU.add))
                        step(nc.vector.tensor_tensor(near_one, near_one, o_root, ALU.mult))
                        nc.vector.scalar_tensor_tensor(out=o_f, in0=o_f, scalar=out_gain, in1=near_one,
                                                       op0=ALU.mult, op1=ALU.mult).then_inc(o_normed, 1)

                    def pair_out(p, src):
                        dve.wait_ge(oT_high, p + 1)
                        nc.vector.tensor_tensor(oT_lo[:, p % BC, :], src, oT_hi[:, p % BC, :].bitcast(F32), ALU.subtract)\
                            .then_inc(oT_ready, 1)

                    def tiles(i):
                        for d in ROUND[i]:
                            if ends(d) is not None:
                                tile_out(ends(d))

                    for d in ROUND[0]:
                        split(s0 + d + 4)
                        if ends(d) is not None:
                            tile_out(ends(d))
                    dve.wait_ge(far_ready, 1)
                    maxima_of(0)
                    weights_of(0)
                    for u in range(3 * HEADS):
                        delayed = (u - 3) // 2 if u % 2 == 1 and (u - 3) // 2 // BC == DIFF else None
                        tiles(u + 1)
                        if delayed is not None:
                            pair_spread(delayed)
                        if u + 1 < 2 * HEADS:
                            maxima_of(u + 1)
                        if u + 1 < 3 * HEADS:
                            weights_of(u + 1)
                        if u % 2 == 0 and u > 0 and (u // 2 - 1) // BC != DIFF:
                            pair_out(u // 2 - 1, bank[7][:, 0:S])
                        if delayed is not None:
                            pair_norm(delayed)
                            pair_out(delayed, o_f)
                    pair_out(3 * BC - 1, bank[7][:, 0:S])
                    for d in ROUND[-1]:
                        if ends(d) is not None:
                            tile_out(ends(d))
                    evacuate_input(inputs_before(n) + 1, HALVES_FIRST)
                    dve.wait_ge(low_ready, s0 + 36)
                    for d in range(KC // 2 - 2):
                        split(s0 + 32 + d + 4)
                    boundary(n, 1.0, s0 + 36)
                    for d in range(KC // 2 - 2, KC // 2):
                        split(s0 + 32 + d + 4)
                if kind == CONV:
                    nc.vector.memset(conv_v[:, :, 0:2], 0.0)
                    for j in range(6):
                        split(s0 + 2 * j + 4)
                        if j < 4:
                            dve.wait_ge(conv_c_ready, j + 1)
                            nc.vector.tensor_tensor(conv_v[:, 2 * j:2 * j + 2, 2:S + 2],
                                                    conv_c[:, j % 2, :].rearrange("p (k m) -> p k m", k=2),
                                                    bank[4 * (j % 2) + 1][:].rearrange("p (k m) -> p k m", k=2),
                                                    ALU.mult).then_inc(conv_v_ready, 1)
                            dve.wait_ge(conv_v_ready, j + 1)
                            for k in (2 * j, 2 * j + 1):
                                a = conv_a[:, k, :]
                                w = [cols[:, CONV_W + tap * KC + k:CONV_W + tap * KC + k + 1] for tap in range(3)]
                                step(nc.vector.tensor_scalar(a, conv_v[:, k, 2:S + 2], w[2], None, ALU.mult))
                                for tap in (1, 0):
                                    step(nc.vector.scalar_tensor_tensor(out=a, in0=conv_v[:, k, tap:tap + S], scalar=w[tap],
                                                                        in1=a, op0=ALU.mult, op1=ALU.add))
                        else:
                            dve.wait_ge(slab_used, s0 + 2 * j + 2)
                            for b in range(2):
                                k, done = 4 * (j - 4) + 2 * b, 2 * (j - 4) + b + 1
                                if j == 5:
                                    dve.wait_ge(yT_ready, done - 2)
                                nc.vector.tensor_tensor(conv_y[:, b, :], bank[4 * (j % 2) + b][:],
                                                        conv_a[:, k:k + 2, :].rearrange("p k m -> p (k m)"),
                                                        ALU.mult).then_inc(conv_y_ready, 1)
                            for b in range(2):
                                k, done = 4 * (j - 4) + 2 * b, 2 * (j - 4) + b + 1
                                dve.wait_ge(yT_high, done)
                                nc.vector.tensor_tensor(yT_lo[:, k:k + 2, :], conv_y[:, b, :].rearrange("p (k m) -> p k m", k=2),
                                                        yT_hi[:, k:k + 2, :].bitcast(F32), ALU.subtract).then_inc(yT_ready, 1)
                        split(s0 + 2 * j + 5)
                    for d in range(KC // 2 - 2):
                        split(s0 + 12 + d + 4)
                    boundary(n, 1.0, s0 + 16)
                    for d in range(KC // 2 - 2, KC // 2):
                        split(s0 + 12 + d + 4)
                if kind == KV:
                    zero = ident[:].rearrange("p (a g t) -> p a g t", a=2, g=GROUPS)
                    for x in (xc_hi, xc_lo):
                        last_token = tokens_of(x)[HD:P, :, 0:GROUPS, S - 1:S]
                        nc.vector.tensor_tensor(last_token, zero[HD:P, :, :, 0:1], zero[HD:P, :, :, 0:1], ALU.subtract)
                        for kv in range(2):
                            ins = nc.vector.tensor_tensor(x[:, kv, GROUPS * S:], x_sb[:, 0, 0:XC - GROUPS * S], x_sb[:, 0, 0:XC - GROUPS * S],
                                                          ALU.subtract)
                    step(ins)
                    nc.vector.engine_nop().then_inc(xc_zero, 1)
                    step(nc.vector.memset(v_cmp[:], 0.0))
                    step(nc.vector.memset(hid_v[:], 0.0))
                    split(s0 + 4)
                    dve.wait_ge(xc_high, 1)
                    nc.vector.tensor_tensor(tokens_of(xc_lo)[:, :, GROUPS, 0:32:2], cols[:, POS:POS + 32].rearrange("p (a c) -> p a c", a=2),
                                            tokens_of(xc_hi)[:, :, GROUPS, 0:32:2].bitcast(F32), ALU.subtract).then_inc(xc_ready, 1)
                    for kv in range(2):
                        dve.wait_ge(xc_high, 1 + 4 * (kv + 1))
                        for gp in range(2):
                            src = bank[kv][HD * gp:HD * (gp + 1), :].rearrange("p (b m) -> p b m", b=2)
                            for on in range(2):
                                part = slice(HD * on, HD * (on + 1))
                                nc.vector.tensor_tensor(tokens_of(xc_lo)[part, kv, gp:GROUPS:2, 0:S - on], src[:, :, on:S],
                                                        tokens_of(xc_hi)[part, kv, gp:GROUPS:2, 0:S - on].bitcast(F32), ALU.subtract).then_inc(xc_ready, 1)
                    split(s0 + 5)

                    def keys_spread(slot):
                        dve.wait_ge(key_squared, NT * (slot + 1))
                        ms = key_ms[:, slot, 0, :]
                        step(nc.vector.tensor_reduce(ms, key_sq[:, slot, :, :].rearrange("p t (g d) -> p (t g) d", g=GROUPS), AX.X, ALU.add))
                        nc.vector.tensor_scalar(ms, ms, 1.0 / HD, RMS_EPS, ALU.mult, ALU.add).then_inc(key_spread, 1)

                    def keys_norm(slot):
                        dve.wait_ge(key_rstd, slot + 1)
                        dve.wait_ge(values_ready, NT * (slot + 1))
                        for tt in range(NT):
                            each = key_ms[:, slot, 1, tt * GROUPS:(tt + 1) * GROUPS].unsqueeze(2).to_broadcast([P, GROUPS, HD])
                            src = bank[([4, 5], [2, 3])[slot][tt]][:, 0:S]
                            ins = nc.vector.tensor_tensor(key_n[:, slot, tt, :].rearrange("p (g d) -> p g d", g=GROUPS),
                                                          src.rearrange("p (g d) -> p g d", g=GROUPS), each, ALU.mult)
                        ins.then_inc(key_normed, 1)

                    split(s0 + 6)
                    keys_spread(0)
                    keys_norm(0)
                    split(s0 + 7)
                    for tt in range(NT):
                        rms_norm(n, tt)
                    for kv in range(2):
                        split(s0 + 8 + 2 * kv)
                        split(s0 + 9 + 2 * kv)
                        dve.wait_ge(hidT_psum, kv + 1)
                        for hb in range(2):
                            c0 = CMP_B + 2 * kv + hb
                            ins = nc.vector.tensor_tensor(cmp_bias[:, kv, hb:hb + 1], hidden_of(kv, hb)[:, GROUPS * 16:GROUPS * 16 + 1],
                                                          cols[:, c0:c0 + 1], ALU.add)
                        ins.then_inc(bias_ready, 1)
                    dve.wait_ge(hid_ready, 4)
                    for hb in range(2):
                        for r in range(PER_GROUP):
                            ins = nc.vector.tensor_copy(hid_v[:, hb, :, r, 0:16], hid[:, 1, hb, :].rearrange("p (g n) -> p g n", g=GROUPS))
                    ins.then_inc(hid_v_ready, 1)
                    split(s0 + 12)
                    keys_spread(1)
                    dve.wait_ge(kc_squared, 1)
                    nc.vector.tensor_scalar(kc_ms[:, 1:2], kc_ms[:, 0:1], 1.0 / HD, RMS_EPS, ALU.mult, ALU.add).then_inc(kc_spread, 1)
                    evacuate_input(inputs_before(n + 1), TOKENS_FIRST[0:2])
                    keys_norm(1)
                    dve.wait_ge(cmp_psum, 2)
                    for r in range(PER_GROUP):
                        part = slice(32 * r, 32 * (r + 1))
                        ins = nc.vector.tensor_copy(v_cmp[part, :, HD * r:HD * (r + 1)], bank[7][part, 0:S].rearrange("p (g d) -> p g d", g=GROUPS))
                    ins.then_inc(cmp_ready, 1)
                    dve.wait_ge(kc_rstd, 1)
                    for twice in range(2):
                        ins = nc.vector.tensor_scalar(kc_n[:, twice * HD:(twice + 1) * HD], bank[6][0:GROUPS * 16, 0:HD], kc_ms[:, 2:3], None, ALU.mult)
                    ins.then_inc(kc_normed, 1)
                    evacuate_input(inputs_before(n + 1), TOKENS_FIRST[2:4], 2)
                    split(s0 + 13)
                if kind == NSA:
                    dve.wait_ge(wg_high, 1)
                    nc.vector.tensor_tensor(wg_lo[:], wg[:], wg_hi[:].bitcast(F32), ALU.subtract).then_inc(wg_ready, 1)
                    def queries_spread(j):
                        dve.wait_ge(q_squared, NT * (j + 1))
                        ms = q_ms[:, j, 0, :]
                        squares = z_sb[:, :, 512 * j:512 * (j + 1)].rearrange("p t (h d) -> p t h d", h=8)
                        step(nc.vector.tensor_reduce(ms.rearrange("p (t h) -> p t h", t=NT), squares, AX.X, ALU.add))
                        nc.vector.tensor_scalar(ms, ms, 1.0 / HD, RMS_EPS, ALU.mult, ALU.add).then_inc(q_spread, 1)

                    def queries_norm(j):
                        dve.wait_ge(q_rstd, j + 1)
                        for tt in range(NT):
                            for gp in range(2):
                                at = 256 * gp
                                each = q_ms[:, j, 1, 8 * tt + 4 * gp:8 * tt + 4 * gp + 4].unsqueeze(2).to_broadcast([P, PER_GROUP, HD])
                                ins = nc.vector.tensor_tensor(q_n[:, tt, j, :].rearrange("p (r g d) -> p r g d", r=PER_GROUP, g=2)[:, :, gp, :],
                                                              bank[Q_IN[j][tt]][:, at:at + 256].rearrange("p (r d) -> p r d", r=PER_GROUP),
                                                              each, ALU.mult)
                        ins.then_inc(q_normed, 1)

                    def queries_out(j):
                        for rp in range(2):
                            dve.wait_ge(qT_psum, 2 * j + rp + 1)
                            nc.vector.tensor_scalar(qT[:, j, 2 * rp:2 * rp + 2, :].rearrange("p r m -> p (r m)"), bank[Q_T[j][rp]][:],
                                                    cols[:, Q_NORM:Q_NORM + 1], HD ** -0.5, ALU.mult, ALU.mult).then_inc(qT_ready, 1)

                    split(s0 + 4)
                    queries_spread(0)
                    queries_norm(0)
                    split(s0 + 5)
                    split(s0 + 6)
                    queries_out(0)
                    queries_spread(1)
                    queries_norm(1)

                    def per_query(x):
                        return x[:].unsqueeze(2).to_broadcast([P, NT, NQ, 16])

                    def per_head(x):
                        return x.unsqueeze(3).to_broadcast([P, NT, NQ, 16])

                    def row_maxima(w):
                        dve.wait_ge(sel_scored, w + 1)
                        if w >= 2:
                            dve.wait_ge(sel_exped, w - 1)
                        for b in range(3):
                            heads = 4 if b == 0 else 2
                            to = sel_max[:, w % 2, 0:4] if b == 0 else sel_max[:, w % 2, 2 + 2 * b:4 + 2 * b]
                            ins = nc.vector.tensor_reduce(to, bank[SCORES[w % 2][b]][:].rearrange("p (r m) -> p r m", r=heads), AX.X, ALU.max)
                        step(ins)
                        nc.vector.tensor_scalar(sel_max[:, w % 2, :], sel_max[:, w % 2, :], -1.0, None, ALU.mult).then_inc(sel_neg, 1)

                    def transposed_weights(w):
                        dve.wait_ge(selT_psum, w + 1)
                        if w >= 2:
                            dve.wait_ge(sel_out, w - 1)
                        nc.vector.tensor_copy(sel_pT[:, w % 2, 2, :], bank[SCORES[w % 2][2]][:]).then_inc(selT_dve, 1)

                    def weigh(w):
                        g, branch = w // 2, 1 + w % 2
                        dve.wait_ge(sel_exped, w + 1)
                        step(nc.vector.reciprocal(sel_sum[:, w % 2, :, :], sel_sum[:, w % 2, :, :]))
                        gate = branch_gate[:].rearrange("p t (h c) -> p t h c", c=3)[:, :, PER_GROUP * g:PER_GROUP * (g + 1), branch]
                        nc.vector.tensor_tensor(sel_coef[:, w % 2, :, :], sel_sum[:, w % 2, :, :], gate, ALU.mult).then_inc(sel_weighed, 1)

                    def add_unit(w):
                        g = w // 2
                        dve.wait_ge(sel_weighed, w + 1)
                        dve.wait_ge(sel_out, w + 1)
                        each = sel_coef[:, w % 2, :, :].rearrange("p t r -> p (t r)").unsqueeze(2).to_broadcast([P, NT * PER_GROUP, HD])
                        step(nc.vector.tensor_tensor(sel_add[:].rearrange("p (r d) -> p r d", d=HD),
                                                     bank[6 + w % 2][:].rearrange("p (r d) -> p r d", d=HD), each, ALU.mult))
                        zg = z_sb[:, :, 256 * g:256 * (g + 1)]
                        nc.vector.tensor_tensor(zg, zg, sel_add[:].rearrange("p (t n) -> p t n", t=NT), ALU.add).then_inc(attended, 1)
                        dve.wait_ge(attended, w + 1)

                    row_maxima(0)
                    queries_out(1)
                    split(s0 + 7)
                    dve.wait_ge(cmp_masks, 1)
                    dve.wait_ge(cmp_scored, 1)
                    top, total = cmp_row[:, 0, :, :], cmp_row[:, 1, :, :]
                    for gp in range(2):
                        for tt in range(NT):
                            o = cmp_l[:, tt, :, :].rearrange("p (j g r) n -> p j g r n", j=2, g=2)[:, :, gp, :, :]
                            mask = cmp_mask[:, tt, :].unsqueeze(1).unsqueeze(1).to_broadcast([P, 2, PER_GROUP, 16])
                            ins = nc.vector.tensor_tensor(o, bank[6 + gp][:, tt * P:(tt + 1) * P].rearrange("p (j r n) -> p j r n", j=2, r=PER_GROUP),
                                                          mask, ALU.add)
                    step(ins)
                    step(nc.vector.tensor_reduce(top, cmp_l, AX.X, ALU.max))
                    nc.vector.tensor_tensor(cmp_l, cmp_l, per_head(top), ALU.subtract).then_inc(cmp_shifted, 1)
                    dve.wait_ge(cmp_exped, 1)
                    step(nc.vector.tensor_reduce(total, cmp_l, AX.X, ALU.add))
                    step(nc.vector.reciprocal(total, total))
                    dve.wait_ge(branch_gates, 1)
                    gate = branch_gate[:].rearrange("p t (h c) -> p t h c", c=3)[:, :, :, 0]
                    step(nc.vector.tensor_tensor(total, total, gate, ALU.mult))
                    step(nc.vector.tensor_tensor(cmp_l, cmp_l, per_query(cmp_valid), ALU.mult))
                    nc.vector.tensor_tensor(cmp_p[:, :, :, 0:16], cmp_l, per_head(total), ALU.mult).then_inc(cmp_weighted, 1)
                    row_maxima(1)
                    for w in range(UNITS):
                        transposed_weights(w)
                        weigh(w)
                        if w == 1:
                            dve.wait_ge(z_started, 2 * NT)
                        if w > 0:
                            add_unit(w - 1)
                        if w + 2 < UNITS:
                            row_maxima(w + 2)
                    evacuate_input(inputs_before(n) + 1, HALVES_FIRST[0:2])
                    add_unit(UNITS - 1)
                    evacuate_input(inputs_before(n) + 1, HALVES_FIRST[2:4], 2)
                    for d in range(KC // 2 - 2):
                        split(s0 + 4 + d + 4)
                    boundary(n, 1.0, s0 + 8)
                    for d in range(KC // 2 - 2, KC // 2):
                        split(s0 + 4 + d + 4)
                if kind == FFN:
                    f = ffn_number[n]

                    def hidden(j, i=0):
                        dve.wait_ge(hT_high, FT * f + j + 1 + 2 * i)
                        nc.vector.tensor_tensor(hT_lo[:, bass.ds(2 * j + 4 * i, 2), :],
                                                bank[4 + j % 2][:].rearrange("p (c m) -> p c m", c=2),
                                                hT_hi[:, bass.ds(2 * j + 4 * i, 2), :].bitcast(F32),
                                                ALU.subtract).then_inc(hT_ready, 1)

                    def tile(j, i=0):
                        if not (isinstance(i, int) and j == 0):
                            hidden(j - 1, i)
                        split(s0 + 2 * j + 4, i)
                        for tt in range(NT):
                            dve.wait_ge(silu_ready, 2 * FT * f + 2 * j + tt + 1 + 4 * i)
                            nc.vector.tensor_tensor(h[:, tt, :], silu[:, tt, :], bank[2 * (j % 2) + tt][:, 256:512],
                                                    ALU.mult).then_inc(h_ready, 1)
                        split(s0 + 2 * j + 5, i)

                    def keys_out(slot, b):
                        dve.wait_ge(keyT_psum, slot + 1)
                        nc.vector.tensor_scalar((k_sel, k_win)[slot][:].rearrange("p b m -> p (b m)"), bank[b][:],
                                                cols[:, K_NORM + 1 + slot:K_NORM + 2 + slot], None, ALU.mult).then_inc(keys_ready, 1)

                    for j in range(3):
                        tile(j)
                        if behind_kv(n) and j == 1:
                            dve.wait_ge(kcT_psum, 1)
                            nc.vector.tensor_scalar(k_cmp[:], bank[6][:, P:P + GROUPS * 16], cols[:, K_NORM:K_NORM + 1], None,
                                                    ALU.mult).then_inc(cmp_ready, 1)
                            keys_out(0, 7)
                        if behind_kv(n) and j == 2:
                            keys_out(1, 6)
                    if n == 0:
                        small_parameters()
                    with dve.Fori(0, (FT - 3) // 2) as i:
                        for j in range(3, 5):
                            tile(j, i)
                    for d in range(FC // 2):
                        if d == 1:
                            hidden(FT - 1)
                        if d < FC // 2 - 2:
                            split(s0 + 2 * FT + d + 4)
                    boundary(n, 0.5, s0 + 33)
                    for d in range(FC // 2 - 2, FC // 2):
                        split(s0 + 2 * FT + d + 4)

        @block.tensor
        def _(pe):
            def product(o, x_hi, x_lo, wh, wl, first, last_one, shared=False):
                nc.tensor.matmul(o, x_lo, wh, start=first, stop=False, skip_group_check=shared)
                nc.tensor.matmul(o, x_hi, wl, start=False, stop=False, skip_group_check=shared)
                return nc.tensor.matmul(o, x_hi, wh, start=False, stop=last_one, skip_group_check=shared)

            def transpose_input(src, places):
                for tt, q, dst in places:
                    for c in range(4):
                        k = 4 * q + c
                        ins = nc.tensor.transpose(dst[:, c * P:(c + 1) * P], src[:, tt, k * P:(k + 1) * P], ident[:])
                    ins.then_inc(xT_psum, 1)

            def next_input(n, tt):
                if n == 0:
                    pe.wait_ge(loaded_x[tt], 16)
                else:
                    pe.wait_ge(normed, last_norm(n - 1, tt))
                transpose_input(operand(n), TOKENS_FIRST[2 * tt:2 * tt + 2])

            def slab_view(slot, chunks, width):
                hi = w_hi[:, slot, 0:chunks * width].rearrange("p (k n) -> p k n", k=chunks)
                lo = w_lo[:, slot, 0:chunks * width].rearrange("p (k n) -> p k n", k=chunks)
                return hi, lo

            def project_slab(k, d, slabs, lhs_hi, lhs_lo, second_free=None):
                pe.wait_ge(low_ready, k + 1)
                hi, lo = slab_view(k % SLOTS, 2, D)
                last_slab = d == slabs - 1
                apart = last_slab or second_free is not None
                order = [(c, tt) for tt in range(NT) for c in range(2)] if apart else [(c, tt) for c in range(2) for tt in range(NT)]
                for c, tt in order:
                    if second_free is not None and (c, tt) == (0, 1):
                        second_free()
                    for half in range(2):
                        at = slice(half * 512, (half + 1) * 512)
                        toks = slice(tt * P, (tt + 1) * P)
                        ins = product(Y[tt][half][:], lhs_hi[:, 2 * d + c, toks], lhs_lo[:, 2 * d + c, toks],
                                      hi[:, c, at], lo[:, c, at], d == 0 and c == 0, last_slab and c == 1)
                    if last_slab and c == 1 and tt == 0:
                        ins.then_inc(y_ready, 1)
                ins.then_inc(slab_used, 1)

            def feature_slab(k, kh, banks, blocks):
                pe.wait_ge(low_ready, k + 1)
                hi, lo = slab_view(k % SLOTS, 4, 512)
                for c in range(4):
                    for fb in range(blocks):
                        at = slice(fb * P, (fb + 1) * P)
                        ins = product(banks[fb // 2][:, (fb % 2) * S:(fb % 2 + 1) * S], hi[:, c, at], lo[:, c, at],
                                      xT_hi[:, 4 * kh + c, :], xT_lo[:, 4 * kh + c, :],
                                      kh == 0 and c == 0 and fb % 2 == 0, kh == 1 and c == 3, shared=True)
                return ins

            def token_slab(k, kh, width, at, dst, shared=False):
                pe.wait_ge(low_ready, k + 1)
                hi, lo = slab_view(k % SLOTS, 4, width)
                for c in range(4):
                    for tt in range(NT):
                        toks = slice(tt * P, (tt + 1) * P)
                        ins = product(dst(tt), xT_hi[:, 4 * kh + c, toks], xT_lo[:, 4 * kh + c, toks], hi[:, c, at], lo[:, c, at],
                                      kh == 0 and c == 0 and not (shared and tt), kh == 1 and c == 3, shared=shared)
                return ins

            pe.wait_ge(consts, 1)
            for tt in range(NT):
                next_input(0, tt)
            for n, kind in enumerate(phases):
                s0 = first_slab[n]
                if kind != FFN:
                    pe.wait_ge(xT_ready, 4 * (inputs_before(n) + 1))
                if kind == FFN:
                    f = ffn_number[n]

                    def gate_up(j, kh, i=0, tiles=range(NT)):
                        k = s0 + 2 * j + kh
                        pe.wait_ge(low_ready, k + 1 + 4 * i)
                        hi, lo = slab_view(k % SLOTS, 4, 512)
                        for c in range(4):
                            for tt in tiles:
                                toks = slice(tt * P, (tt + 1) * P)
                                ins = product(bank[2 * (j % 2) + tt][:], xT_hi[:, 4 * kh + c, toks], xT_lo[:, 4 * kh + c, toks],
                                              hi[:, c, :], lo[:, c, :], kh == 0 and c == 0, kh == 1 and c == 3)
                        if NT - 1 in tiles:
                            ins.then_inc(slab_used, 1)

                    def hidden(j, i=0, free=True):
                        pe.wait_ge(h_ready, 2 * FT * f + 2 * j + 2 + 4 * i)
                        if j >= 2:
                            pe.wait_ge(hT_ready, FT * f + j - 1 + 2 * i)
                        dst = bank[4 + j % 2][:].rearrange("p (c m) -> p c m", c=2)
                        for c in range(2):
                            for tt in range(NT):
                                ins = nc.tensor.transpose(dst[:, c, tt * P:(tt + 1) * P], h[:, tt, c * P:(c + 1) * P], ident[:])
                        ins.then_inc(hT_psum, 1)

                    def tile(j, i=0):
                        gate_up(j, 0, i)
                        hidden(j - 1, i)
                        gate_up(j, 1, i)

                    for tt in range(NT):
                        for kh in range(2):
                            pe.wait_ge(xT_ready, 4 * inputs_before(n) + 2 * tt + kh + 1)
                            gate_up(0, kh, tiles=[tt])
                            if tt == 0 and kh == 0 and n > 0:
                                next_input(n, 1)
                    def transpose_keys(slot, b):
                        for blk in range(2):
                            for tt in range(NT):
                                o = bank[b][:, blk * S + tt * P:blk * S + (tt + 1) * P]
                                ins = nc.tensor.transpose(o, key_n[:, slot, tt, blk * P:(blk + 1) * P], ident[:])
                        ins.then_inc(keyT_psum, 1)

                    for j in range(1, 3):
                        if behind_kv(n) and j == 1:
                            pe.wait_ge(key_normed, 2)
                        tile(j)
                        if behind_kv(n) and j == 1:
                            pe.wait_ge(kc_normed, 1)
                            nc.tensor.transpose(bank[6][:, P:P + GROUPS * 16], kc_n[:], ident[0:GROUPS * 16, 0:GROUPS * 16]).then_inc(kcT_psum, 1)
                            pe.wait_ge(cmp_ready, 1)
                            transpose_keys(0, 7)
                        if behind_kv(n) and j == 2:
                            pe.wait_ge(cmp_ready, 2)
                            transpose_keys(1, 6)
                    if n == 0:
                        pe.wait_ge(loaded_rows, 16 * 9)
                        nc.tensor.transpose(bank[7][:, 0:ROWS], z_sb[0:ROWS, 0, 0:P], ident[0:ROWS, 0:ROWS]).then_inc(cols_psum, 1)
                    with pe.Fori(0, (FT - 3) // 2) as i:
                        for j in range(3, 5):
                            tile(j, i)
                    if n == 0:
                        pe.wait_ge(cols_ready, 1)
                    if behind_kv(n):
                        pe.wait_ge(keys_ready, 2)
                    for d in range(FC // 2):
                        pe.wait_ge(hT_ready, FT * f + d + 1)
                        project_slab(s0 + 2 * FT + d, d, FC // 2, hT_hi, hT_lo)
                        if d == 0:
                            hidden(FT - 1)
                if kind == MIXER:
                    def slab(d):
                        tile, kh = MIX_SLABS[d]
                        what, k, banks = TILES[tile], s0 + d, pair_of(tile)
                        if kh == 0 and tile >= 2:
                            pe.wait_ge(pair_read[tile % 2], pair_reads(tile))
                        if what[0] == "gate":
                            ins = token_slab(k, kh, 512, slice(0, 512), lambda tt: banks[tt][:])
                        elif what[0] == "branch":
                            pe.wait_ge(oT_ready, BC * (what[1] + 1))
                            pe.wait_ge(low_ready, k + 1)
                            hi, lo = slab_view(k % SLOTS, BC, 512)
                            for c in range(BC):
                                for tt in range(NT):
                                    toks = slice(tt * P, (tt + 1) * P)
                                    ins = product(banks[tt][:], oT_hi[:, c, toks], oT_lo[:, c, toks], hi[:, c, :], lo[:, c, :],
                                                  c == 0, c == BC - 1)
                        else:
                            spans, blocks, _ = QKV[what[0]]
                            width = sum(c for _, c in spans)
                            if blocks:
                                ins = feature_slab(k, kh, banks, blocks)
                            if blocks == 2:
                                ins = token_slab(k, kh, width, slice(256, 512), lambda tt: banks[1][:, tt * 256:(tt + 1) * 256], True)
                            if blocks == 0:
                                ins = token_slab(k, kh, width, slice(0, width), lambda tt: banks[tt][:, 0:width])
                        ins.then_inc(slab_used, 1)

                    def projected(name):
                        tile = TILES.index((name,))
                        pe.wait_ge(pair_read[tile % 2], pair_reads(tile) + 2)

                    def scores(u):
                        b, hd = u // HEADS, u % HEADS
                        if before(u) > 0:
                            pe.wait_ge(score_read, before(u))
                        for m in range(2 if b == DIFF else 1):
                            dst = bank[4 + (m if b == DIFF else u % 2)]
                            size = 32 if b == DIFF else HD
                            rows_at = slice(HD * (hd % 2) + 32 * m, HD * (hd % 2) + 32 * m + size)
                            q, key = qk[rows_at, 2 * BC * b + hd // 2, :], qk[rows_at, 2 * BC * b + BC + hd // 2, :]
                            if b == STICK:
                                for tt in range(NT):
                                    toks = slice(tt * P, (tt + 1) * P)
                                    o = dst[:, 2 * tt * P:(2 * tt + 1) * P]
                                    nc.tensor.matmul(o, q[:, toks], key[:, toks], start=True, stop=False)
                                    nc.tensor.matmul(o, ident_b[:], near[:], start=False, stop=True)
                                ins = nc.tensor.matmul(dst[:, P:2 * P], q[:, P:S], key[:, 0:P], start=True, stop=True)
                            else:
                                nc.tensor.matmul(dst[:, ROWS_A], q[:, 0:P], key[:, 0:P], start=True, stop=True)
                                ins = nc.tensor.matmul(dst[:, ROWS_B], q[:, P:S], key, start=True, stop=True)
                        ins.then_inc(scored, 1)

                    def transpose_weights(u):
                        side = 0 if u // HEADS == DIFF else u % 2
                        pe.wait_ge(prob_ready, u + 1)
                        if u > 0:
                            pe.wait_ge(probT_ready, u)
                        for i in range(3):
                            ins = nc.tensor.transpose(bank[6][:, i * P:(i + 1) * P], prob[:, side, i * P:(i + 1) * P], ident[:])
                        ins.then_inc(probT_psum, 1)

                    def outputs(u):
                        b, hd = u // HEADS, u % HEADS
                        pe.wait_ge(probT_ready, u + 1)
                        if hd == 0:
                            for name in (["v of moba, sb"], ["v of diff"], ["k, v of sb"])[b]:
                                projected(name)
                        if u % 2 == 0 and u > 0:
                            p = u // 2 - 1
                            if p // BC == DIFF:
                                pe.wait_ge(o_spread, p - BC + 1)
                            else:
                                pe.wait_ge(oT_ready, p + 1)
                        dst = bank[7][HD * (hd % 2):HD * (hd % 2 + 1), :]
                        v = [v_mix[:, tt, b * BW + hd * HD:b * BW + (hd + 1) * HD] for tt in range(NT)]
                        p = probT[:, u % 2, :]
                        nc.tensor.matmul(dst[:, 0:P], v[0], p[:, 0:P], start=True, stop=True)
                        nc.tensor.matmul(dst[:, P:S], v[0], p[:, P:2 * P], start=True, stop=False)
                        nc.tensor.matmul(dst[:, P:S], v[1], p[:, 2 * P:3 * P], start=False, stop=True).then_inc(o_psum, 1)

                    def square_sums(p):
                        pe.wait_ge(o_square, p - BC + 1)
                        nc.tensor.matmul(bank[7][:, S:2 * S], same_head[:], ms_d, start=True, stop=True).then_inc(o_sums, 1)

                    for d in ROUND[0]:
                        slab(d)
                    projected("q, k of moba")
                    projected("k of moba, q of diff")
                    pe.wait_ge(consts, 2)
                    scores(0)
                    scores(1)
                    for u in range(3 * HEADS):
                        b, hd = u // HEADS, u % HEADS
                        for d in ROUND[u + 1]:
                            slab(d)
                        if u % 2 == 1 and (u - 3) // 2 // BC == DIFF:
                            square_sums((u - 3) // 2)
                        transpose_weights(u)
                        for ahead in {MOBA: [u + 2] if hd < 4 else [u + 1] if hd == 5 else [],
                                      DIFF: [u + 1] if hd < 5 else [u + 1, u + 2],
                                      STICK: [u + 2] if hd < 4 else []}[b]:
                            if ahead == HEADS:
                                projected("q, k of diff")
                            if ahead == 2 * HEADS:
                                projected("q, k of sb")
                                projected("k, v of sb")
                            scores(ahead)
                        if u > 0:
                            outputs(u - 1)
                    outputs(3 * HEADS - 1)
                    for d in ROUND[-1]:
                        slab(d)
                    first_input = 4 * (inputs_before(n) + 1)
                    pe.wait_ge(merged, 10)
                    transpose_input(z_sb, HALVES_FIRST[0:2])
                    for d in range(KC // 2):
                        pe.wait_ge(xT_ready, first_input + (2 if d < 2 else 4))
                        project_slab(s0 + 32 + d, d, KC // 2, xT_hi, xT_lo)
                        if d == 0:
                            pe.wait_ge(merged, 12)
                            transpose_input(z_sb, HALVES_FIRST[2:4])
                if kind == CONV:
                    for j in range(6):
                        if j >= 2:
                            pe.wait_ge(conv_v_ready, j - 1)
                        for kh in range(2):
                            feature_slab(s0 + 2 * j + kh, kh, [bank[4 * (j % 2)], bank[4 * (j % 2) + 1]], 4)\
                                .then_inc(slab_used, 1)
                    for d in range(KC // 2):
                        pe.wait_ge(yT_ready, d + 1)
                        project_slab(s0 + 12 + d, d, KC // 2, yT_hi, yT_lo)
                if kind == KV:
                    def two_slots(slab, banks):
                        for kh in range(2):
                            token_slab(s0 + slab + kh, kh, 512, slice(0, 512), lambda tt: banks[tt][:]).then_inc(slab_used, 1)
                            if slab == 8 and kh == 0:
                                transpose_hidden(1)

                    def transpose_hidden(kv):
                        pe.wait_ge(hid_rows, kv + 1)
                        for hb in range(2):
                            ins = nc.tensor.transpose(hidden_of(kv, hb), hid_row[:, kv, hb * P:(hb + 1) * P], ident[0:CMP_ROWS, 0:CMP_ROWS])
                        ins.then_inc(hidT_psum, 1)

                    for kh in range(2):
                        feature_slab(s0 + kh, kh, [bank[0], bank[1]], 4).then_inc(slab_used, 1)
                    two_slots(2, [bank[4], bank[5]])
                    for kv in range(2):
                        pe.wait_ge(xc_ready, 1 + 4 * (kv + 1))
                        for part in range(2):
                            k = s0 + 4 + 2 * kv + part
                            pe.wait_ge(low_ready, k + 1)
                            hi, lo = slab_view(k % SLOTS, 8, 256)
                            for c in range(8):
                                chunk = 8 * part + c
                                at = slice(2 * chunk, 2 * chunk + 16 * CMP_ROWS - 15, 16)
                                ins = product(bank[6 + kv][0:CMP_ROWS, 0:CMP_HID], xc_hi[:, kv, at], xc_lo[:, kv, at],
                                              hi[:, c, :], lo[:, c, :], chunk == 0, chunk == 15)
                            ins.then_inc(slab_used, 1)
                            if kv == 1 and part == 0:
                                transpose_hidden(0)
                    two_slots(8, [bank[2], bank[3]])
                    pe.wait_ge(loaded_kv, 32)
                    pe.wait_ge(hid_ready, 4)
                    for hb in range(2):
                        ins = nc.tensor.matmul(bank[6][0:GROUPS * 16, 0:HD], hid[:, 0, hb, :], cmp_w2[:, 0, hb, :], start=hb == 0, stop=hb == 1)
                    ins.then_inc(cmp_psum, 1)
                    pe.wait_ge(hid_v_ready, 1)
                    for g in range(GROUPS):
                        for hb in range(2):
                            ins = nc.tensor.matmul(bank[7][:, g * HD:(g + 1) * HD], hid_v[:, hb, g, :, :].rearrange("p r n -> p (r n)"),
                                                   cmp_w2[:, 1, hb, :], start=hb == 0, stop=hb == 1)
                    ins.then_inc(cmp_psum, 1)
                    pe.wait_ge(key_normed, 1)
                if kind == NSA:
                    def project_queries(j):
                        for kh in range(2):
                            token_slab(s0 + 2 * j + kh, kh, 512, slice(0, 512), lambda tt: bank[Q_IN[j][tt]][:]).then_inc(slab_used, 1)

                    def transpose_queries(j):
                        pe.wait_ge(q_normed, j + 1)
                        for rp in range(2):
                            for r in range(2):
                                for tt in range(NT):
                                    at = slice((2 * rp + r) * P, (2 * rp + r + 1) * P)
                                    o = bank[Q_T[j][rp]][:, r * S + tt * P:r * S + (tt + 1) * P]
                                    ins = nc.tensor.transpose(o, q_n[:, tt, j, at], ident[:])
                            ins.then_inc(qT_psum, 1)

                    project_queries(0)
                    pe.wait_ge(wg_ready, 1)
                    for c in range(KC):
                        for tt in range(NT):
                            toks = slice(tt * P, (tt + 1) * P)
                            ins = product(bank[2][:, tt * 3 * NQ:(tt + 1) * 3 * NQ], xT_hi[:, c, toks], xT_lo[:, c, toks], wg_hi[:, c, :], wg_lo[:, c, :],
                                          c == 0 and tt == 0, c == KC - 1, shared=True)
                    ins.then_inc(gates_psum, 1)
                    project_queries(1)
                    pe.wait_ge(branch_gates, 1)
                    transpose_queries(0)

                    def query(g, r, tt):
                        return qT[HD * (g % 2):HD * (g % 2 + 1), g // 2, r, tt * P:(tt + 1) * P]

                    def scores(w):
                        g, keys = w // 2, (k_sel, k_win)[w % 2]
                        key = keys[HD * (g % 2):HD * (g % 2 + 1), g // 2, :]
                        if w >= 2:
                            pe.wait_ge(selT_act, w - 1)
                            pe.wait_ge(selT_dve, w - 1)
                        banks = [bank[i] for i in SCORES[w % 2]]
                        for b in range(3):
                            heads = 4 if b == 0 else 2
                            o = banks[b][:].rearrange("p (r m) -> p r m", r=heads)[:, :, (S - P) * (b > 0):]
                            nc.tensor.matmul(o, ident_b[:], causal[:].unsqueeze(1).to_broadcast([P, heads, P]), start=True, stop=False,
                                             skip_group_check=True)
                        for tt in range(NT):
                            for r in range(PER_GROUP):
                                b, at = score_place(tt, r)
                                ins = nc.tensor.matmul(banks[b][:, at], query(g, r, tt), key[:, 0:P * (tt + 1)], start=False, stop=True,
                                                       skip_group_check=True)
                        ins.then_inc(sel_scored, 1)

                    def transpose_weights(w):
                        pe.wait_ge(sel_exped, w + 1)
                        for b in range(3):
                            for i in range(4):
                                at = slice(i * P, (i + 1) * P)
                                ins = nc.tensor.transpose(bank[SCORES[w % 2][b]][:, at], sel_p[:, w % 2, b, at], ident[:])
                        ins.then_inc(selT_psum, 1)

                    def outputs(w):
                        g, values = w // 2, (v_sel, v_win)[w % 2]
                        pe.wait_ge(selT_act, w + 1)
                        pe.wait_ge(selT_dve, w + 1)
                        if w >= 2:
                            pe.wait_ge(attended, w - 1)
                        for tt in range(NT):
                            for r in range(PER_GROUP):
                                b, at = score_place(tt, r)
                                o = bank[6 + w % 2][:, (tt * PER_GROUP + r) * HD:(tt * PER_GROUP + r + 1) * HD]
                                for key_tile in range(tt + 1):
                                    p = sel_pT[:, w % 2, b, at.start + key_tile * P:at.start + (key_tile + 1) * P]
                                    ins = nc.tensor.matmul(o, p, values[:, key_tile, g * HD:(g + 1) * HD], start=key_tile == 0, stop=key_tile == tt)
                        ins.then_inc(sel_out, 1)

                    pe.wait_ge(qT_ready, 2)
                    pe.wait_ge(consts, 2)
                    scores(0)
                    transpose_queries(1)
                    pe.wait_ge(qT_ready, 4)
                    for tt in range(NT):
                        for hd in range(NQ):
                            g, r = hd // PER_GROUP, hd % PER_GROUP
                            at = tt * P + (g // 2 * PER_GROUP + r) * 16
                            o = bank[6 + g % 2][:, at:at + 16]
                            ins = nc.tensor.matmul(o, query(g, r, tt), k_cmp[HD * (g % 2):HD * (g % 2 + 1), 16 * g:16 * (g + 1)], start=True, stop=True)
                    ins.then_inc(cmp_scored, 1)
                    scores(1)
                    pe.wait_ge(cmp_weighted, 1)
                    for tt in range(NT):
                        for g in range(GROUPS):
                            p = cmp_p[:, tt, PER_GROUP * g:PER_GROUP * (g + 1), :].rearrange("p r n -> p (r n)")
                            ins = nc.tensor.transpose(bank[CMP_OUT[tt]][:, g * P:(g + 1) * P], p, ident[:])
                        ins.then_inc(cmpT_psum, 1)
                    transpose_weights(0)
                    pe.wait_ge(cmpT_ready, NT)
                    for tt in range(NT):
                        if tt > 0:
                            pe.wait_ge(z_started, 2 * tt)
                        for g in range(GROUPS):
                            o = bank[CMP_OUT[g // 2]][:, (g % 2) * S:(g % 2 + 1) * S]
                            ins = nc.tensor.matmul(o, cmp_pT[:, tt, g, :], v_cmp[:, g, :], start=True, stop=True)
                        ins.then_inc(cmp_out, 1)
                    scores(2)
                    pe.wait_ge(z_started, 2 * NT)
                    for w in range(1, UNITS):
                        transpose_weights(w)
                        outputs(w - 1)
                        if w + 2 < UNITS:
                            scores(w + 2)
                    first_input = 4 * (inputs_before(n) + 1)
                    pe.wait_ge(attended, UNITS // 2)
                    transpose_input(z_sb, HALVES_FIRST[0:2])
                    outputs(UNITS - 1)
                    for d in range(KC // 2):
                        pe.wait_ge(xT_ready, first_input + (2 if d < 2 else 4))
                        project_slab(s0 + 4 + d, d, KC // 2, xT_hi, xT_lo, (lambda: pe.wait_ge(attended, UNITS)) if d == 0 else None)
                        if d == 0:
                            transpose_input(z_sb, HALVES_FIRST[2:4])
                if n < last:
                    for tt in range(1 if phases[n + 1] == FFN else NT):
                        next_input(n + 1, tt)


_INS = ["x", "ln_g", "ln_b", "ffn_w_gate", "ffn_w_up", "ffn_w_down", "w_in", "b_gate", "diff_lambda", "diff_subln_g",
        "w_br_moba", "w_br_diff", "w_br_sb", "w_out", "ffn_norm_2", "ffn_w_gate_up_2", "ffn_w_down_2", "mix_norm_2",
        "conv_w_in_2", "conv_w_2", "conv_w_out_2", "kv_norm_2", "kv_w_2", "cmp_pos_2", "cmp_w1_2", "cmp_b1_2",
        "cmp_w2_2", "k_norm_2", "nsa_w_qg_2", "q_norm_2", "nsa_w_o_2"]


def kernel(**inputs):
    import numpy as _np
    import concourse.bacc as _bacc
    from concourse import mybir as _mybir
    from concourse.bass_utils import run_bass_kernel_spmd as _run

    nc = _bacc.Bacc("TRN2", target_bir_lowering=False, num_devices=1)
    arrays, t = {}, {}
    for name in _INS:
        a = _np.ascontiguousarray(inputs[name])
        arrays[f"in_{name}_dram"] = a
        t[name] = nc.dram_tensor(f"in_{name}_dram", a.shape, _mybir.dt.from_np(a.dtype), kind="ExternalInput").ap()
    out = nc.dram_tensor("out_0_dram", (1, S, D), _mybir.dt.float32, kind="ExternalOutput").ap()
    two_block_kernel(nc, t, out[0])
    r = _run(nc, [arrays], core_ids=[0])
    return r.results[0]["out_0_dram"]
```
